# Optimizing a Trainium2 kernel written in Bass

```python
import math
import jax, jax.numpy as jnp
from jax import lax
import numpy as np

D_MODEL = 1024
BATCH = 1
SEQ = 1024
DEPTH = 2

HEAD_DIM = 64
BLOCK_Q = 128
NEG_INF = -1e30
RMS_EPS = 1e-6
MLA_HEADS = 8
MLA_NOPE_DIM = 64
MLA_ROPE_DIM = 32
MLA_V_DIM = 64
MLA_Q_RANK = 256
MLA_KV_RANK = 128
ROPE_THETA = 10000.0
FOX_HEADS = 8
DIL_GROUPS = ((128, 1), (512, 4), (2048, 16))
DIL_HEADS = 4
DIL_WIDTH = 3 * DIL_HEADS * HEAD_DIM
NSA_HEADS = 4
NSA_CMP_LEN = 32
NSA_CMP_STRIDE = 16
NSA_CMP_HIDDEN = 256
NSA_SEL_BLOCK = 64
NSA_TOPK = 16
NSA_WINDOW = 512
NSA_FORCE_SCORE = 1e9
T5_BUCKETS = 32
T5_MAX_DIST = 2048
T5_HEADS = 3 * DIL_HEADS + NSA_HEADS
D_FF = 4 * D_MODEL
PLE_DIM = 256

EVEN_IN_SIZES = (MLA_Q_RANK, MLA_KV_RANK, MLA_ROPE_DIM,
                 FOX_HEADS * HEAD_DIM, FOX_HEADS * HEAD_DIM, FOX_HEADS * HEAD_DIM, FOX_HEADS)
EVEN_IN_WIDTH = MLA_Q_RANK + MLA_KV_RANK + MLA_ROPE_DIM + 3 * FOX_HEADS * HEAD_DIM + FOX_HEADS
EVEN_OUT_WIDTH = MLA_HEADS * MLA_V_DIM + FOX_HEADS * HEAD_DIM
ODD_IN_SIZES = (DIL_WIDTH, DIL_WIDTH, DIL_WIDTH, NSA_HEADS * HEAD_DIM,
                HEAD_DIM, HEAD_DIM, HEAD_DIM, HEAD_DIM, HEAD_DIM, HEAD_DIM, NSA_HEADS * 3)
ODD_IN_WIDTH = 3 * DIL_WIDTH + NSA_HEADS * HEAD_DIM + 6 * HEAD_DIM + NSA_HEADS * 3
ODD_OUT_WIDTH = DIL_HEADS * HEAD_DIM + NSA_HEADS * HEAD_DIM
N_EVEN = (DEPTH + 1) // 2
N_ODD = DEPTH // 2

kernel_name = "hybrid_mla_fox_dilated_nsa_trunk"

def rms_norm(x, g):
    x32 = x.astype(jnp.float32)
    y = x32 * lax.rsqrt(jnp.mean(x32 * x32, axis=-1, keepdims=True) + RMS_EPS)
    return (y * g.astype(jnp.float32)).astype(x.dtype)

def split_cols(y, sizes):
    idx, acc = [], 0
    for s in sizes[:-1]:
        acc += s
        idx.append(acc)
    return jnp.split(y, idx, axis=-1)

def t5_bucket(dist):
    n = jnp.maximum(dist, 0)
    max_exact = T5_BUCKETS // 2
    ratio = jnp.log(jnp.maximum(n, 1).astype(jnp.float32) / max_exact) / math.log(T5_MAX_DIST / max_exact)
    large = jnp.minimum(max_exact + (ratio * (T5_BUCKETS - max_exact)).astype(jnp.int32), T5_BUCKETS - 1)
    return jnp.where(n < max_exact, n, large)

def apply_rope(x, cos, sin):
    x1, x2 = jnp.split(x, 2, axis=-1)
    return jnp.concatenate([x1 * cos - x2 * sin, x2 * cos + x1 * sin], axis=-1).astype(x.dtype)

def dense_causal_attention(q, k, v, scale, cum_log_forget=None):
    B, S, H, _ = q.shape
    Dv = v.shape[-1]
    s_pos = jnp.arange(S)
    cum_k = None if cum_log_forget is None else jnp.transpose(cum_log_forget, (0, 2, 1))

    def one_block(i):
        q0 = i * BLOCK_Q
        t = q0 + jnp.arange(BLOCK_Q)
        qb = lax.dynamic_slice_in_dim(q, q0, BLOCK_Q, axis=1)
        logits = jnp.einsum('bqhd,bkhd->bhqk', qb, k, preferred_element_type=jnp.float32) * scale
        if cum_k is not None:
            cq = lax.dynamic_slice_in_dim(cum_k, q0, BLOCK_Q, axis=2)
            logits = logits + cq[..., None] - cum_k[:, :, None, :]
        logits = jnp.where(s_pos[None, :] <= t[:, None], logits, NEG_INF)
        p = jax.nn.softmax(logits, axis=-1)
        return jnp.einsum('bhqk,bkhd->bqhd', p.astype(v.dtype), v)

    out = lax.map(one_block, jnp.arange(S // BLOCK_Q))
    return jnp.moveaxis(out, 0, 1).reshape(B, S, H, Dv)

def dilated_attention(q, k, v, bias_table):
    B, S, G, H, Dh = q.shape
    scale = Dh ** -0.5
    k_groups = [k[:, :, g] for g in range(G)]
    v_groups = [v[:, :, g] for g in range(G)]
    offsets, group_bias = [], []
    for g, (w, d) in enumerate(DIL_GROUPS):
        offs = d * jnp.arange(w // d + 1)
        offsets.append(offs)
        group_bias.append(bias_table[t5_bucket(offs), g * H:(g + 1) * H].T)

    def one_block(i):
        q0 = i * BLOCK_Q
        t = q0 + jnp.arange(BLOCK_Q)
        qb = lax.dynamic_slice_in_dim(q, q0, BLOCK_Q, axis=1)
        outs, lses = [], []
        for g in range(G):
            idx = t[:, None] - offsets[g][None, :]
            valid = idx >= 0
            idx = jnp.maximum(idx, 0)
            kg = k_groups[g][:, idx]
            vg = v_groups[g][:, idx]
            logits = jnp.einsum('bqhd,bqkhd->bhqk', qb[:, :, g], kg, preferred_element_type=jnp.float32) * scale
            logits = logits + group_bias[g][None, :, None, :].astype(jnp.float32)
            logits = jnp.where(valid[None, None], logits, NEG_INF)
            lse = jax.nn.logsumexp(logits, axis=-1)
            p = jnp.exp(logits - lse[..., None])
            outs.append(jnp.einsum('bhqk,bqkhd->bqhd', p.astype(v.dtype), vg))
            lses.append(lse)
        wts = jax.nn.softmax(jnp.stack(lses, axis=0), axis=0)
        return jnp.einsum('gbhq,gbqhd->bqhd', wts.astype(v.dtype), jnp.stack(outs, axis=0))

    out = lax.map(one_block, jnp.arange(S // BLOCK_Q))
    return jnp.moveaxis(out, 0, 1).reshape(B, S, H, Dh)

def nsa_attention(q, k_cmp_src, v_cmp_src, k_sel, v_sel, k_win, v_win, gates, bias_table,
                  cmp_pos_k, cmp_pos_v, w1_k, w2_k, w1_v, w2_v):
    B, S, H, Dh = q.shape
    scale = Dh ** -0.5
    n_cmp = (S - NSA_CMP_LEN) // NSA_CMP_STRIDE + 1
    n_sel = S // NSA_SEL_BLOCK
    topk = min(NSA_TOPK, n_sel)
    cmp_start = jnp.arange(n_cmp) * NSA_CMP_STRIDE
    blk_idx = cmp_start[:, None] + jnp.arange(NSA_CMP_LEN)[None, :]

    def compress(src, pos, w1, w2):
        blocks = src[:, blk_idx] + pos
        return jax.nn.gelu(blocks.reshape(B, n_cmp, NSA_CMP_LEN * Dh) @ w1) @ w2

    kc = compress(k_cmp_src, cmp_pos_k, w1_k, w2_k)
    vc = compress(v_cmp_src, cmp_pos_v, w1_v, w2_v)
    cmp_end = cmp_start + NSA_CMP_LEN - 1
    sel_start = jnp.arange(n_sel) * NSA_SEL_BLOCK
    overlap = ((cmp_start[:, None] < sel_start[None, :] + NSA_SEL_BLOCK) &
               (cmp_start[:, None] + NSA_CMP_LEN > sel_start[None, :])).astype(jnp.float32)
    k_win_pad = jnp.pad(k_win, ((0, 0), (NSA_WINDOW, 0), (0, 0)))
    v_win_pad = jnp.pad(v_win, ((0, 0), (NSA_WINDOW, 0), (0, 0)))
    win_len = BLOCK_Q + NSA_WINDOW
    gather_rows = jax.vmap(lambda a, i: a[i])

    def one_block(i):
        q0 = i * BLOCK_Q
        t = q0 + jnp.arange(BLOCK_Q)
        qb = lax.dynamic_slice_in_dim(q, q0, BLOCK_Q, axis=1)
        gb = lax.dynamic_slice_in_dim(gates, q0, BLOCK_Q, axis=1)
        c_mask = cmp_end[None, :] <= t[:, None]
        logits = jnp.einsum('bqhd,bnd->bhqn', qb, kc, preferred_element_type=jnp.float32) * scale
        p_cmp = jax.nn.softmax(jnp.where(c_mask, logits, NEG_INF), axis=-1) * c_mask
        o_cmp = jnp.einsum('bhqn,bnd->bqhd', p_cmp.astype(vc.dtype), vc)
        importance = jnp.einsum('bhqn,nj->bqj', p_cmp, overlap)
        tb = t // NSA_SEL_BLOCK
        j = jnp.arange(n_sel)
        forced = (j[None, :] == 0) | (j[None, :] == tb[:, None]) | (j[None, :] == tb[:, None] - 1)
        causal_blk = sel_start[None, :] <= t[:, None]
        score = jnp.where(forced, NSA_FORCE_SCORE, jnp.where(causal_blk, importance, -NSA_FORCE_SCORE))
        _, sel = lax.top_k(score, topk)
        tok = (sel[..., None] * NSA_SEL_BLOCK + jnp.arange(NSA_SEL_BLOCK)).reshape(B, BLOCK_Q, topk * NSA_SEL_BLOCK)
        ks = gather_rows(k_sel, tok)
        vs = gather_rows(v_sel, tok)
        dist = t[None, :, None] - tok
        logits = jnp.einsum('bqhd,bqkd->bhqk', qb, ks, preferred_element_type=jnp.float32) * scale
        logits = logits + jnp.moveaxis(bias_table[t5_bucket(dist)], -1, 1).astype(jnp.float32)
        logits = jnp.where((dist >= 0)[:, None], logits, NEG_INF)
        o_sel = jnp.einsum('bhqk,bqkd->bqhd', jax.nn.softmax(logits, axis=-1).astype(vs.dtype), vs)
        kw = lax.dynamic_slice_in_dim(k_win_pad, q0, win_len, axis=1)
        vw = lax.dynamic_slice_in_dim(v_win_pad, q0, win_len, axis=1)
        s = q0 - NSA_WINDOW + jnp.arange(win_len)
        dist_w = t[:, None] - s[None, :]
        w_mask = (dist_w >= 0) & (dist_w < NSA_WINDOW) & (s[None, :] >= 0)
        logits = jnp.einsum('bqhd,bkd->bhqk', qb, kw, preferred_element_type=jnp.float32) * scale
        logits = logits + jnp.transpose(bias_table[t5_bucket(dist_w)], (2, 0, 1))[None].astype(jnp.float32)
        logits = jnp.where(w_mask[None, None], logits, NEG_INF)
        o_win = jnp.einsum('bhqk,bkd->bqhd', jax.nn.softmax(logits, axis=-1).astype(vw.dtype), vw)
        return gb[..., 0:1] * o_cmp + gb[..., 1:2] * o_sel + gb[..., 2:3] * o_win

    out = lax.map(one_block, jnp.arange(S // BLOCK_Q))
    return jnp.moveaxis(out, 0, 1).reshape(B, S, H, Dh)

def even_mixer(hn, cos, sin, w_in, q_norm, w_uq, kv_norm, w_ukv, forget_bias, w_out):
    B, S, _ = hn.shape
    c_q, c_kv, k_r, fq, fk, fv, f_logit = split_cols(hn @ w_in, EVEN_IN_SIZES)
    q = (rms_norm(c_q, q_norm) @ w_uq).reshape(B, S, MLA_HEADS, MLA_NOPE_DIM + MLA_ROPE_DIM)
    q_nope, q_rope = jnp.split(q, [MLA_NOPE_DIM], axis=-1)
    q_rope = apply_rope(q_rope, cos[:, :, None], sin[:, :, None])
    kv = (rms_norm(c_kv, kv_norm) @ w_ukv).reshape(B, S, MLA_HEADS, MLA_NOPE_DIM + MLA_V_DIM)
    k_nope, v_mla = jnp.split(kv, [MLA_NOPE_DIM], axis=-1)
    k_r = apply_rope(k_r, cos, sin)
    q_mla = jnp.concatenate([q_nope, q_rope], axis=-1)
    k_mla = jnp.concatenate([k_nope, jnp.broadcast_to(k_r[:, :, None], (B, S, MLA_HEADS, MLA_ROPE_DIM))], axis=-1)
    o_mla = dense_causal_attention(q_mla, k_mla, v_mla, (MLA_NOPE_DIM + MLA_ROPE_DIM) ** -0.5)
    log_f = jax.nn.log_sigmoid((f_logit + forget_bias).astype(jnp.float32))
    cum = jnp.cumsum(log_f, axis=1)
    shp = (B, S, FOX_HEADS, HEAD_DIM)
    o_fox = dense_causal_attention(fq.reshape(shp), fk.reshape(shp), fv.reshape(shp), HEAD_DIM ** -0.5, cum)
    o = jnp.concatenate([o_mla.reshape(B, S, -1), o_fox.reshape(B, S, -1)], axis=-1)
    return o @ w_out

def odd_mixer(hn, t5_bias, w_in, cmp_pos_k, cmp_pos_v, cmp_w1_k, cmp_w2_k, cmp_w1_v, cmp_w2_v, w_out):
    B, S, _ = hn.shape
    (dq, dk, dv, nq, k_cmp_src, v_cmp_src, k_sel, v_sel, k_win, v_win,
     gate_logit) = split_cols(hn @ w_in, ODD_IN_SIZES)
    G = len(DIL_GROUPS)
    shp = (B, S, G, DIL_HEADS, HEAD_DIM)
    o_dil = dilated_attention(dq.reshape(shp), dk.reshape(shp), dv.reshape(shp), t5_bias[:, :G * DIL_HEADS])
    gates = jax.nn.sigmoid(gate_logit.reshape(B, S, NSA_HEADS, 3))
    o_nsa = nsa_attention(nq.reshape(B, S, NSA_HEADS, HEAD_DIM), k_cmp_src, v_cmp_src, k_sel, v_sel,
                          k_win, v_win, gates, t5_bias[:, G * DIL_HEADS:],
                          cmp_pos_k, cmp_pos_v, cmp_w1_k, cmp_w2_k, cmp_w1_v, cmp_w2_v)
    o = jnp.concatenate([o_dil.reshape(B, S, -1), o_nsa.reshape(B, S, -1)], axis=-1)
    return o @ w_out

def setup_inputs(seed: int = 0) -> dict:
    key = jax.random.key(seed)
    ks = iter(jax.random.split(key, 40))

    def dense(shape, fan_in):
        return jax.random.normal(next(ks), shape, jnp.float32) * fan_in ** -0.5

    def gain(shape):
        return 1.0 + 0.05 * jax.random.normal(next(ks), shape, jnp.float32)

    x = jax.random.normal(next(ks), (BATCH, SEQ, D_MODEL), jnp.float32)
    p = jax.random.normal(next(ks), (DEPTH, BATCH, SEQ, PLE_DIM), jnp.float32)
    offset = jax.random.randint(next(ks), (BATCH, 1), 0, 1024, jnp.int32)
    positions = offset + jnp.arange(SEQ, dtype=jnp.int32)[None, :]
    return {
        "x": x,
        "p": p,
        "positions": positions,
        "t5_bias": 0.5 * jax.random.normal(next(ks), (T5_BUCKETS, T5_HEADS), jnp.float32),
        "ev_w_in": dense((N_EVEN, D_MODEL, EVEN_IN_WIDTH), D_MODEL),
        "ev_q_norm": gain((N_EVEN, MLA_Q_RANK)),
        "ev_w_uq": dense((N_EVEN, MLA_Q_RANK, MLA_HEADS * (MLA_NOPE_DIM + MLA_ROPE_DIM)), MLA_Q_RANK),
        "ev_kv_norm": gain((N_EVEN, MLA_KV_RANK)),
        "ev_w_ukv": dense((N_EVEN, MLA_KV_RANK, MLA_HEADS * (MLA_NOPE_DIM + MLA_V_DIM)), MLA_KV_RANK),
        "ev_forget_bias": jax.random.uniform(next(ks), (N_EVEN, FOX_HEADS), jnp.float32, 2.0, 5.0),
        "ev_w_out": dense((N_EVEN, EVEN_OUT_WIDTH, D_MODEL), EVEN_OUT_WIDTH),
        "od_w_in": dense((N_ODD, D_MODEL, ODD_IN_WIDTH), D_MODEL),
        "od_cmp_pos_k": 0.1 * jax.random.normal(next(ks), (N_ODD, NSA_CMP_LEN, HEAD_DIM), jnp.float32),
        "od_cmp_pos_v": 0.1 * jax.random.normal(next(ks), (N_ODD, NSA_CMP_LEN, HEAD_DIM), jnp.float32),
        "od_cmp_w1_k": dense((N_ODD, NSA_CMP_LEN * HEAD_DIM, NSA_CMP_HIDDEN), NSA_CMP_LEN * HEAD_DIM),
        "od_cmp_w2_k": dense((N_ODD, NSA_CMP_HIDDEN, HEAD_DIM), NSA_CMP_HIDDEN),
        "od_cmp_w1_v": dense((N_ODD, NSA_CMP_LEN * HEAD_DIM, NSA_CMP_HIDDEN), NSA_CMP_LEN * HEAD_DIM),
        "od_cmp_w2_v": dense((N_ODD, NSA_CMP_HIDDEN, HEAD_DIM), NSA_CMP_HIDDEN),
        "od_w_out": dense((N_ODD, ODD_OUT_WIDTH, D_MODEL), ODD_OUT_WIDTH),
        "norm_mix_pre": gain((DEPTH, D_MODEL)),
        "norm_mix_post": gain((DEPTH, D_MODEL)),
        "norm_mlp_pre": gain((DEPTH, D_MODEL)),
        "norm_mlp_post": gain((DEPTH, D_MODEL)),
        "w_mlp_up": dense((DEPTH, D_MODEL, D_FF), D_MODEL),
        "w_mlp_down": dense((DEPTH, D_FF, D_MODEL), D_FF),
        "ple_norm": gain((DEPTH, D_MODEL)),
        "w_ple_gate": dense((DEPTH, D_MODEL, D_MODEL), D_MODEL),
        "w_ple_proj": dense((DEPTH, PLE_DIM, D_MODEL), PLE_DIM),
    }

def reference(x, p, positions, t5_bias, ev_w_in, ev_q_norm, ev_w_uq, ev_kv_norm, ev_w_ukv, ev_forget_bias,
              ev_w_out, od_w_in, od_cmp_pos_k, od_cmp_pos_v, od_cmp_w1_k, od_cmp_w2_k, od_cmp_w1_v, od_cmp_w2_v,
              od_w_out, norm_mix_pre, norm_mix_post, norm_mlp_pre, norm_mlp_post, w_mlp_up, w_mlp_down,
              ple_norm, w_ple_gate, w_ple_proj):
    inv_freq = ROPE_THETA ** (-jnp.arange(0, MLA_ROPE_DIM, 2, dtype=jnp.float32) / MLA_ROPE_DIM)
    angles = positions.astype(jnp.float32)[..., None] * inv_freq
    cos, sin = jnp.cos(angles), jnp.sin(angles)
    h = x
    for i in range(DEPTH):
        j = i // 2
        hn = rms_norm(h, norm_mix_pre[i])
        if i % 2 == 0:
            mix = even_mixer(hn, cos, sin, ev_w_in[j], ev_q_norm[j], ev_w_uq[j], ev_kv_norm[j], ev_w_ukv[j],
                             ev_forget_bias[j], ev_w_out[j])
        else:
            mix = odd_mixer(hn, t5_bias, od_w_in[j], od_cmp_pos_k[j], od_cmp_pos_v[j], od_cmp_w1_k[j],
                            od_cmp_w2_k[j], od_cmp_w1_v[j], od_cmp_w2_v[j], od_w_out[j])
        h = h + rms_norm(mix, norm_mix_post[i])
        hn = rms_norm(h, norm_mlp_pre[i])
        m = jnp.square(jax.nn.relu(hn @ w_mlp_up[i])) @ w_mlp_down[i]
        h = h + rms_norm(m, norm_mlp_post[i])
        gate = jax.nn.sigmoid(rms_norm(h, ple_norm[i]) @ w_ple_gate[i])
        h = h + gate * (p[i] @ w_ple_proj[i])
    return h


_drawn_inputs = setup_inputs


def setup_inputs(seed=0):
    import zlib

    import numpy as np

    out = dict(_drawn_inputs(seed))
    spreads = {}
    factors = {'ev_q_norm': 3.706, 'od_cmp_pos_k': 8.0, 'ple_norm': 7.672}
    for name, (base, spread) in spreads.items():
        noise = np.random.default_rng([zlib.crc32(name.encode()), seed]).standard_normal(out[name].shape)
        drawn = base * np.exp(spread * noise) if base else spread * noise
        out[name] = __import__('jax').numpy.asarray(drawn.astype(out[name].dtype))
    for name, factor in factors.items():
        out[name] = (out[name] * factor).astype(out[name].dtype)
    return out
```

```python
import math
from contextlib import ExitStack

import numpy as np

import concourse.bass as bass
from concourse import mybir

F32 = mybir.dt.float32
F32R = mybir.dt.float32r
I32 = mybir.dt.int32
ALU = mybir.AluOpType
ACT = mybir.ActivationFunctionType
AX_X = mybir.AxisListType.X

P = 128
S = 1024
D = 1024
DC = D // P
NB = S // P
HALF = 512
HD = 64
KB = 1024
EPS = 1e-6
NEG = -1e30
ISCALE = 8.0
MLA_SCALE = 96 ** -0.5
HID_GROUP = 4
N_GROUPS = 4 * D // P // HID_GROUP
N_CMP = 63
WIN_BLOCKS = 4

SEL_W, WIN_W, DIL_W, D16_W = S, (WIN_BLOCKS + 1) * P, 2 * P, P
BROW = {"sel": 0, "win": 1152, "d1": 1920, "d4": 2304, "d16": 2688}
BROW_N = 2944


def unit_plan():
    full = lambda *tile: (8, "x", [tile])
    mlp = [(8, "x", [("up", c, 0)]) for c in range(HID_GROUP)]
    mlp += [(4, "hid", [("down", 2 * j, 0), ("down", 2 * j + 1, 0)]) for j in range(DC // 2)]
    ple = [(2, "p", [("ple", 4 * a + j, 0) for j in range(4)]) for a in range(2)]
    segs = []
    segs.append(("in0a", 1, [full("cq", 0, 0), full("cq", 1, 0), full("cq", 2, 0), full("misc", 0, 0)]))
    segs.append(("in0b", 4, [full("foxs", 0, 2), full("foxs", 1, 2)]))
    segs.append(("in0c", 2, [full("fox", 0, 2), full("fox", 1, 2)]))
    segs.append(("up0", 1, [(2, "cq", [("uq", 4 * a + j, 0) for j in range(4)]) for a in range(2)]
                 + [(1, "ckv", [("ukv", j, 0) for j in range(8)])]))
    segs.append(("out0", 4, [full("out", 0, 2), full("out", 1, 2)]))
    segs.append(("mlp0", N_GROUPS, mlp))
    segs.append(("ple0", 1, ple))
    segs.append(("gate0", 4, [full("gate", 0, 2), full("gate", 1, 2)]))
    segs.append(("in1a", 6, [full("odds", 0, 2), full("odds", 1, 2)]))
    segs.append(("in1b", 3, [full("odd", 0, 2), full("odd", 1, 2)]))
    segs.append(("in1c", 1, [full("odds", 12, 0), full("odds", 13, 0)] + [full("odd", c, 0) for c in range(6, 10)]))
    segs.append(("cmp", 1, [(8, "cmp", []) for _ in range(8)]))
    segs.append(("out1", 2, [(4, "x", [("out", 2 * a, 4), ("out", 2 * a + 1, 4)]) for a in range(2)]))
    segs.append(("mlp1", N_GROUPS, mlp))
    segs.append(("ple1", 1, ple))
    segs.append(("gate1", 4, [full("gate", 0, 2), full("gate", 1, 2)]))
    return segs


EXTRA = {"cmp": [("brow", 0), ("brow", 1), ("brow", 2), ("gt", 0)], "out1": [("kc", 0)]}
GELU_STEPS = 6
T_SLOTS = 2
MERGE_STEPS = 14
ROPE_KEY_STEPS = 3
DVE_ANGLE = 10
DVE_FZ = 11
DVE_ALL = 17
ACT_RELEASES = {"gt", "kc", "cq", "misc", "fox", "foxs", "odd", "odds", "uq", "ukv", "out", "up", "ple", "gate", "hid", "brow"}
DVE_RELEASES = {"uq", "down", "kc", "foxs", "odds"}
SPLIT = {"foxs", "odds"}
STORED = {"fox", "odd", "uq", "ukv"} | SPLIT


class Tile:

    def __init__(self, kind, idx, no, prev):
        self.kind, self.idx, self.no, self.pair = kind, idx, no, no % 2
        self.act = (prev.act if prev else 0) + (kind in ACT_RELEASES)
        self.dve = (prev.dve if prev else 2) + (kind in DVE_RELEASES)
        self.store = list(prev.store) if prev else [1, 1]
        self.up = (prev.up if prev else 0) + (kind == "up")
        self.down = (prev.down if prev else 0) + (kind == "down")
        self.gate = (prev.gate if prev else 0) + (kind == "gate")
        self.slot_before = list(self.store)
        if kind in STORED:
            self.store[self.pair] += 1


    def released(self):
        return {"act": self.act, "dve": self.dve}


class Unit:
    def __init__(self, no, k, src, tiles, tiles_end):
        self.no, self.k, self.src, self.tiles, self.tiles_end = no, k, src, tiles, tiles_end


class Seg:
    def __init__(self, name, n, iters):
        self.name, self.n, self.iters = name, n, iters


def build_segments(extra_before):
    segs, extras, tiles, units = {}, {}, [], []

    def tile(kind, idx):
        tiles.append(Tile(kind, idx, len(tiles), tiles[-1] if tiles else None))
        return tiles[-1]

    for name, n, body in unit_plan():
        extras[name] = [tile(*x) for x in extra_before.get(name, [])]
        iters = []
        for it in range(n):
            row = []
            for pos, (k, src, kinds) in enumerate(body):
                made = [tile(kind, i0 + it * step) for kind, i0, step in kinds]
                if name == "cmp" and pos in (3, 7):
                    made = [tile("hid", pos // 4)]
                end = len(tiles)
                units.append(Unit(len(units), k, src, made, end))
                row.append(units[-1])
            iters.append(row)
        segs[name] = Seg(name, n, iters)
    return segs, extras, tiles, units


def need(eng, sem, vals, it):
    if len(vals) == 1:
        if vals[0] > 0:
            eng.wait_ge(sem, vals[0])
        return
    if len(vals) == 2:
        slope = vals[1] - vals[0]
    else:
        slope = vals[2] - vals[1]
        assert all(vals[k + 1] - vals[k] == slope for k in range(1, len(vals) - 1)), vals
    first = vals[1] - slope
    assert first >= (slope > 0), vals
    if first < vals[0]:
        eng.wait_ge(sem, vals[0])
    if slope == 0:
        if first > 0:
            eng.wait_ge(sem, first)
        return
    eng.wait_ge(sem, it * slope + first)
    eng.nop(nofuse=True)


def at(idx0, step, it):
    return idx0 if step == 0 or isinstance(it, int) and it == 0 else it * step + idx0


TASK0 = 2 * NB
DILATED = ("d1", "d4", "d16")
NSA = ("cmp", "sel", "win")


class Job:

    def __init__(self, kind, pair, slot, prev_same_slot, c0):
        self.kind, self.pair, self.slot, self.prev = kind, pair, slot, prev_same_slot
        self.c0 = dict(c0)
        self.heads = 1 if kind == "mla" else 2
        self.nt = NB * self.heads
        self.tasks = []
        tr, a, d, pv = c0["tr"], c0["ptA"], c0["ptD"], c0["pv"]
        self.vgroups = []
        if kind != "cmp":
            for g in range(2):
                self.vgroups.append(dict(g=g, ring=tr % 2, tr=tr + 1, prev=None, eng="A"))
                tr, a = tr + 1, a + 1
        for n in range(self.nt):
            e, i = divmod(n, NB)
            blocks = self.blocks(i)
            t = dict(n=n, e=e, i=i, blocks=blocks, T=c0["task"] + n, groups=[])
            g0 = 0
            while g0 < len(blocks):
                g1 = min(len(blocks), g0 + 4)
                eng = "D" if (len(blocks) <= 4 or g0 > 0) else "A"
                t["groups"].append(dict(g0=g0, g1=g1, ring=tr % 2, tr=tr + 1, eng=eng, pv=pv + 1))
                tr, pv = tr + 1, pv + 1
                if eng == "A":
                    a += 1
                else:
                    d += 1
                t["groups"][-1]["copies"] = (a, d)
                g0 = g1
            self.tasks.append(t)
        self.ogroups = []
        kinds = {"fox": ["o"], "mla": ["o"] if pair % 2 else [], "d1": ["u", "l", "m"],
                 "d4": ["u", "l", "m"], "d16": ["u", "l", "m"], "win": ["o"]}.get(kind, [])
        for what in kinds:
            for g in range(2):
                self.ogroups.append(dict(what=what, g=g, ring=tr % 2, tr=tr + 1))
                tr, d = tr + 1, d + 1
                self.ogroups[-1]["rel"] = d
        n_ops = {"mla": 2, "sel": 1, "win": 1}.get(kind, 0)
        loads = {"fox": 2, "mla": 4, "d1": 2, "d4": 2, "d16": 2, "sel": 5, "win": 5, "cmp": 0}[kind]
        hloads = {"mla": 0, "sel": 2, "win": 2, "cmp": 2}.get(kind, 6)
        self.kfree = c0["task"] - {"mla": NB, "sel": 2 * NB, "win": 4 * NB}.get(kind, 0)
        self.c1 = dict(task=c0["task"] + self.nt, tr=tr, ptA=a, ptD=d, pv=pv, ops=c0["ops"] + n_ops,
                       load=c0["load"] + loads, hload=c0["hload"] + hloads,
                       vA=self.vgroups and c0["ptA"] + 2 or c0["vA"], ttr_prev=self.tail(),
                       rl=c0["rl"] + (0 if kind in DILATED else self.nt),
                       cf=c0["cf"] + (self.nt if kind in NSA else 0),
                       oh=c0["oh"] + sum(g["what"] == "o" for g in self.ogroups))

    def tail(self):
        return [self.tasks[-2]["groups"][-1]["tr"], self.tasks[-1]["groups"][-1]["tr"]]

    def blocks(self, i):
        k = self.kind
        if k in ("fox", "mla", "sel"):
            return list(range(i + 1))
        if k == "win":
            return list(range(max(0, i - WIN_BLOCKS), i + 1))
        if k == "d1":
            return list(range(max(0, i - 1), i + 1))
        if k == "d4":
            return [i - 1, i] if i % 2 else [i]
        return [i] if k == "d16" else [0]

    def width(self, i):
        return HD if self.kind == "cmp" else P * len(self.blocks(i))


def kind_ops(j):
    return j.kind in ("mla", "sel", "win")


def token(kind, block):
    if kind == "d4":
        return block // 2 + 4 * P * (block % 2)
    return block if kind == "d16" else block * P


def build_jobs():
    c = dict(task=TASK0, tr=2, ptA=2, ptD=2, pv=2, ops=2, load=0, hload=0, vA=2, ttr_prev=[2, 2], rl=2, cf=2, oh=2)
    last = {0: None, 1: None}
    phases, flat = {}, []
    bodies = {
        "fox": (2, [("fox", 2, 0, 0), ("fox", 2, 1, 1)]),
        "mla": (4, [("mla", 2, 0, 0), ("mla", 2, 1, 1)]),
        "dil": (2, [("d1", 1, 0, 0), ("d4", 1, 0, 1), ("d16", 1, 0, 0)]),
        "nsa": (2, [("cmp", 1, 0, 0), ("sel", 1, 0, 1), ("win", 1, 0, 0)]),
    }
    groups = []
    for name, (n, body) in bodies.items():
        rows = []
        for it in range(n):
            row = []
            for kind, step, first, slot in body:
                j = Job(kind, first + step * it, slot, last[slot], c)
                j.step, j.first, j.no = step, first, len(flat)
                last[slot] = j
                c = j.c1
                row.append(j)
                flat.append(j)
            rows.append(row)
        phases[name] = (n, rows)
    a = d = 2
    for j in flat:
        for g in j.vgroups:
            a += 1
            g["rel"] = ("A", a)
            groups.append(g["rel"])
        for t in j.tasks:
            for g in t["groups"]:
                if g["eng"] == "A":
                    a += 1
                    g["rel"] = ("A", a)
                else:
                    d += 1
                    g["rel"] = ("D", d)
                groups.append(g["rel"])
        for g in j.ogroups:
            d += 1
            g["rel"] = ("D", d)
            groups.append(g["rel"])
    return phases, flat, groups


def program(nc, ins, out, stop=None):
    segs, extras, tiles, units = build_segments(EXTRA)
    phases, jobs, pt_groups = build_jobs()

    ctx = ExitStack()
    with ctx:
        nc_base = 16512 // 32 * 32

        def sb(name, shape, kb, dt=F32):
            return nc.alloc_sbuf_tensor_at(name, shape, dt, offset=nc_base + int(kb * KB))

        def sem(name):
            return ctx.enter_context(nc.semaphore(name))

        H = sb("H", [P, DC, S], 0)
        XH = sb("XH", [P, DC, S], 32, F32R)
        XL = sb("XL", [P, DC, S], 64, F32R)
        HH = sb("HH", [P, HID_GROUP, S], 96, F32R)
        HL = sb("HL", [P, HID_GROUP, S], 112, F32R)
        PP = sb("PP", [P, DC, S], 96)
        M = sb("M", [P, DC, S], 128)
        T = sb("T", [P, 2, S], 160)
        HALVES = sb("HALVES", [P, 2, 2, S], 160, F32R)
        TL, QR = HALVES[:, 0], HALVES[:, 1]
        Q = sb("Q", [P, 2, S], 168)
        R = sb("R", [P, S], 176)
        RAW = sb("RAW", [P, 2, S], 180)
        WH = sb("WH", [P, 2, S], 188, F32R)
        WL = sb("WL", [P, 2, S], 196, F32R)
        CQ = sb("CQ", [P, 3, S], 96)
        CQH = sb("CQH", [P, 3, S], 108, F32R)
        CQL = sb("CQL", [P, 3, S], 120, F32R)
        MISC1 = sb("MISC", [P, 1, S], 132)
        MISC = MISC1[:, 0]
        CS = sb("CS", [P, S], 136)
        ANG = sb("ANG", [P, 3, S], 140)
        POS = sb("POS", [P, S], 152, I32)
        KR = sb("KR", [P, S], 156)
        KT = sb("KT", [P, S], 152)
        PRAW = sb("PRAW", [P, 2, S], 40)
        QK = sb("QK", [P, 2, 4, S], 96, F32R)
        V = sb("V", [P, 2, NB, P], 128)
        RQ = sb("RQ", [P, S], 136)
        RK = sb("RK", [P, S], 140)
        RV = sb("RV", [P, S], 144)
        PB = sb("PB", [P, 2, S], 148)
        PT = sb("PT", [P, 2, HALF], 156)
        BIAS = sb("BIAS", [P, 2, 2 * S], 160)
        OT = sb("OT", [P, NB, P], 176)
        BIASD = sb("BIASD", [P, 2, 2, DIL_W], 160)
        DU = sb("DU", [P, 3, S], 48)
        DL = sb("DL", [P, 3, S], 80)
        DM = sb("DM", [P, 3, S], 164)
        OL = sb("OL", [P, NB, P], 60)
        OM = sb("OM", [P, NB, P], 92)
        CMPX = sb("CMPX", [P, 2, S + 32], 128)
        CBH = sb("CBH", [P, 2, 16, HD], 96, F32R)
        CBL = sb("CBL", [P, 2, 16, HD], 104, F32R)
        CBF = sb("CBF", [P, 2, 16, HD], 112)
        HIDF = sb("HIDF", [P, 2, 2, HD], 120)
        HIDT = sb("HIDT", [P, 2, 2, HD], 121)
        HIDU = sb("HIDU", [P, 2, 2, HD], 122)
        W2K = sb("W2K", [P, 2, P], 123)
        W2V = sb("W2V", [P, 2, HD], 124)
        GTT = sb("GTT", [12, S], 140)
        CMPMASK = sb("CMPMASK", [P, NB * HD], 137)
        BRS = sb("BRS", [16, BROW_N], 148)
        ONEHOT = sb("ONEHOT", [33, BROW_N], 160)
        o = 204.0
        IDENT = sb("IDENT", [P, P], o)
        ONES = sb("ONES", [P, P], o + 0.5)
        IDR = sb("IDR", [P, P], o + 1, F32R)
        MKR = sb("MKR", [P, P], o + 1.5, F32R)
        GAINS = sb("GAINS", [P, 10, DC], o + 2)
        QKVG = sb("QKVG", [P, 3], o + 2.3125)
        CONST = sb("CONST", [P, 8], o + 2.34375)
        NM = sb("NM", [P, 16], o + 2.375)
        L = sb("L", [P, 16], o + 2.4375)
        RL = sb("RL", [P, 16], o + 2.5)
        CF = sb("CF", [P, 16], o + 2.5625)
        GT = sb("GT", [P, NB, 12], o + 2.625)
        KCH = sb("KCH", [P, HD], o + 3, F32R)
        KCL = sb("KCL", [P, HD], o + 3.25, F32R)
        VC = sb("VC", [HD, HD], o + 3.5)
        T5 = sb("T5", [33, 16], o + 3.75)
        POSC = sb("POSC", [P, 16, 2], 127)

        ps = lambda name, shape: ctx.enter_context(nc.psum_tensor(name, shape, F32))
        ACC = ps("ACC", [P, 2, S])
        TR = ps("TR", [P, 2, HALF])
        OP = ps("OP", [P, 2, HALF])

        dram = lambda name, shape: nc.dram_tensor(name, shape, F32, kind="Internal").ap()
        y_foxs = dram("y_foxs", (8, 2, P, S))
        y_fox = dram("y_fox", (4, P, S))
        y_q = dram("y_q", (8, P, S))
        y_kv = dram("y_kv", (8, P, S))
        y_kr = dram("y_kr", (32, S))
        y_f = dram("y_f", (8, S))
        y_odds = dram("y_odds", (14, 2, P, S))
        y_odd = dram("y_odd", (10, P, S))
        b_rows = dram("b_rows", (16, BROW_N))
        b_tile = {"sel": dram("b_sel", (4, P, SEL_W)), "win": dram("b_win", (4, P, WIN_W)),
                  "d1": dram("b_d1", (4, P, DIL_W)), "d4": dram("b_d4", (4, P, DIL_W)),
                  "d16": dram("b_d16", (4, P, D16_W))}

        s_const = sem("s_const")
        s_ones = sem("s_ones")
        s_h = sem("s_h")
        s_raw = [sem("s_raw0"), sem("s_raw1")]
        s_whi = sem("s_whi")
        s_split = sem("s_split")
        s_tile = sem("s_tile")
        s_evA = sem("s_evA")
        s_evD = sem("s_evD")
        s_store = [sem("s_store0"), sem("s_store1")]
        s_cq = sem("s_cq")
        s_relu = sem("s_relu")
        s_sqh = sem("s_sqh")
        s_hhi = sem("s_hhi")
        s_hid = sem("s_hid")
        s_rope = sem("s_rope")
        s_sq = sem("s_sq")
        s_st = sem("s_st")
        s_rt = sem("s_rt")
        s_R = sem("s_R")
        s_T = sem("s_T")
        s_xh = sem("s_xh")
        s_x = sem("s_x")
        s_res = sem("s_res")
        s_sig = sem("s_sig")
        s_gm = sem("s_gm")
        s_pload = sem("s_pload")
        s_phi = sem("s_phi")
        s_p = sem("s_p")
        s_dve = sem("s_dve")
        s_ft = sem("s_ft")
        s_misc = sem("s_misc")
        s_load = sem("s_load")
        s_head = [sem("s_head0"), sem("s_head1")]
        s_phi2 = sem("s_phi2")
        s_ops = sem("s_ops")
        s_qk = sem("s_qk")
        s_ttr = sem("s_ttr")
        s_exp = sem("s_exp")
        s_tr = sem("s_tr")
        s_ptA = sem("s_ptA")
        s_ptD = sem("s_ptD")
        s_pv = sem("s_pv")
        s_ox = sem("s_ox")
        s_mg = sem("s_mg")
        s_rl = sem("s_rl")
        s_cf = sem("s_cf")
        s_o = sem("s_o")
        s_oh = sem("s_oh")
        s_bd = sem("s_bd")
        s_cb = sem("s_cb")
        s_cu = sem("s_cu")
        s_gl = sem("s_gl")
        s_ge = sem("s_ge")
        s_md = sem("s_md")
        s_cmp = sem("s_cmp")
        s_cl = sem("s_cl")
        s_cz = sem("s_cz")
        s_out = sem("s_out")

        N_CONST = 7
        block = ctx.enter_context(nc.Block())

        rounds = [("x", 8), ("cq", 2), ("ckv", 1), ("m0", 8), ("h0", 8), ("n0", 8), ("g0", 8), ("x1", 8),
                  ("m1", 8), ("h1", 8), ("n1", 8), ("g1", 8)]
        rnd, q0 = {}, 0
        for no, (name, n) in enumerate(rounds):
            rnd[name] = (no, q0, n)
            q0 += n
        src_of = {"x": H, "m0": M, "h0": H, "n0": M, "g0": H, "x1": H, "m1": M, "h1": H, "n1": M, "g1": H}
        GAIN = {"x": 0, "x1": 1, "m0": 2, "m1": 3, "h0": 4, "h1": 5, "n0": 6, "n1": 7, "g0": 8, "g1": 9}
        applies, x0 = {}, 0
        for name, n in (("x", 8), ("cq", 3), ("h0", 8), ("g0", 8), ("x1", 8), ("h1", 8), ("g1", 8)):
            applies[name] = x0
            x0 += n
        resids = {"m0": 0, "n0": 8, "ga0": 16, "m1": 24, "n1": 32, "ga1": 40}
        gate_base = [resids["ga0"], resids["ga1"]]
        tcount = {}
        t0 = 0
        for name, n in (("x", 8), ("cq", 3), ("m0", 8), ("h0", 8), ("n0", 8), ("g0", 8), ("x1", 8),
                        ("m1", 8), ("h1", 8), ("n1", 8), ("g1", 8)):
            tcount[name] = t0
            t0 += n
        TASKS_EVEN = phases["mla"][1][-1][-1].c1
        TASKS_ODD = phases["nsa"][1][-1][-1].c1
        seg_end = {n: s.iters[-1][-1].tiles_end for n, s in segs.items()}

        def chunk_of(x, name, pos, it):
            c = {"fox": it * 2 + (4 + pos), "mla": it, "dil": it, "nsa": it + 2}[name]
            return x[:, bass.ds(c, 1)].rearrange("p o s -> p (o s)")

        def run(eng, n, body):
            if n > 1:
                with eng.Fori(0, n) as it:
                    body(it)
            else:
                body(0)

        @block.sync
        def _(sp):
            sp.dma_start(H[:], ins["xT"].rearrange("c p s -> p c s")).then_inc(s_h, 16)
            for dst, key in ((IDENT, "ident"), (GAINS, "gains"), (QKVG, "qkvg"), (CONST, "const")):
                sp.dma_start(dst[:], ins[key]).then_inc(s_const, 16)
            sp.dma_start(POS[:], bass.AP(ins["positions"].tensor, 0, [[0, P], [1, S]])).then_inc(s_const, 16)
            sp.dma_start(KR[:, 0:P], ins["mask"]).then_inc(s_const, 16)
            sp.dma_start(T5[0:32, :], ins["t5"]).then_inc(s_const, 16)

            def weights(name):
                seg = segs[name]

                def body(it):
                    for pos in range(len(seg.iters[0])):
                        us = [row[pos] for row in seg.iters]
                        slot = us[0].no % 2
                        need(sp, s_split, [u.no - 1 for u in us], it)
                        sp.dma_start(RAW[:, slot], ins["w"][bass.ds(at(us[0].no, len(seg.iters[0]), it), 1)]
                                     .rearrange("o p n -> p (o n)")).then_inc(s_raw[slot], 16)
                run(sp, seg.n, body)

            def attention(name):
                n, rows = phases[name]

                def body(it):
                    for pos, j in enumerate(rows[0]):
                        js = [row[pos] for row in rows]
                        slot = j.slot
                        pair = at(j.first, j.step, it)

                        def load(dst, src):
                            sp.dma_start(dst, src).then_inc(s_load, 16)

                        def rows_of(t, idx, lo=0, hi=P):
                            return t[bass.ds(idx, 1), lo:hi].rearrange("o p s -> (o p) s")

                        def bias_free():
                            need(sp, s_ttr, [k.prev.c1["task"] if k.prev else TASK0 for k in js], it)

                        if j.vgroups:
                            need(sp, s_ptA, [k.c0["vA"] for k in js], it)
                        if kind_ops(j):
                            need(sp, s_ops, [k.c0["ops"] for k in js], it)
                        if name == "fox":
                            load(RV[:], rows_of(y_fox, pair))
                            bias_free()
                            load(BIAS[:, slot], y_f[bass.ds(pair * 2, 2)].rearrange("(o h) s -> o (h s)", o=1)
                                 .to_broadcast([P, 2 * S]))
                        elif name == "mla":
                            load(RQ[0:96], rows_of(y_q, pair, 0, 96))
                            load(RK[0:64], rows_of(y_kv, pair, 0, 64))
                            load(RK[64:96], y_kr)
                            load(RV[0:64], rows_of(y_kv, pair, 64, 128))
                        elif name == "dil":
                            g = DILATED.index(j.kind)
                            w = D16_W if g == 2 else DIL_W
                            load(RV[:], rows_of(y_odd, pair + 2 * g))
                            bias_free()
                            load(BIASD[:, slot, :, 0:w],
                                 b_tile[j.kind][bass.ds(pair * 2, 2)].rearrange("h p u -> p h u"))
                        elif j.kind != "cmp":
                            c = 7 if j.kind == "sel" else 8
                            w = SEL_W if j.kind == "sel" else WIN_W
                            for r in (0, 64):
                                load(RK[r:r + 64], y_odd[c, 0:64])
                                load(RV[r:r + 64], y_odd[c, 64:128])
                            bias_free()
                            load(BIAS[:, slot, 0:2 * w].rearrange("p (h u) -> p h u", h=2),
                                 b_tile[j.kind][bass.ds(pair * 2, 2)].rearrange("h p u -> p h u"))
                        if name == "mla":
                            continue
                        y, q, k_ = {"fox": (y_foxs, 0, 4), "dil": (y_odds, 0, 6), "nsa": (y_odds, 12, None)}[name]
                        g = 2 * DILATED.index(j.kind) if name == "dil" else 0
                        for e in range(2):
                            need(sp, s_qk, [k.c0["task"] - NB * (1 - e) for k in js], it)
                            rows_e = slice(e * HD, (e + 1) * HD)
                            for half in range(2):
                                src = y[bass.ds(pair + q + g, 1), 1 - half, rows_e].rearrange("o p s -> (o p) s")
                                sp.dma_start(QK[half * HD:(half + 1) * HD, e, 0].bitcast(F32), src).then_inc(s_head[e], 16)
                            if k_ is None:
                                continue
                            for r in (0, 64):
                                for half in range(2):
                                    src = y[bass.ds(pair + k_ + g, 1), 1 - half, rows_e].rearrange("o p s -> (o p) s")
                                    sp.dma_start(QK[r:r + HD, e, 2 + half].bitcast(F32), src).then_inc(s_head[e], 16)
                run(sp, n, body)

            def p_load(l):
                sp.wait_ge(s_tile, seg_end[f"mlp{l}"])
                sp.dma_start(PRAW[:], ins["pT"][l].rearrange("c p s -> p c s")).then_inc(s_pload, 16)

            for name in ("in0a", "in0b", "in0c", "up0"):
                weights(name)
            last = tiles[seg_end["up0"] - 1]
            sp.wait_ge(s_store[0], 16 * last.store[0])
            sp.wait_ge(s_store[1], 16 * last.store[1])
            sp.wait_ge(s_misc, 32)
            sp.wait_ge(s_tile, seg_end["up0"])
            sp.wait_ge(s_evD, last.dve)
            sp.wait_ge(s_x, applies["cq"] + 3)
            attention("fox")
            sp.wait_ge(s_ttr, phases["fox"][1][-1][-1].c1["task"])
            sp.dma_start(BIAS[:, 0, 0:S], ins["mlamask"]).then_inc(s_const, 16)
            attention("mla")
            weights("out0")
            weights("mlp0")
            p_load(0)
            weights("ple0")
            weights("gate0")
            if stop == "l0":
                sp.wait_ge(s_res, resids["ga0"] + 8)
                sp.dma_start(out.rearrange("c p s -> p c s"), H[:]).then_inc(s_out, 16)
                sp.wait_ge(s_out, 16)
                return
            for name in ("in1a", "in1b", "in1c"):
                weights(name)
            last = tiles[seg_end["in1c"] - 1]
            sp.wait_ge(s_store[0], 16 * last.store[0])
            sp.wait_ge(s_store[1], 16 * last.store[1])
            sp.dma_start(ONEHOT[:], ins["onehot"]).then_inc(s_cl, 16)
            for which in range(2):
                src = y_odd[6, 64 * which:64 * which + 64]
                sp.dma_start(CMPX[0:64, which, 0:S], src).then_inc(s_cl, 16)
                sp.dma_start(CMPX[64:128, which, 0:S - 1], src[:, 1:S]).then_inc(s_cl, 16)
            sp.dma_start(POSC[:], ins["posc"]).then_inc(s_cl, 16)
            sp.dma_start(GTT[:], y_odd[9, 0:12]).then_inc(s_cl, 16)
            sp.dma_start(CMPMASK[:], ins["cmpmask"]).then_inc(s_cl, 16)
            sp.dma_start(W2K[:], ins["w2k"]).then_inc(s_cl, 16)
            sp.dma_start(W2V[:], ins["w2v"]).then_inc(s_cl, 16)
            weights("cmp")
            sp.wait_ge(s_evA, extras["cmp"][2].act)
            sp.dma_start(b_rows, BRS[:]).then_inc(s_bd, 16)
            sp.wait_ge(s_bd, 16)

            def skew(kind, head0, width):
                src = bass.AP(b_rows.tensor, head0 * BROW_N + BROW[kind] + P - 1, [[BROW_N, 4], [-1, P], [1, width]])
                sp.dma_start(b_tile[kind], src).then_inc(s_bd, 16)

            skew("sel", 12, SEL_W)
            skew("win", 12, WIN_W)
            skew("d1", 0, DIL_W)
            skew("d4", 4, DIL_W)
            skew("d16", 8, D16_W)
            sp.wait_ge(s_bd, 16 * 6)
            kc = extras["out1"][0]
            sp.wait_ge(s_evA, kc.act)
            sp.wait_ge(s_evD, kc.dve)
            attention("dil")
            sp.wait_ge(s_ox, 2)
            attention("nsa")
            weights("out1")
            weights("mlp1")
            p_load(1)
            weights("ple1")
            weights("gate1")
            sp.wait_ge(s_res, resids["ga1"] + 8)
            sp.dma_start(out.rearrange("c p s -> p c s"), H[:]).then_inc(s_out, 16)
            sp.wait_ge(s_out, 16)


        @block.gpsimd
        def _(pool):
            for s in (s_ops, s_phi2):
                pool.sem_inc(s, 2)
            nc.gpsimd.memset(ONES[:], 1.0).then_inc(s_ones, 1)
            pool.wait_ge(s_ones, 1)
            nc.gpsimd.memset(T5[32:33, :], NEG).then_inc(s_ones, 1)
            pool.wait_ge(s_ones, 2)
            pool.wait_ge(s_const, 16 * N_CONST)
            nc.gpsimd.tensor_copy(IDR[:], IDENT[:]).then_inc(s_ones, 1)
            nc.gpsimd.tensor_copy(MKR[:], KR[:, 0:P]).then_inc(s_ones, 1)

            def weights(name):
                seg = segs[name]

                def body(it):
                    for pos in range(len(seg.iters[0])):
                        us = [row[pos] for row in seg.iters]
                        slot = us[0].no % 2
                        need(pool, s_raw[slot], [16 * (u.no // 2 + 1) for u in us], it)
                        need(pool, s_tile, [units[u.no - 2].tiles_end if u.no > 1 else 0 for u in us], it)
                        if name == "cmp" and pos in (2, 3, 4, 6, 7):
                            pool.wait_ge(s_cu, pos - 1 if pos < 5 else pos - 2)
                        nc.gpsimd.tensor_copy(WH[:, slot], RAW[:, slot]).then_inc(s_whi, 1)
                        need(pool, s_whi, [u.no + 1 for u in us], it)
                        nc.gpsimd.tensor_tensor(WL[:, slot], RAW[:, slot], WH[:, slot].bitcast(F32),
                                                ALU.subtract).then_inc(s_split, 1)
                run(pool, seg.n, body)

            def attention(name):
                n, rows = phases[name]

                def body(it):
                    for pos, j in enumerate(rows[0]):
                        js = [row[pos] for row in rows]
                        pairs = {"mla": [(0, RQ), (2, RK)], "sel": [(2, RK)], "win": [(2, RK)]}.get(j.kind, [])
                        if not pairs:
                            continue
                        need(pool, s_load, [16 * k.c1["load"] for k in js], it)
                        need(pool, s_qk, [k.kfree for k in js], it)
                        for part, raw in pairs:
                            nc.gpsimd.tensor_copy(QK[:, j.slot, part], raw[:]).then_inc(s_phi2, 1)
                        for m, (part, raw) in enumerate(pairs):
                            need(pool, s_phi2, [k.c0["ops"] + m + 1 for k in js], it)
                            nc.gpsimd.tensor_tensor(QK[:, j.slot, part + 1], raw[:],
                                                    QK[:, j.slot, part].bitcast(F32), ALU.subtract).then_inc(s_ops, 1)
                run(pool, n, body)

            def split_p(l):
                pool.wait_ge(s_pload, 16 * (l + 1))
                nc.gpsimd.tensor_copy(XH[:, 0:2], PRAW[:]).then_inc(s_phi, 1)
                pool.wait_ge(s_phi, l + 1)
                nc.gpsimd.tensor_tensor(XL[:, 0:2], PRAW[:], XH[:, 0:2].bitcast(F32),
                                        ALU.subtract).then_inc(s_p, 1)

            for name in ("in0a", "in0b", "in0c", "up0"):
                weights(name)
            last = tiles[seg_end["up0"] - 1]
            pool.wait_ge(s_evD, last.dve)
            pool.wait_ge(s_misc, 32)
            pool.wait_ge(s_split, segs["up0"].iters[0][-1].no + 1)
            nc.gpsimd.memset(RQ[96:128], 0.0).then_inc(s_ones, 1)
            pool.wait_ge(s_ones, 5)
            nc.gpsimd.memset(RK[96:128], 0.0).then_inc(s_ones, 1)
            pool.wait_ge(s_ones, 6)
            attention("mla")
            weights("out0")
            weights("mlp0")
            split_p(0)
            weights("ple0")
            weights("gate0")
            if stop == "l0":
                return
            for name in ("in1a", "in1b", "in1c"):
                weights(name)
            pool.wait_ge(s_tile, seg_end["in1c"])
            nc.gpsimd.memset(CMPX[0:64, :, S:S + 32], 0.0).then_inc(s_cz, 1)
            pool.wait_ge(s_cz, 1)
            nc.gpsimd.memset(CMPX[64:128, :, S - 1:S + 32], 0.0).then_inc(s_cz, 1)
            pool.wait_ge(s_cz, 2)
            weights("cmp")
            attention("nsa")
            pool.wait_ge(s_cu, 6)
            weights("out1")
            weights("mlp1")
            split_p(1)
            weights("ple1")
            weights("gate1")

        @block.tensor
        def _(pe):
            def operands(src):
                return {"x": (XH, XL), "hid": (HH, HL), "cq": (CQH[:, 0:2], CQL[:, 0:2]),
                        "ckv": (CQH[:, 2:3], CQL[:, 2:3]), "p": (XH, XL)}[src]

            def evacuated(ts, it):
                for s, what in ((s_evA, "act"), (s_evD, "dve")):
                    vals = [tiles[t.no - 2].released()[what] if t.no > 1 else 0 for t in ts]
                    need(pe, s, vals, it)

            def three_pass(acc, k0, kn, ws, wl_, xh, xl, first, last):
                mm = None
                for k in range(k0, kn):
                    for w, x in ((ws, xh), (ws, xl), (wl_, xh)):
                        for h in range(2):
                            mm = nc.tensor.matmul(acc[:, h * HALF:(h + 1) * HALF], w(k), x[:, k, h * HALF:(h + 1) * HALF],
                                                  start=first and k == k0 and w is ws and x is xh,
                                                  stop=last and k == kn - 1 and w is wl_)
                return mm

            def weights(name, ready=None):
                seg = segs[name]

                def body(it):
                    for pos in range(len(seg.iters[0])):
                        us = [row[pos] for row in seg.iters]
                        u, slot = us[0], us[0].no % 2
                        need(pe, s_split, [v.no + 1 for v in us], it)
                        xh, xl = operands(u.src)
                        for m in range(len(u.tiles)):
                            ts = [v.tiles[m] for v in us]
                            evacuated(ts, it)
                            for k in range(u.k):
                                if ready:
                                    ready(pe, k, it, us, m)
                                col = (m * u.k + k) * P
                                mm = three_pass(ACC[:, ts[0].pair], k, k + 1,
                                                lambda _: WH[:, slot, col:col + P],
                                                lambda _: WL[:, slot, col:col + P], xh, xl,
                                                k == 0, k == u.k - 1)
                            mm.then_inc(s_tile, 1)
                run(pe, seg.n, body)

            def stats(name):
                no, q, n = rnd[name]
                if no:
                    pe.wait_ge(s_rt, no)
                for c in range(n):
                    pe.wait_ge(s_sq, q + c + 1)
                    for h in range(2):
                        mm = nc.tensor.matmul(OP[:, h], ONES[:], Q[:, (q + c) % 2, h * HALF:(h + 1) * HALF],
                                              start=c == 0, stop=c == n - 1)
                    mm.then_inc(s_st, 1)

            def x_ready(name):
                def ready(pe, k, it, us, m):
                    if us[0].no == 0:
                        pe.wait_ge(s_x, applies[name] + k + 1)
                return ready

            def ring_free(gs, it, eng=pe):
                prev = [pt_groups[g["tr"] - 5] if g["tr"] > 4 else None for g in gs]
                who = {p[0] for p in prev if p}
                assert len(who) <= 1, prev
                if who:
                    need(eng, s_ptA if who == {"A"} else s_ptD, [p[1] if p else 2 for p in prev], it)

            def attention(name):
                n, rows = phases[name]

                def body(it):
                    for pos, j in enumerate(rows[0]):
                        js = [row[pos] for row in rows]
                        slot, kind = j.slot, j.kind
                        for g, vg in enumerate(j.vgroups):
                            gs = [k.vgroups[g] for k in js]
                            if g == 0:
                                need(pe, s_load, [16 * k.c1["load"] for k in js], it)
                            ring_free(gs, it)
                            r = HD if kind == "mla" else P
                            for b in range(4):
                                i = 4 * g + b
                                c, t0 = {"d4": 4, "d16": 8}.get(kind, 1), token(kind, i)
                                src = RV[0:r, t0:t0 + c * (P - 1) + 1:c]
                                tr = nc.tensor.transpose(TR[:, vg["ring"], b * r:(b + 1) * r], src,
                                                         IDENT[0:r, 0:r])
                            tr.then_inc(s_tr, 1)
                        if kind_ops(j):
                            need(pe, s_ops, [k.c1["ops"] for k in js], it)

                        def logits(n):
                            t = j.tasks[n]
                            e, i, b = t["e"], t["i"], t["T"] % 2
                            need(pe, s_ttr, [k.tasks[n]["T"] - 1 for k in js], it)
                            w = j.width(i)
                            if kind != "mla" and i == 0:
                                need(pe, s_head[e], [16 * k.c1["hload"] for k in js], it)
                            c = {"d4": 4, "d16": 8}.get(kind, 1)
                            span = lambda x, b0, n: x[:, token(kind, b0):token(kind, b0) + c * (n - 1) + 1:c]
                            hs = slot if kind == "mla" else e
                            ks = slot if kind in ("mla", "sel", "win") else e
                            q, ql = (span(QK[:, hs, m], i, P) for m in range(2))
                            if kind == "cmp":
                                kh, kl = KCH[:], KCL[:]
                            else:
                                kh, kl = (span(QK[:, ks, 2 + m], t["blocks"][0], w) for m in range(2))
                            passes = [(q, kh), (ql, kh), (q, kl)] if kind == "mla" else [(q, kh), (q, kl)]
                            for c0 in range(0, w, HALF):
                                c1 = min(w, c0 + HALF)
                                masked = kind == "fox" and c1 == w
                                for m, (x, k) in enumerate(passes):
                                    mm = nc.tensor.matmul(ACC[:, b, c0:c1], x, k[:, c0:c1], start=m == 0,
                                                          stop=m == len(passes) - 1 and not masked)
                                if masked:
                                    mm = nc.tensor.matmul(ACC[:, b, w - P:w], IDR[:], MKR[:],
                                                          start=False, stop=True)
                            mm.then_inc(s_qk, 1)

                        def turn(n):
                            t = j.tasks[n]
                            b = t["T"] % 2
                            need(pe, s_exp, [k.tasks[n]["T"] + 1 for k in js], it)
                            for m, g in enumerate(t["groups"]):
                                ring_free([k.tasks[n]["groups"][m] for k in js], it)
                                for x in range(g["g0"], g["g1"]):
                                    w = HD if kind == "cmp" else P
                                    y = x - g["g0"]
                                    tr = nc.tensor.transpose(TR[0:w, g["ring"], y * P:(y + 1) * P],
                                                             PB[:, b, x * w:(x + 1) * w], IDENT[:])
                                tr.then_inc(s_tr, 1)

                        def values(n):
                            t = j.tasks[n]
                            e, b = t["e"], t["T"] % 2
                            need(pe, s_o, [k.tasks[n]["T"] - 1 for k in js], it)
                            for m, g in enumerate(t["groups"]):
                                need(pe, s_ptA if g["eng"] == "A" else s_ptD,
                                     [k.tasks[n]["groups"][m]["rel"][1] for k in js], it)
                                pr = (g["pv"] - 1) % 2
                                for x in range(g["g0"], g["g1"]):
                                    y = x - g["g0"]
                                    if kind == "cmp":
                                        lhs, rhs = PT[0:HD, pr, 0:P], VC[:]
                                    else:
                                        lhs = PT[:, pr, y * P:(y + 1) * P]
                                        rhs = V[:, slot, t["blocks"][x], HD * e:HD * e + HD]
                                    mm = nc.tensor.matmul(OP[:, b, 0:HD], lhs, rhs, start=x == 0,
                                                          stop=x == len(t["blocks"]) - 1)
                                mm.then_inc(s_pv, 1)

                        for step in range(j.nt + 2):
                            if step >= 2:
                                turn(step - 2)
                            if step < j.nt:
                                logits(step)
                            if step == 2 and j.vgroups:
                                need(pe, s_ptA, [k.vgroups[1]["rel"][1] for k in js], it)
                            if step >= 2:
                                values(step - 2)
                        for m, g in enumerate(j.ogroups):
                            if m == 0:
                                need(pe, s_o, [k.c1["task"] for k in js], it)
                            ring_free([k.ogroups[m] for k in js], it)
                            src = {"o": OT, "u": OT, "l": OL, "m": OM}[g["what"]]
                            for y in range(4):
                                tr = nc.tensor.transpose(TR[:, g["ring"], y * P:(y + 1) * P],
                                                         src[:, 4 * g["g"] + y], IDENT[:])
                            tr.then_inc(s_tr, 1)
                run(pe, n, body)

            def ple(l, round_name):
                pe.wait_ge(s_p, l + 1)
                weights(f"ple{l}")

            def hid_ready(l):
                def ready(pe, k, it, us, m):
                    if us[0].src == "hid" and us[0].tiles[0].idx == 0 and m == 0:
                        need(pe, s_hid, [T_SLOTS + u.tiles[0].up - HID_GROUP + k + 1 for u in us], it)
                    if us[0].src == "x" and us[0].tiles[0].idx == 0 and k == 0:
                        pe.wait_ge(s_x, applies[f"h{l}"] + 8)
                return ready

            for s, n in ((s_tr, 2), (s_pv, 2), (s_qk, TASK0)):
                pe.sem_inc(s, n)
            pe.wait_ge(s_ones, 4)
            stats("x")
            weights("in0a", x_ready("x"))
            stats("cq")
            stats("ckv")
            weights("in0b")
            weights("in0c")
            pe.wait_ge(s_x, applies["cq"] + 3)
            weights("up0")
            last = tiles[seg_end["up0"] - 1]
            pe.wait_ge(s_evA, last.act)
            pe.wait_ge(s_evD, last.dve)
            pe.wait_ge(s_rt, 3)
            attention("fox")
            attention("mla")
            pe.wait_ge(s_ttr, TASKS_EVEN["task"])
            pe.wait_ge(s_ptD, TASKS_EVEN["ptD"])
            weights("out0")
            pe.wait_ge(s_o, TASKS_EVEN["task"])
            stats("m0")
            stats("h0")
            weights("mlp0", hid_ready(0))
            stats("n0")
            ple(0, "n0")
            stats("g0")
            pe.wait_ge(s_x, applies["g0"] + 8)
            weights("gate0")
            if stop == "l0":
                return
            stats("x1")
            pe.wait_ge(s_x, applies["x1"] + 8)
            for name in ("in1a", "in1b", "in1c"):
                weights(name)

            pe.wait_ge(s_cl, 16 * 10)
            for g in range(3):
                t = extras["cmp"][g]
                evacuated([t], 0)
                for h in range(2):
                    c0 = g * S + h * HALF
                    c1 = min(BROW_N, c0 + HALF)
                    mm = nc.tensor.matmul(ACC[0:16, t.pair, h * HALF:h * HALF + c1 - c0], T5[:], ONEHOT[:, c0:c1],
                                          start=True, stop=True)
                mm.then_inc(s_tile, 1)
            t = extras["cmp"][3]
            evacuated([t], 0)
            for i in range(NB):
                tr = nc.tensor.transpose(ACC[:, t.pair, i * 12:(i + 1) * 12], GTT[:, i * P:(i + 1) * P],
                                         IDENT[0:12, 0:12])
            tr.then_inc(s_tile, 1)
            for pos, u in enumerate(segs["cmp"].iters[0]):
                which, slot = pos // 4, u.no % 2
                t = segs["cmp"].iters[0][4 * which + 3].tiles[0]
                if pos % 4 == 0:
                    evacuated([t], 0)
                if pos == 0:
                    pe.wait_ge(s_cmp, 2)
                pe.wait_ge(s_split, u.no + 1)
                for mm4 in range(4):
                    m = 4 * (pos % 4) + mm4
                    for c in range(2):
                        for n3, (w, x) in enumerate(((WH, CBH), (WH, CBL), (WL, CBH))):
                            mm = nc.tensor.matmul(ACC[:, t.pair, c * HALF:c * HALF + HD],
                                                  w[:, slot, mm4 * 256 + c * P:mm4 * 256 + (c + 1) * P],
                                                  x[:, which, m], start=m == 0 and n3 == 0,
                                                  stop=m == 15 and n3 == 2)
                mm.then_inc(s_tile if pos % 4 == 3 else s_cu, 1)
            t = extras["out1"][0]
            evacuated([t], 0)
            pe.wait_ge(s_gl, GELU_STEPS)
            for c in range(2):
                nc.tensor.matmul(ACC[:, t.pair, 0:HD], W2K[:, c], HIDU[:, 0, c], start=c == 0, stop=c == 1)
            for c in range(2):
                mm = nc.tensor.matmul(ACC[0:HD, t.pair, HALF:HALF + HD], HIDU[:, 1, c], W2V[:, c],
                                      start=c == 0, stop=c == 1)
            mm.then_inc(s_tile, 1)
            pe.wait_ge(s_evA, t.act)
            pe.wait_ge(s_evD, t.dve)
            pe.wait_ge(s_rt, rnd["x1"][0] + 1)
            attention("dil")
            attention("nsa")
            pe.wait_ge(s_ttr, TASKS_ODD["task"])
            pe.wait_ge(s_ox, 2)
            pe.wait_ge(s_ptD, TASKS_ODD["ptD"])
            weights("out1")
            pe.wait_ge(s_o, TASKS_ODD["task"])
            stats("m1")
            stats("h1")
            weights("mlp1", hid_ready(1))
            stats("n1")
            ple(1, "n1")
            stats("g1")
            pe.wait_ge(s_x, applies["g1"] + 8)
            weights("gate1")

        @block.scalar
        def _(act):
            def stats(name, src, ready):
                no, q, n = rnd[name]
                for c in range(n):
                    ready(c)
                    if q + c > 1:
                        act.wait_ge(s_st, q + c - 1)
                    nc.scalar.activation(Q[:, (q + c) % 2], src(c), ACT.Square).then_inc(s_sq, 1)
                act.wait_ge(s_st, q + n)
                nc.scalar.activation(R[:], OP[:].rearrange("p h s -> p (h s)"), ACT.Sqrt, bias=CONST[:, 0:1],
                                     scale=1.0 / (n * P)).then_inc(s_rt, 1)

            def apply(name, hi, n=8):
                for c in range(n):
                    act.wait_ge(s_T, tcount[name] + c + 1)
                    nc.scalar.activation(hi[:, c], T[:, (tcount[name] + c) % 2], ACT.Copy).then_inc(s_xh, 1)

            def tile_loop(name, fn):
                seg = segs[name]

                def body(it):
                    for pos in range(len(seg.iters[0])):
                        us = [row[pos] for row in seg.iters]
                        for m in range(len(us[0].tiles)):
                            fn([u.tiles[m] for u in us], it)
                run(act, seg.n, body)

            def wide(t):
                return ACC[:, t.pair]

            def store(ts, it):
                t = ts[0]
                need(act, s_tile, [x.no + 1 for x in ts], it)
                need(act, s_store[t.pair], [16 * x.slot_before[t.pair] for x in ts], it)
                rows = HD if t.kind == "uq" else P
                split = t.kind in SPLIT
                nc.scalar.activation((QR if split else Q)[0:rows, t.pair], ACC[0:rows, t.pair],
                                     ACT.Copy).then_inc(s_evA, 1)
                step = ts[1].idx - ts[0].idx if len(ts) > 1 else 0
                need(act, s_evA, [x.act for x in ts], it)
                if split:
                    need(act, s_evD, [x.dve for x in ts], it)
                    y = y_foxs if t.kind == "foxs" else y_odds
                    act.dma_start(y[bass.ds(at(t.idx, step, it), 1)].rearrange("o h p s -> p (o h) s"),
                                  HALVES[:, :, t.pair].bitcast(F32)).then_inc(s_store[t.pair], 16)
                    return
                if t.kind == "uq":
                    act.wait_ge(s_rope, ROPE_KEY_STEPS + 2 * t.idx + 2)
                dst = {"fox": y_fox, "odd": y_odd, "uq": y_q, "ukv": y_kv}[t.kind]
                rows = 96 if t.kind == "uq" else P
                act.dma_start(dst[bass.ds(at(t.idx, step, it), 1), 0:rows].rearrange("o p s -> (o p) s"),
                              Q[0:rows, t.pair]).then_inc(s_store[t.pair], 16)

            def keep(dst):
                def fn(ts, it):
                    t = ts[0]
                    need(act, s_tile, [x.no + 1 for x in ts], it)
                    step = ts[1].idx - ts[0].idx if len(ts) > 1 else 0
                    if step:
                        d = dst[:, bass.ds(at(t.idx, step, it), 1)].rearrange("p o s -> p (o s)")
                    else:
                        d = dst[:, t.idx]
                    nc.scalar.activation(d, wide(t), ACT.Copy).then_inc(s_evA, 1)
                return fn

            def mlp(ts, it):
                t = ts[0]
                if t.kind != "up":
                    return
                slot = (t.up - 1) % 2
                need(act, s_tile, [x.no + 1 for x in ts], it)
                need(act, s_hid, [T_SLOTS + x.up - 2 for x in ts], it)
                nc.scalar.activation(T[:, slot], wide(t), ACT.Relu).then_inc(s_evA, 1)
                need(act, s_evA, [x.act for x in ts], it)
                nc.scalar.activation(T[:, slot], T[:, slot], ACT.Square).then_inc(s_sqh, 1)

            def gate(ts, it):
                t = ts[0]
                slot = (t.gate - 1) % 2
                need(act, s_tile, [x.no + 1 for x in ts], it)
                need(act, s_res, [gate_base[x.gate > 8] + (x.gate - 1) % 8 - 1 for x in ts], it)
                nc.scalar.activation(T[:, slot], wide(t), ACT.Sigmoid).then_inc(s_evA, 1)

            def attention(name):
                n, rows = phases[name]

                def body(it):
                    for pos, j in enumerate(rows[0]):
                        js = [row[pos] for row in rows]
                        slot, kind = j.slot, j.kind
                        for g, vg in enumerate(j.vgroups):
                            need(act, s_tr, [k.vgroups[g]["tr"] for k in js], it)
                            if g == 0:
                                need(act, s_pv, [k.prev.c1["pv"] if k.prev else 2 for k in js], it)
                            r = HD if kind == "mla" else P
                            nc.scalar.activation(V[:, slot, 4 * g:4 * g + 4, 0:r],
                                                 TR[:, vg["ring"], 0:4 * r].rearrange("p (b f) -> p b f", b=4),
                                                 ACT.Copy).then_inc(s_ptA, 1)

                        def copies(n):
                            for m, g in enumerate(j.tasks[n]["groups"]):
                                if g["eng"] != "A":
                                    continue
                                gs = [k.tasks[n]["groups"][m] for k in js]
                                need(act, s_tr, [x["tr"] for x in gs], it)
                                need(act, s_pv, [x["pv"] - 2 for x in gs], it)
                                w = (g["g1"] - g["g0"]) * P
                                nc.scalar.activation(PT[:, (g["pv"] - 1) % 2, 0:w], TR[:, g["ring"], 0:w],
                                                     ACT.Copy).then_inc(s_ptA, 1)

                        for step in range(j.nt + 2):
                            if step >= 2:
                                copies(step - 2)
                            if step < j.nt:
                                t = j.tasks[step]
                                need(act, s_ttr, [k.tasks[step]["T"] + 1 for k in js], it)
                                x = PB[:, t["T"] % 2, 0:j.width(t["i"])]
                                nc.scalar.activation(x, x, ACT.Exp, bias=NM[:, step:step + 1], scale=-1.0,
                                                     accum_out=L[:, step:step + 1]).then_inc(s_exp, 1)
                        for m, g in enumerate(j.ogroups):
                            if g["what"] != "o":
                                continue
                            need(act, s_tr, [k.ogroups[m]["tr"] for k in js], it)
                            nc.scalar.activation(chunk_of(XH, name, pos, it)[:, g["g"] * HALF:(g["g"] + 1) * HALF],
                                                 TR[:, g["ring"]], ACT.Copy).then_inc(s_oh, 1)
                        if kind == "d16":
                            need(act, s_md, [MERGE_STEPS * k + 5 for k in range(n)], it)
                            nc.scalar.activation(DM[:], DM[:], ACT.Exp, scale=-1.0).then_inc(s_mg, 1)
                run(act, n, body)

            for s, n in ((s_exp, TASK0), (s_ptA, 2), (s_oh, 2)):
                act.sem_inc(s, n)
            for s in s_store:
                act.sem_inc(s, 16)
            stats("x", lambda c: H[:, c], lambda c: act.wait_ge(s_h, 16) if c == 0 else None)
            apply("x", XH)
            tile_loop("in0a", lambda ts, it: keep(CQ if ts[0].kind == "cq" else MISC1)(ts, it))
            a0 = segs["in0a"].iters[0][2].tiles[0].act
            stats("cq", lambda c: CQ[:, c], lambda c: act.wait_ge(s_evA, a0) if c == 0 else None)
            apply("cq", CQH, 2)
            act.wait_ge(s_x, applies["cq"] + 2)
            stats("ckv", lambda c: CQ[:, 2 + c], lambda c: None)
            act.wait_ge(s_T, tcount["cq"] + 3)
            nc.scalar.activation(CQH[:, 2], T[:, (tcount["cq"] + 2) % 2], ACT.Copy).then_inc(s_xh, 1)
            act.wait_ge(s_dve, DVE_ANGLE)
            nc.scalar.activation(CS[:], ANG[:, 0], ACT.Sin).then_inc(s_ft, 1)
            act.wait_ge(s_dve, DVE_FZ)
            nc.scalar.activation(ANG[64:72, 2], ANG[64:72, 1], ACT.Abs).then_inc(s_ft, 1)
            act.wait_ge(s_ft, 2)
            nc.scalar.activation(ANG[64:72, 2], ANG[64:72, 2], ACT.Exp, scale=-1.0).then_inc(s_ft, 1)
            act.wait_ge(s_ft, 3)
            nc.scalar.activation(ANG[64:72, 2], ANG[64:72, 2], ACT.Ln, bias=1.0).then_inc(s_ft, 1)
            act.wait_ge(s_rope, ROPE_KEY_STEPS)
            act.dma_start(y_kr, KR[0:32]).then_inc(s_misc, 16)
            act.wait_ge(s_dve, DVE_ALL)
            act.dma_start(y_f, ANG[64:72, 0]).then_inc(s_misc, 16)
            tile_loop("in0b", store)
            tile_loop("in0c", store)
            tile_loop("up0", store)
            attention("fox")
            attention("mla")
            tile_loop("out0", keep(M))

            def layer_end(l):
                a0 = tiles[seg_end[f"out{l}"] - 1].act
                stats(f"m{l}", lambda c: M[:, c], lambda c: act.wait_ge(s_evA, a0) if c == 0 else None)
                stats(f"h{l}", lambda c: H[:, c], lambda c: act.wait_ge(s_res, resids[f"m{l}"] + c + 1))
                apply(f"h{l}", XH)
                act.wait_ge(s_x, applies[f"h{l}"] + 8)
                tile_loop(f"mlp{l}", mlp)
                d0 = tiles[seg_end[f"mlp{l}"] - 1].dve
                stats(f"n{l}", lambda c: M[:, c], lambda c: act.wait_ge(s_evD, d0 - 7 + c))
                tile_loop(f"ple{l}", keep(PP))
                stats(f"g{l}", lambda c: H[:, c], lambda c: act.wait_ge(s_res, resids[f"n{l}"] + c + 1))
                act.wait_ge(s_tile, seg_end[f"ple{l}"])
                apply(f"g{l}", XH)
                act.wait_ge(s_x, applies[f"g{l}"] + 8)
                tile_loop(f"gate{l}", gate)

            layer_end(0)
            if stop == "l0":
                return
            stats("x1", lambda c: H[:, c], lambda c: act.wait_ge(s_res, resids["ga0"] + c + 1))
            act.wait_ge(s_tile, seg_end["gate0"])
            apply("x1", XH)
            for name in ("in1a", "in1b", "in1c"):
                tile_loop(name, store)
            for g in range(3):
                t = extras["cmp"][g]
                c1 = min(BROW_N, (g + 1) * S)
                act.wait_ge(s_tile, t.no + 1)
                nc.scalar.activation(BRS[:, g * S:c1], ACC[0:16, t.pair, 0:c1 - g * S], ACT.Copy).then_inc(s_evA, 1)
            t = extras["cmp"][3]
            act.wait_ge(s_tile, t.no + 1)
            nc.scalar.activation(GT[:], ACC[:, t.pair, 0:NB * 12].rearrange("p (b g) -> p b g", g=12),
                                 ACT.Sigmoid).then_inc(s_evA, 1)
            for which in range(2):
                t = segs["cmp"].iters[0][4 * which + 3].tiles[0]
                act.wait_ge(s_tile, t.no + 1)
                nc.scalar.activation(HIDF[:, which], ACC[:, t.pair].rearrange("p (c s) -> p c s", c=2)[:, :, 0:HD],
                                     ACT.Copy).then_inc(s_evA, 1)
            act.wait_ge(s_gl, 3)
            nc.scalar.activation(HIDT[:], HIDT[:], ACT.Exp, scale=-2.0 * math.sqrt(2.0 / math.pi)).then_inc(s_ge, 1)
            t = extras["out1"][0]
            act.wait_ge(s_tile, t.no + 1)
            nc.scalar.activation(VC[:], ACC[0:HD, t.pair, HALF:HALF + HD], ACT.Copy)
            nc.scalar.activation(KCH[:], ACC[:, t.pair, 0:HD], ACT.Copy).then_inc(s_evA, 1)
            attention("dil")
            attention("nsa")
            tile_loop("out1", keep(M))
            layer_end(1)

        @block.vector
        def _(dve):
            V_ = nc.vector
            steps = [0]
            added = [0]

            def link(ins):
                steps[0] += 1
                ins.then_inc(s_dve, 1)
                dve.wait_ge(s_dve, steps[0])

            def inverse_rms(name):
                no = rnd[name][0]
                dve.wait_ge(s_rt, no + 1)
                V_.reciprocal(R[:], R[:]).then_inc(s_R, 1)
                dve.wait_ge(s_R, no + 1)

            def apply(name, src, gain, hi, lo, x0, t0, n):
                def low(c):
                    dve.wait_ge(s_xh, x0 + c + 1)
                    V_.tensor_tensor(lo(c), T[:, (t0 + c) % 2], hi(c).bitcast(F32), ALU.subtract).then_inc(s_x, 1)

                for c in range(n):
                    if x0 + c > 1:
                        dve.wait_ge(s_x, x0 + max(c - 1, 0))
                    if c == 0 and added[0]:
                        dve.wait_ge(s_res, added[0])
                    V_.scalar_tensor_tensor(out=T[:, (t0 + c) % 2], in0=src(c), scalar=gain(c), in1=R[:],
                                            op0=ALU.mult, op1=ALU.mult).then_inc(s_T, 1)
                    dve.wait_ge(s_T, t0 + c + 1)
                    if c:
                        low(c - 1)
                low(n - 1)

            def norm_h(name):
                inverse_rms(name)
                apply(name, lambda c: H[:, c], lambda c: GAINS[:, GAIN[name], c:c + 1], lambda c: XH[:, c],
                      lambda c: XL[:, c], applies[name], tcount[name], 8)

            def residual(name):
                inverse_rms(name)
                for c in range(8):
                    t0 = tcount[name] + c
                    if c > 1:
                        dve.wait_ge(s_res, added[0] + c - 1)
                    V_.scalar_tensor_tensor(out=T[:, t0 % 2], in0=M[:, c], scalar=GAINS[:, GAIN[name], c:c + 1],
                                            in1=R[:], op0=ALU.mult, op1=ALU.mult).then_inc(s_T, 1)
                    dve.wait_ge(s_T, t0 + 1)
                    V_.tensor_tensor(H[:, c], H[:, c], T[:, t0 % 2], ALU.add).then_inc(s_res, 1)
                added[0] += 8

            def tile_loop(name, fn):
                seg = segs[name]

                def body(it):
                    for pos in range(len(seg.iters[0])):
                        us = [row[pos] for row in seg.iters]
                        for m in range(len(us[0].tiles)):
                            fn([u.tiles[m] for u in us], it)
                run(dve, seg.n, body)

            def mlp(ts, it):
                t = ts[0]
                if t.kind == "up":
                    x = T[:, (t.up - 1) % 2]
                    need(dve, s_sqh, [y.up for y in ts], it)
                    V_.tensor_copy(HH[:, t.idx], x).then_inc(s_hhi, 1)
                    need(dve, s_hhi, [y.up for y in ts], it)
                    V_.tensor_tensor(HL[:, t.idx], x, HH[:, t.idx].bitcast(F32), ALU.subtract).then_inc(s_hid, 1)
                else:
                    need(dve, s_tile, [y.no + 1 for y in ts], it)
                    need(dve, s_evD, [max(0, y.dve - 8) for y in ts], it)
                    V_.tensor_tensor(M[:, t.idx], M[:, t.idx], ACC[:, t.pair], ALU.add).then_inc(s_evD, 1)

            def gate(ts, it):
                t = ts[0]
                x = T[:, (t.gate - 1) % 2]
                step = ts[1].idx - ts[0].idx
                c = lambda y: y[:, bass.ds(at(t.idx, step, it), 1)].rearrange("p o s -> p (o s)")
                need(dve, s_evA, [y.act for y in ts], it)
                V_.tensor_tensor(x, x, c(PP), ALU.mult).then_inc(s_gm, 1)
                need(dve, s_gm, [y.gate for y in ts], it)
                V_.tensor_tensor(c(H), c(H), x, ALU.add).then_inc(s_res, 1)

            def low_half(ts, it):
                t = ts[0]
                if t.kind not in SPLIT:
                    return
                need(dve, s_evA, [x.act for x in ts], it)
                need(dve, s_store[t.pair], [16 * x.slot_before[t.pair] for x in ts], it)
                V_.tensor_tensor(TL[:, t.pair], ACC[:, t.pair], QR[:, t.pair].bitcast(F32),
                                 ALU.subtract).then_inc(s_evD, 1)

            def rotate(ts, it):
                t = ts[0]
                if t.kind != "uq":
                    return
                dve.wait_ge(s_tile, t.no + 1)
                dve.wait_ge(s_store[t.pair], 16 * t.slot_before[t.pair])
                dve.wait_ge(s_rope, ROPE_KEY_STEPS + 2 * t.idx)
                V_.tensor_tensor(KT[64:96], ACC[96:128, t.pair], CS[96:128], ALU.mult).then_inc(s_rope, 1)
                V_.tensor_tensor(Q[64:96, t.pair], ACC[64:96, t.pair], CS[64:96], ALU.mult).then_inc(s_evD, 1)
                dve.wait_ge(s_rope, ROPE_KEY_STEPS + 2 * t.idx + 1)
                dve.wait_ge(s_evD, t.dve)
                V_.tensor_tensor(Q[64:96, t.pair], Q[64:96, t.pair], KT[64:96], ALU.add).then_inc(s_rope, 1)

            def attention(name):
                n_it, rows = phases[name]

                def body(it):
                    for pos, j in enumerate(rows[0]):
                        js = [row[pos] for row in rows]
                        slot, kind = j.slot, j.kind

                        def bias(t):
                            e, i, w = t["e"], t["i"], j.width(t["i"])
                            if kind == "fox":
                                return BIAS[:, slot, e * S:e * S + w]
                            if kind == "mla":
                                return BIAS[:, 0, S - P - i * P:S]
                            if kind == "sel":
                                return BIAS[:, slot, e * S + S - P - i * P:(e + 1) * S]
                            if kind == "win":
                                return BIAS[:, slot, (e + 1) * WIN_W - w:(e + 1) * WIN_W]
                            if kind == "cmp":
                                return CMPMASK[:, i * HD:(i + 1) * HD]
                            wt = D16_W if kind == "d16" else DIL_W
                            return BIASD[:, slot, e, wt - w:wt]

                        def copies(n):
                            for m, g in enumerate(j.tasks[n]["groups"]):
                                if g["eng"] != "D":
                                    continue
                                gs = [k.tasks[n]["groups"][m] for k in js]
                                need(dve, s_tr, [x["tr"] for x in gs], it)
                                need(dve, s_pv, [x["pv"] - 2 for x in gs], it)
                                w, r = (g["g1"] - g["g0"]) * P, HD if kind == "cmp" else P
                                V_.tensor_copy(PT[0:r, (g["pv"] - 1) % 2, 0:w], TR[0:r, g["ring"], 0:w])\
                                    .then_inc(s_ptD, 1)

                        def scores(n):
                            t = j.tasks[n]
                            w, b = j.width(t["i"]), t["T"] % 2
                            need(dve, s_qk, [k.tasks[n]["T"] + 1 for k in js], it)
                            if n == 0 and kind != "cmp":
                                need(dve, s_load, [16 * k.c1["load"] for k in js], it)
                            need(dve, s_tr, [k.c0["ttr_prev"][n] if n < 2 else k.tasks[n - 2]["groups"][-1]["tr"]
                                             for k in js], it)
                            V_.tensor_tensor_reduce(PB[:, b, 0:w], ACC[:, b, 0:w], bias(t),
                                                    -MLA_SCALE if kind == "mla" else -1.0 / ISCALE, 3e38,
                                                    ALU.add, ALU.min, NM[:, n:n + 1]).then_inc(s_ttr, 1)

                        def output(n):
                            t = j.tasks[n]
                            e, i, b = t["e"], t["i"], t["T"] % 2
                            need(dve, s_pv, [k.tasks[n]["groups"][-1]["pv"] for k in js], it)
                            if n == 0:
                                need(dve, s_tr, [k.c0["tr"] for k in js], it)
                            f = HD * (pos if kind == "mla" else e)
                            dst = OT[:, i, f:f + HD]
                            if kind in DILATED:
                                V_.tensor_copy(OL[:, i, f:f + HD], L[:, n:n + 1].to_broadcast([P, HD]))
                                V_.tensor_copy(OM[:, i, f:f + HD], NM[:, n:n + 1].to_broadcast([P, HD]))
                                V_.tensor_copy(dst, OP[:, b, 0:HD]).then_inc(s_o, 1)
                                return
                            V_.reciprocal(RL[:, n:n + 1], L[:, n:n + 1]).then_inc(s_rl, 1)
                            need(dve, s_rl, [k.c0["rl"] + n + 1 for k in js], it)
                            if kind not in NSA:
                                V_.tensor_scalar(dst, OP[:, b, 0:HD], RL[:, n:n + 1], None, ALU.mult)\
                                    .then_inc(s_o, 1)
                                return
                            col = at(e * 3 + NSA.index(kind), 6, it)
                            V_.tensor_tensor(CF[:, n:n + 1], RL[:, n:n + 1], GT[:, i, bass.ds(col, 1)], ALU.mult)\
                                .then_inc(s_cf, 1)
                            need(dve, s_cf, [k.c0["cf"] + n + 1 for k in js], it)
                            if kind == "cmp":
                                V_.tensor_scalar(dst, OP[:, b, 0:HD], CF[:, n:n + 1], None, ALU.mult)\
                                    .then_inc(s_o, 1)
                            else:
                                need(dve, s_o, [k.tasks[n]["T"] - 15 for k in js], it)
                                V_.scalar_tensor_tensor(out=dst, in0=OP[:, b, 0:HD], scalar=CF[:, n:n + 1], in1=dst,
                                                        op0=ALU.mult, op1=ALU.add).then_inc(s_o, 1)

                        for step in range(j.nt + 2):
                            if step >= 2:
                                copies(step - 2)
                            if step < j.nt:
                                scores(step)
                            if step >= 2:
                                output(step - 2)
                        for m, g in enumerate(j.ogroups):
                            need(dve, s_tr, [k.ogroups[m]["tr"] for k in js], it)
                            cols = slice(g["g"] * HALF, (g["g"] + 1) * HALF)
                            if g["what"] == "o":
                                need(dve, s_oh, [k.c0["oh"] + m + 1 for k in js], it)
                                V_.tensor_tensor(chunk_of(XL, name, pos, it)[:, cols], TR[:, g["ring"]],
                                                 chunk_of(XH, name, pos, it)[:, cols].bitcast(F32),
                                                 ALU.subtract).then_inc(s_ptD, 1)
                                continue
                            dst = {"u": DU, "l": DL, "m": DM}[g["what"]]
                            c = {"d1": 1, "d4": 4, "d16": 8}[kind]
                            d = dst[:, DILATED.index(kind)]
                            src = TR[:, g["ring"]]
                            if c == 1:
                                d = d[:, cols]
                            else:
                                d = d.rearrange("p (a c) -> p c a", c=c)[:, g["g"] * c // 2:(g["g"] + 1) * c // 2, :]
                                src = src.rearrange("p (c a) -> p c a", c=c // 2)
                            V_.tensor_copy(d, src).then_inc(s_ptD, 1)
                        if kind == "d16":
                            merge([k.c1["ptD"] for k in js], it)

                def merge(evacuated, it):
                    m = [0]

                    def step(ins):
                        m[0] += 1
                        ins.then_inc(s_md, 1)

                    def done():
                        need(dve, s_md, [MERGE_STEPS * k + m[0] for k in range(n_it)], it)

                    mm = OM[:].rearrange("p b f -> p (b f)")
                    need(dve, s_ptD, evacuated, it)
                    step(V_.tensor_tensor(mm, DM[:, 0], DM[:, 1], ALU.min))
                    done()
                    step(V_.tensor_tensor(mm, mm, DM[:, 2], ALU.min))
                    done()
                    for g in range(3):
                        step(V_.tensor_tensor(DM[:, g], DM[:, g], mm, ALU.subtract))
                    need(dve, s_mg, [k + 1 for k in range(n_it)], it)
                    step(V_.tensor_tensor(DU[:], DU[:], DM[:], ALU.mult))
                    step(V_.tensor_tensor(DL[:], DL[:], DM[:], ALU.mult))
                    done()
                    for g in (1, 2):
                        step(V_.tensor_tensor(DU[:, 0], DU[:, 0], DU[:, g], ALU.add))
                        step(V_.tensor_tensor(DL[:, 0], DL[:, 0], DL[:, g], ALU.add))
                        done()
                    step(V_.reciprocal(DL[:, 0], DL[:, 0]))
                    done()
                    step(V_.tensor_tensor(DU[:, 0], DU[:, 0], DL[:, 0], ALU.mult))
                    done()
                    xh, xl = chunk_of(XH, "dil", 0, it), chunk_of(XL, "dil", 0, it)
                    step(V_.tensor_copy(xh, DU[:, 0]))
                    done()
                    assert m[0] == MERGE_STEPS
                    V_.tensor_tensor(xl, DU[:, 0], xh.bitcast(F32), ALU.subtract).then_inc(s_ox, 1)

                run(dve, n_it, body)

            two_pi = 2 * math.pi
            c1 = 6.28125
            c2 = float(np.float32(np.round((two_pi - c1) * 2 ** 20) / 2 ** 20))
            c3 = float(np.float32(two_pi - c1 - c2))
            magic = float(3 << 22)
            for s, n in ((s_evD, 2), (s_ttr, TASK0), (s_o, TASK0), (s_ptD, 2), (s_rl, 2), (s_cf, 2)):
                dve.sem_inc(s, n)
            dve.wait_ge(s_const, 16 * N_CONST)
            link(V_.tensor_copy(ANG[:, 0], POS[:]))
            link(V_.tensor_scalar(ANG[:, 1], ANG[:, 0], CONST[:, 1:2], None, ALU.mult))
            link(V_.tensor_scalar(ANG[:, 2], ANG[:, 1], 1.0 / two_pi, CONST[:, 2:3], ALU.mult, ALU.add))
            link(V_.tensor_scalar(ANG[:, 2], ANG[:, 2], magic, None, ALU.add))
            link(V_.tensor_scalar(ANG[:, 2], ANG[:, 2], -magic, None, ALU.add))
            link(V_.scalar_tensor_tensor(out=ANG[:, 0], in0=ANG[:, 2], scalar=-c1, in1=ANG[:, 1], op0=ALU.mult, op1=ALU.add))
            link(V_.scalar_tensor_tensor(out=ANG[:, 1], in0=ANG[:, 2], scalar=-c2, in1=ANG[:, 0], op0=ALU.mult, op1=ALU.add))
            link(V_.scalar_tensor_tensor(out=ANG[:, 0], in0=ANG[:, 2], scalar=-c3, in1=ANG[:, 1], op0=ALU.mult, op1=ALU.add))
            link(V_.tensor_scalar(ANG[:, 0], ANG[:, 0], CONST[:, 3:4], None, ALU.add))
            link(V_.tensor_scalar(ANG[:, 0], ANG[:, 0], 3.1415925, -3.1415925, ALU.min, ALU.max))
            assert steps[0] == DVE_ANGLE
            norm_h("x")
            V_.memset(RL[:, 0:1], 0.0).then_inc(s_hid, T_SLOTS)
            for name, c0, n in (("cq", 0, 2), ("ckv", 2, 1)):
                inverse_rms(name)
                apply(name, lambda c: CQ[:, c0 + c], lambda c: QKVG[:, c0 + c:c0 + c + 1], lambda c: CQH[:, c0 + c],
                      lambda c: CQL[:, c0 + c], applies["cq"] + c0, tcount["cq"] + c0, n)
            t = segs["in0a"].iters[0][3].tiles[0]
            dve.wait_ge(s_evA, t.act)
            f0, f1, f2 = ANG[64:72, 0], ANG[64:72, 1], ANG[64:72, 2]
            link(V_.tensor_scalar(f1, MISC[64:72], CONST[64:72, 5:6], None, ALU.add))
            assert steps[0] == DVE_FZ
            dve.wait_ge(s_ft, 1)
            link(V_.tensor_scalar(CS[:], CS[:], CONST[:, 4:5], None, ALU.mult))
            link(V_.tensor_scalar(f0, f1, 0.0, None, ALU.min))
            dve.wait_ge(s_ft, 4)
            link(V_.tensor_tensor(f0, f0, f2, ALU.subtract))
            link(V_.memset(f1, 1.0))
            link(V_.tensor_tensor_scan(f2, f1, f0, 0.0, ALU.mult, ALU.add))
            link(V_.tensor_scalar(f0, f2, -ISCALE, None, ALU.mult))
            assert steps[0] == DVE_ALL, steps
            dve.wait_ge(s_ones, 4)
            V_.tensor_tensor(KT[0:32], MISC[32:64], CS[32:64], ALU.mult).then_inc(s_rope, 1)
            V_.tensor_tensor(KR[0:32], MISC[0:32], CS[0:32], ALU.mult).then_inc(s_rope, 1)
            dve.wait_ge(s_rope, 2)
            V_.tensor_tensor(KR[0:32], KR[0:32], KT[0:32], ALU.add).then_inc(s_rope, 1)
            tile_loop("in0b", low_half)
            tile_loop("up0", rotate)
            attention("fox")
            attention("mla")

            def layer_end(l):
                residual(f"m{l}")
                norm_h(f"h{l}")
                link(V_.memset(M[:], 0.0))
                tile_loop(f"mlp{l}", mlp)
                residual(f"n{l}")
                dve.wait_ge(s_tile, seg_end[f"ple{l}"])
                norm_h(f"g{l}")
                tile_loop(f"gate{l}", gate)
                added[0] += 8

            layer_end(0)
            if stop == "l0":
                return
            dve.wait_ge(s_tile, seg_end["gate0"])
            norm_h("x1")
            for name in ("in1a", "in1c"):
                tile_loop(name, low_half)
            dve.wait_ge(s_cl, 16 * 10)
            dve.wait_ge(s_cz, 2)
            for which in range(2):
                for m in range(16):
                    last = V_.tensor_scalar(CBF[:, which, m], CMPX[:, which, 2 * m:2 * m + 16 * 63 + 1:16],
                                            POSC[:, m, which:which + 1], None, ALU.add)
            last.then_inc(s_cb, 1)
            dve.wait_ge(s_cb, 1)
            V_.tensor_copy(CBH[:], CBF[:]).then_inc(s_cmp, 1)
            dve.wait_ge(s_cmp, 1)
            V_.tensor_tensor(CBL[:], CBF[:], CBH[:].bitcast(F32), ALU.subtract).then_inc(s_cmp, 1)
            t = extras["cmp"][3]
            dve.wait_ge(s_evA, t.act)
            g = GT[:, 0].rearrange("p (h b) -> p h b", b=3)[:, :, 0]
            V_.tensor_scalar(g, g, CONST[:, 6:7], None, ALU.mult).then_inc(s_cmp, 1)
            t = segs["cmp"].iters[0][7].tiles[0]
            dve.wait_ge(s_evA, t.act)
            n = [0]

            def gelu(ins):
                n[0] += 1
                ins.then_inc(s_gl, 1)
                dve.wait_ge(s_gl, n[0])

            gelu(V_.tensor_tensor(HIDT[:], HIDF[:], HIDF[:], ALU.mult))
            gelu(V_.tensor_scalar(HIDT[:], HIDT[:], 0.044715, 1.0, ALU.mult, ALU.add))
            gelu(V_.tensor_tensor(HIDT[:], HIDT[:], HIDF[:], ALU.mult))
            dve.wait_ge(s_ge, 1)
            gelu(V_.tensor_scalar(HIDT[:], HIDT[:], 1.0, None, ALU.add))
            gelu(V_.reciprocal(HIDT[:], HIDT[:]))
            gelu(V_.tensor_tensor(HIDU[:], HIDF[:], HIDT[:], ALU.mult))
            assert n[0] == GELU_STEPS
            t = extras["out1"][0]
            dve.wait_ge(s_evA, t.act)
            V_.tensor_tensor(KCL[:], ACC[:, t.pair, 0:HD], KCH[:].bitcast(F32), ALU.subtract).then_inc(s_evD, 1)
            attention("dil")
            attention("nsa")
            layer_end(1)


def t5_bucket(dist):
    n = np.maximum(dist, 0)
    ratio = np.log(np.maximum(n, 1).astype(np.float32) / np.float32(16)) / np.float32(math.log(2048 / 16))
    large = np.minimum(16 + (ratio * np.float32(16)).astype(np.int32), 31)
    return np.where(n < 16, n, large)


def onehot_rows():
    oh = np.zeros((33, BROW_N), np.float32)

    def fill(kind, width, top, ok, step=1):
        x = np.arange(width)
        d = top - x
        good = ok(d)
        b = np.where(good, t5_bucket(d * step), 32)
        oh[b, BROW[kind] + x] = ISCALE

    fill("sel", 1152, S - 1, lambda d: d >= 0)
    fill("win", 768, WIN_W - 1, lambda d: (d >= 0) & (d < 512))
    fill("d1", 384, DIL_W - 1, lambda d: (d >= 0) & (d <= 128))
    fill("d4", 384, DIL_W - 1, lambda d: (d >= 0) & (d <= 128), 4)
    fill("d16", 256, D16_W - 1, lambda d: (d >= 0) & (d % 2 == 0), 8)
    return oh


def constants():
    c = {"ident": np.eye(P, dtype=np.float32), "onehot": onehot_rows()}
    q, k = np.arange(P)[:, None], np.arange(P)[None]
    c["mask"] = np.where(k > q, np.float32(NEG * ISCALE), np.float32(0))
    u = np.arange(S)[None]
    c["mlamask"] = np.where(u - (S - P) > q, np.float32(NEG), np.float32(0))
    t = np.arange(S).reshape(NB, P).T[:, :, None]
    n = np.arange(HD)[None, None]
    ok = (16 * n + 31 <= t) & (n < N_CMP)
    c["cmpmask"] = np.where(ok, np.float32(0), np.float32(NEG * ISCALE)).reshape(P, NB * HD).copy()
    k = np.zeros((P, 8), np.float32)
    inv = (10000.0 ** (-np.arange(0, 32, 2, dtype=np.float32) / np.float32(32))).astype(np.float32)
    row = np.arange(P)
    k[:, 0] = EPS
    k[:, 1] = inv[row % 16]
    cos = (row // 32) % 2 == 0
    k[:, 2] = np.where(cos, 0.25, 0.0)
    k[:, 3] = np.where(cos, math.pi / 2, 0.0)
    k[:, 4] = np.where(cos, 1.0, np.where(row % 32 < 16, -1.0, 1.0))
    k[:, 6] = (row >= 31).astype(np.float32)
    c["const"] = k
    return c


def weight_stream(a):
    f = lambda w: np.asarray(w)[0]
    out = []

    def full(w, cols):
        x = np.zeros((D, P), np.float32)
        cols = np.asarray(cols)
        x[:, cols >= 0] = w[:, cols[cols >= 0]]
        out.append(x.reshape(DC, P, P).transpose(1, 0, 2).reshape(P, D))

    def span(w, kc, c0, tiles):
        x = w[:, c0:c0 + tiles * P].reshape(kc, P, tiles, P)
        out.append(x.transpose(1, 2, 0, 3).reshape(P, D))

    r = lambda c0, n=P: list(range(c0, c0 + n))
    w = f(a["ev_w_in"])
    for c in range(3):
        full(w, r(c * P))
    kr = 384
    full(w, r(kr, 32) + r(kr + 16, 16) + r(kr, 16) + r(kr + 32 + 3 * 512, 8) + [-1] * 56)
    for c in range(12):
        full(w, r(kr + 32 + c * P))
    uq = f(a["ev_w_uq"]).reshape(256, 8, 96)
    uq = np.concatenate([uq, uq[:, :, 80:96], uq[:, :, 64:80]], axis=2).reshape(256, 1024)
    span(uq, 2, 0, 4)
    span(uq, 2, 512, 4)
    span(f(a["ev_w_ukv"]), 1, 0, 8)
    for c in range(8):
        full(f(a["ev_w_out"]), r(c * P))

    def rest(l):
        up, down = np.asarray(a["w_mlp_up"])[l], np.asarray(a["w_mlp_down"])[l]
        for g in range(N_GROUPS):
            for c in range(HID_GROUP):
                full(up, r((g * HID_GROUP + c) * P))
            for j in range(DC // 2):
                span(down[g * 512:(g + 1) * 512], 4, 2 * j * P, 2)
        for h in range(2):
            span(np.asarray(a["w_ple_proj"])[l], 2, 512 * h, 4)
        for c in range(8):
            full(np.asarray(a["w_ple_gate"])[l], r(c * P))

    rest(0)
    w = f(a["od_w_in"])
    for c in range(23):
        full(w, r(c * P))
    full(w, r(23 * P, 12) + [-1] * 116)
    for key in ("od_cmp_w1_k", "od_cmp_w1_v"):
        x = f(a[key]).reshape(4, 4, P, 256)
        for q in range(4):
            out.append(x[q].transpose(1, 0, 2).reshape(P, D))
    for c in range(4):
        span(f(a["od_w_out"]), 4, 2 * c * P, 2)
    rest(1)
    return np.stack(out)


def layout(a):
    a = {k: np.asarray(v) for k, v in a.items()}
    cols = lambda g: g.reshape(-1, P).T
    m = constants()
    m["xT"] = a["x"][0].T.reshape(DC, P, S)
    m["pT"] = a["p"][:, 0].transpose(0, 2, 1).reshape(2, 2, P, S)
    m["positions"] = a["positions"].reshape(1, S)
    m["w"] = weight_stream(a)
    gains = [a[k][l] for k in ("norm_mix_pre", "norm_mix_post", "norm_mlp_pre", "norm_mlp_post", "ple_norm")
             for l in range(2)]
    m["gains"] = np.stack([cols(g) for g in gains], axis=1)
    m["qkvg"] = np.concatenate([cols(a["ev_q_norm"][0]), cols(a["ev_kv_norm"][0])], axis=1)
    m["const"][64:72, 5] = a["ev_forget_bias"][0]
    m["t5"] = a["t5_bias"]
    pos = np.stack([a["od_cmp_pos_k"][0], a["od_cmp_pos_v"][0]])
    m["posc"] = pos.reshape(2, 16, P).transpose(2, 1, 0)
    k2 = a["od_cmp_w2_k"][0].reshape(2, P, HD).transpose(1, 0, 2)
    m["w2k"] = np.concatenate([k2, k2], axis=2)
    m["w2v"] = a["od_cmp_w2_v"][0].reshape(2, P, HD).transpose(1, 0, 2)
    return {k: np.ascontiguousarray(v) for k, v in m.items()}


STOP = None


def kernel(**inputs):
    import concourse.bacc as bacc
    from concourse.bass_utils import run_bass_kernel_spmd

    nc = bacc.Bacc("TRN2", target_bir_lowering=False, num_devices=1)
    arrays = layout(inputs)
    ins = {k: nc.dram_tensor(f"in_{k}", v.shape, mybir.dt.from_np(v.dtype), kind="ExternalInput").ap()
           for k, v in arrays.items()}
    out = nc.dram_tensor("out", (DC, P, S), F32, kind="ExternalOutput").ap()
    program(nc, ins, out, STOP)
    r = run_bass_kernel_spmd(nc, [{f"in_{k}": v for k, v in arrays.items()}], core_ids=[0])
    y = np.asarray(r.results[0]["out"])
    return np.ascontiguousarray(y.reshape(D, S).T)[None]
```

```python
import math
from contextlib import ExitStack

import numpy as np

import concourse.bass as bass
from concourse import mybir

F32 = mybir.dt.float32
F32R = mybir.dt.float32r
I32 = mybir.dt.int32
ALU = mybir.AluOpType
ACT = mybir.ActivationFunctionType
AX_X = mybir.AxisListType.X

P = 128
S = 1024
D = 1024
DC = D // P
NB = S // P
HALF = 512
HD = 64
KB = 1024
EPS = 1e-6
NEG = -1e30
ISCALE = 8.0
MLA_SCALE = 96 ** -0.5
HID_GROUP = 4
N_GROUPS = 4 * D // P // HID_GROUP
N_CMP = 63
WIN_BLOCKS = 4

SEL_W, WIN_W, DIL_W, D16_W = S, (WIN_BLOCKS + 1) * P, 2 * P, P
BROW = {"sel": 0, "win": 1152, "d1": 1920, "d4": 2304, "d16": 2688}
BROW_N = 2944


def unit_plan():
    full = lambda kind, idx, step=0, src="x": (8, src, [(kind, idx, step)])
    mlp = [full("up", c) for c in range(HID_GROUP)]
    mlp += [(4, "hid", [("down", 2 * j, 0), ("down", 2 * j + 1, 0)]) for j in range(DC // 2)]
    segs = []

    def rest(l):
        segs.append((f"mlpa{l}", 1, mlp))
        segs.append((f"mlp{l}", N_GROUPS - 2, mlp))
        segs.append((f"mlpz{l}", 1, mlp))
        segs.append((f"ple{l}", 1, [(2, "p", [("ple", 4 * a + j, 0) for j in range(4)]) for a in range(2)]))
        segs.append((f"gate{l}", 1, [full("gate", c) for c in range(DC)]))

    segs.append(("in0a", 1, [full("cq", 0), full("cq", 1), full("cq", 2), full("misc", 0)]))
    segs.append(("in0p", 1, [full("foxs", 0), full("foxs", 1)]))
    segs.append(("in0b", 3, [full("foxs", 2, 2), full("foxs", 3, 2)]))
    segs.append(("in0c", 2, [full("fox", 0, 2), full("fox", 1, 2)]))
    segs.append(("up0", 1, [(2, "cq", [("uq", 4 * a + j, 0) for j in range(4)]) for a in range(2)]
                 + [(1, "ckv", [("ukv", j, 0) for j in range(8)])]))
    segs.append(("out0", 1, [full("out", c) for c in range(DC)]))
    rest(0)
    segs.append(("in1p", 1, [full("odds", c, 0, "x1") for c in range(2)]))
    segs.append(("in1a", 5, [full("odds", c, 2, "x1") for c in (2, 3)]))
    segs.append(("in1b", 3, [full("odd", c, 2, "x1") for c in (0, 1)]))
    segs.append(("in1c", 1, [full("odds", c, 0, "x1") for c in (12, 13)] + [full("odd", c, 0, "x1") for c in range(6, 10)]))
    segs.append(("cmp", 1, [(8, "cmp", []) for _ in range(8)]))
    segs.append(("out1", 1, [(4, "x", [("out", 2 * a, 0), ("out", 2 * a + 1, 0)]) for a in range(4)]))
    rest(1)
    return segs


EXTRA = {"cmp": [("brow", 0), ("brow", 1), ("brow", 2), ("gt", 0)], "out1": [("kc", 0)]}
GELU_STEPS = 6
T_SLOTS = 2
MERGE_STEPS = 14
ROPE_KEY_STEPS = 3
DVE_ANGLE = 10
DVE_FZ = 11
DVE_ALL = 17
ACT_RELEASES = {"gt", "kc", "uq", "ukv", "out", "ple", "hid", "brow"}
DVE_RELEASES = {"cq", "misc", "fox", "foxs", "odd", "odds", "up", "down", "gate", "uq", "kc"}
SPLIT = {"foxs", "odds"}
STORED = {"fox", "odd", "uq", "ukv"} | SPLIT


class Tile:

    def __init__(self, kind, idx, no, prev):
        self.kind, self.idx, self.no, self.pair = kind, idx, no, no % 2
        self.act = (prev.act if prev else 0) + (kind in ACT_RELEASES)
        self.dve = (prev.dve if prev else 2) + (kind in DVE_RELEASES)
        self.store = list(prev.store) if prev else [1, 1]
        self.up = (prev.up if prev else 0) + (kind == "up")
        self.down = (prev.down if prev else 0) + (kind == "down")
        self.gate = (prev.gate if prev else 0) + (kind == "gate")
        self.split = (prev.split if prev else 0) + (kind in SPLIT)
        self.slot_before = list(self.store)
        if kind in STORED:
            self.store[self.pair] += 1


    def released(self):
        return {"act": self.act, "dve": self.dve}


class Unit:
    def __init__(self, no, k, src, tiles, tiles_end):
        self.no, self.k, self.src, self.tiles, self.tiles_end = no, k, src, tiles, tiles_end


class Seg:
    def __init__(self, name, n, iters):
        self.name, self.n, self.iters = name, n, iters


def build_segments(extra_before):
    segs, extras, tiles, units = {}, {}, [], []

    def tile(kind, idx):
        tiles.append(Tile(kind, idx, len(tiles), tiles[-1] if tiles else None))
        return tiles[-1]

    for name, n, body in unit_plan():
        extras[name] = [tile(*x) for x in extra_before.get(name, [])]
        iters = []
        for it in range(n):
            row = []
            for pos, (k, src, kinds) in enumerate(body):
                made = [tile(kind, i0 + it * step) for kind, i0, step in kinds]
                if name == "cmp" and pos in (3, 7):
                    made = [tile("hid", pos // 4)]
                end = len(tiles)
                units.append(Unit(len(units), k, src, made, end))
                row.append(units[-1])
            iters.append(row)
        segs[name] = Seg(name, n, iters)
    return segs, extras, tiles, units


def need(eng, sem, vals, it):
    if len(vals) == 1:
        if vals[0] > 0:
            eng.wait_ge(sem, vals[0])
        return
    if len(vals) == 2:
        slope = vals[1] - vals[0]
    else:
        slope = vals[2] - vals[1]
        assert all(vals[k + 1] - vals[k] == slope for k in range(1, len(vals) - 1)), vals
    first = vals[1] - slope
    assert first >= (slope > 0), vals
    if first < vals[0]:
        eng.wait_ge(sem, vals[0])
    if slope == 0:
        if first > 0:
            eng.wait_ge(sem, first)
        return
    eng.wait_ge(sem, it * slope + first)
    eng.nop(nofuse=True)


def at(idx0, step, it):
    return idx0 if step == 0 or isinstance(it, int) and it == 0 else it * step + idx0


TASK0 = 2 * NB
DILATED = ("d1", "d4", "d16")
NSA = ("cmp", "sel", "win")


class Job:

    def __init__(self, kind, pair, slot, prev_same_slot, c0):
        self.kind, self.pair, self.slot, self.prev = kind, pair, slot, prev_same_slot
        self.c0 = dict(c0)
        self.heads = 1 if kind == "mla" else 2
        self.nt = NB * self.heads
        self.vgroups = [] if kind == "cmp" else [dict(g=g, eng="A") for g in range(2)]
        self.tasks = []
        for n in range(self.nt):
            e, i = divmod(n, NB)
            blocks = self.blocks(i)
            t = dict(n=n, e=e, i=i, blocks=blocks, T=c0["task"] + n, groups=[])
            for g0 in range(0, len(blocks), 4):
                eng = "D" if (len(blocks) <= 4 or g0 > 0) else "A"
                t["groups"].append(dict(g0=g0, g1=min(len(blocks), g0 + 4), eng=eng))
            self.tasks.append(t)
        kinds = {"fox": ["o"], "mla": ["o"] if pair % 2 else [], "d1": ["u", "l", "m"],
                 "d4": ["u", "l", "m"], "d16": ["u", "l", "m"], "win": ["o"]}.get(kind, [])
        self.ogroups = [dict(what=what, g=g, eng="D") for what in kinds for g in range(2)]
        n_ops = {"mla": 2, "sel": 1, "win": 1}.get(kind, 0)
        loads = {"fox": 2, "mla": 4, "d1": 2, "d4": 2, "d16": 2, "sel": 5, "win": 5, "cmp": 0}[kind]
        hloads = {"mla": 0, "sel": 2, "win": 2, "cmp": 2}.get(kind, 6)
        self.kfree = c0["task"] - {"mla": NB, "sel": 2 * NB, "win": 4 * NB}.get(kind, 0)
        self.c1 = dict(task=c0["task"] + self.nt, ops=c0["ops"] + n_ops, load=c0["load"] + loads,
                       hload=c0["hload"] + hloads, rl=c0["rl"] + (0 if kind in DILATED else self.nt),
                       cf=c0["cf"] + (self.nt if kind in NSA else 0),
                       oh=c0["oh"] + sum(g["what"] == "o" for g in self.ogroups))

    def blocks(self, i):
        k = self.kind
        if k in ("fox", "mla", "sel"):
            return list(range(i + 1))
        if k == "win":
            return list(range(max(0, i - WIN_BLOCKS), i + 1))
        if k == "d1":
            return list(range(max(0, i - 1), i + 1))
        if k == "d4":
            return [i - 1, i] if i % 2 else [i]
        return [i] if k == "d16" else [0]

    def width(self, i):
        return HD if self.kind == "cmp" else P * len(self.blocks(i))


def kind_ops(j):
    return j.kind in ("mla", "sel", "win")


def token(kind, block):
    if kind == "d4":
        return block // 2 + 4 * P * (block % 2)
    return block if kind == "d16" else block * P


def pipeline(row):
    flat = [(p, n) for p, j in enumerate(row) for n in range(j.nt)]
    ends = {sum(j.nt for j in row[:p + 1]) - 1: p for p in range(len(row))}
    get = lambda k: flat[k] if 0 <= k < len(flat) else None
    return [dict(start=get(k)[0] if get(k) and get(k)[1] == 0 else None, logits=get(k), turn=get(k - 2),
                 values=get(k - 3), end=ends.get(k - 4)) for k in range(len(flat) + 4)]


def build_jobs():
    c = dict(task=TASK0, ops=2, load=0, hload=0, rl=2, cf=2, oh=2)
    last = {0: None, 1: None}
    phases, flat, pv = {}, [], 2
    bodies = {
        "fox": (2, [("fox", 2, 0, 0), ("fox", 2, 1, 1)]),
        "mla": (4, [("mla", 2, 0, 0), ("mla", 2, 1, 1)]),
        "dil": (2, [("d1", 1, 0, 0), ("d4", 1, 0, 1), ("d16", 1, 0, 0)]),
        "nsa": (2, [("cmp", 1, 0, 0), ("sel", 1, 0, 1), ("win", 1, 0, 0)]),
    }
    groups = []
    for name, (n, body) in bodies.items():
        rows = []
        for it in range(n):
            row = []
            for kind, step, first, slot in body:
                j = Job(kind, first + step * it, slot, last[slot], c)
                j.step, j.first = step, first
                for t in j.tasks:
                    for g in t["groups"]:
                        pv += 1
                        g["pv"] = pv
                last[slot] = j
                c = j.c1
                row.append(j)
                flat.append(j)
            rows.append(row)
        phases[name] = (n, rows)
    n = dict(tr=2, A=2, D=2, pv=2, vA=2, ot=2)

    def group(g):
        n["tr"] += 1
        n[g["eng"]] += 1
        g.update(tr=n["tr"], ring=(n["tr"] - 1) % 2, rel=(g["eng"], n[g["eng"]]))
        groups.append(g["rel"])

    for _, rows in phases.values():
        for row in rows:
            for st in pipeline(row):
                if st["start"] is not None:
                    j = row[st["start"]]
                    j.v_before = n["vA"]
                    for g in j.vgroups:
                        group(g)
                    if j.vgroups:
                        n["vA"] = n["A"]
                if st["values"]:
                    t = row[st["values"][0]].tasks[st["values"][1]]
                    for g in t["groups"]:
                        n["pv"] += 1
                        assert g["pv"] == n["pv"]
                if st["turn"]:
                    j = row[st["turn"][0]]
                    t = j.tasks[st["turn"][1]]
                    for g in t["groups"]:
                        group(g)
                    t["done"] = n["tr"]
                if st["end"] is not None:
                    for g in row[st["end"]].ogroups:
                        group(g)
                    if row[st["end"]].ogroups:
                        n["ot"] = n["tr"]
                if st["values"] and st["values"][1] == 0:
                    row[st["values"][0]].ot_before = n["ot"]
    before = [2, 2]
    for j in flat:
        for t in j.tasks:
            t["tr_before"] = before[0]
            before = [before[1], t["done"]]
        j.pv_end = j.tasks[-1]["groups"][-1]["pv"]
    flat[-1].counts = n
    return phases, flat, groups


def program(nc, ins, out, stop=None):
    segs, extras, tiles, units = build_segments(EXTRA)
    phases, jobs, pt_groups = build_jobs()

    ctx = ExitStack()
    with ctx:
        nc_base = 16512 // 32 * 32

        def sb(name, shape, kb, dt=F32):
            return nc.alloc_sbuf_tensor_at(name, shape, dt, offset=nc_base + int(kb * KB))

        def sem(name):
            return ctx.enter_context(nc.semaphore(name))

        H = sb("H", [P, DC, S], 0)
        XH = sb("XH", [P, DC, S], 32, F32R)
        XL = sb("XL", [P, DC, S], 64, F32R)
        HH = sb("HH", [P, HID_GROUP, S], 96, F32R)
        HL = sb("HL", [P, HID_GROUP, S], 112, F32R)
        PP = sb("PP", [P, DC, S], 96)
        M = sb("M", [P, DC, S], 128)
        T = sb("T", [P, 2, S], 160)
        HALVES = sb("HALVES", [P, 2, 2, S], 160, F32R)
        TL, QR = HALVES[:, 0], HALVES[:, 1]
        Q = sb("Q", [P, 2, S], 168)
        R = sb("R", [P, S], 176)
        RAW = sb("RAW", [P, 2, S], 180)
        WH = sb("WH", [P, 2, S], 188, F32R)
        WL = sb("WL", [P, 2, S], 196, F32R)
        CQ = sb("CQ", [P, 3, S], 96)
        CQH = sb("CQH", [P, 3, S], 108, F32R)
        CQL = sb("CQL", [P, 3, S], 120, F32R)
        MISC1 = sb("MISC", [P, 1, S], 132)
        MISC = MISC1[:, 0]
        CS = sb("CS", [P, S], 136)
        ANG = sb("ANG", [P, 3, S], 140)
        POS = sb("POS", [P, S], 152, I32)
        KR = sb("KR", [P, S], 156)
        KT = sb("KT", [P, S], 152)
        RC = sb("RC", [P, S], 148)
        PRAW = sb("PRAW", [P, 2, S], 48)
        X1H = sb("X1H", [P, DC, S], 128, F32R)
        X1L = sb("X1L", [P, DC, S], 96, F32R)
        QK = sb("QK", [P, 2, 4, S], 96, F32R)
        V = sb("V", [P, 2, NB, P], 128)
        RQ = sb("RQ", [P, S], 136)
        RK = sb("RK", [P, S], 140)
        RV = sb("RV", [P, S], 144)
        PB = sb("PB", [P, 2, S], 148)
        PT = sb("PT", [P, 2, HALF], 156)
        BIAS = sb("BIAS", [P, 2, 2 * S], 160)
        OT = sb("OT", [P, NB, P], 176)
        BIASD = sb("BIASD", [P, 2, 2, DIL_W], 160)
        DU = sb("DU", [P, 3, S], 48)
        DL = sb("DL", [P, 3, S], 80)
        DM = sb("DM", [P, 3, S], 164)
        OL = sb("OL", [P, NB, P], 60)
        OM = sb("OM", [P, NB, P], 92)
        CMPX = sb("CMPX", [P, 2, S + 32], 128)
        CBH = sb("CBH", [P, 2, 16, HD], 96, F32R)
        CBL = sb("CBL", [P, 2, 16, HD], 104, F32R)
        CBF = sb("CBF", [P, 2, 16, HD], 112)
        HIDF = sb("HIDF", [P, 2, 2, HD], 120)
        HIDT = sb("HIDT", [P, 2, 2, HD], 121)
        HIDU = sb("HIDU", [P, 2, 2, HD], 122)
        W2K = sb("W2K", [P, 2, P], 123)
        W2V = sb("W2V", [P, 2, HD], 124)
        GTT = sb("GTT", [12, S], 140)
        CMPMASK = sb("CMPMASK", [P, NB * HD], 137)
        BRS = sb("BRS", [16, BROW_N], 148)
        ONEHOT = sb("ONEHOT", [33, BROW_N], 160)
        o = 204.0
        IDENT = sb("IDENT", [P, P], o)
        ONES = sb("ONES", [P, P], o + 0.5)
        IDR = sb("IDR", [P, P], o + 1, F32R)
        MKR = sb("MKR", [P, P], o + 1.5, F32R)
        GAINS = sb("GAINS", [P, 10, DC], o + 2)
        QKVG = sb("QKVG", [P, 3], o + 2.3125)
        CONST = sb("CONST", [P, 8], o + 2.34375)
        NM = sb("NM", [P, 16], o + 2.375)
        L = sb("L", [P, 16], o + 2.4375)
        RL = sb("RL", [P, 16], o + 2.5)
        CF = sb("CF", [P, 16], o + 2.5625)
        GT = sb("GT", [P, NB, 12], o + 2.625)
        KCH = sb("KCH", [P, HD], o + 3, F32R)
        KCL = sb("KCL", [P, HD], o + 3.25, F32R)
        VC = sb("VC", [HD, HD], o + 3.5)
        T5 = sb("T5", [33, 16], o + 3.75)
        POSC = sb("POSC", [P, 16, 2], 127)

        ps = lambda name, shape: ctx.enter_context(nc.psum_tensor(name, shape, F32))
        ACC = ps("ACC", [P, 2, S])
        TR = ps("TR", [P, 2, HALF])
        OP = ps("OP", [P, 2, HALF])

        dram = lambda name, shape: nc.dram_tensor(name, shape, F32, kind="Internal").ap()
        y_foxs = dram("y_foxs", (8, 2, P, S))
        y_fox = dram("y_fox", (4, P, S))
        y_q = dram("y_q", (8, P, S))
        y_kv = dram("y_kv", (8, P, S))
        y_kr = dram("y_kr", (32, S))
        y_f = dram("y_f", (8, S))
        y_odds = dram("y_odds", (14, 2, P, S))
        y_odd = dram("y_odd", (10, P, S))
        b_rows = dram("b_rows", (16, BROW_N))
        b_tile = {"sel": dram("b_sel", (4, P, SEL_W)), "win": dram("b_win", (4, P, WIN_W)),
                  "d1": dram("b_d1", (4, P, DIL_W)), "d4": dram("b_d4", (4, P, DIL_W)),
                  "d16": dram("b_d16", (4, P, D16_W))}

        s_const = sem("s_const")
        s_ones = sem("s_ones")
        s_h = [sem(f"s_h{m}") for m in range(4)]
        s_raw = [sem("s_raw0"), sem("s_raw1")]
        s_whi = sem("s_whi")
        s_split = sem("s_split")
        s_tile = sem("s_tile")
        s_evA = sem("s_evA")
        s_evD = sem("s_evD")
        s_store = [sem("s_store0"), sem("s_store1")]
        s_hi = sem("s_hi")
        s_lo = sem("s_lo")
        s_cqn = sem("s_cqn")
        s_hhi = sem("s_hhi")
        s_sqh = sem("s_sqh")
        s_hid = sem("s_hid")
        s_rope = sem("s_rope")
        s_sq = sem("s_sq")
        s_st = sem("s_st")
        s_rt = sem("s_rt")
        s_R = sem("s_R")
        s_T = sem("s_T")
        s_xh = sem("s_xh")
        s_x = sem("s_x")
        s_res = sem("s_res")
        s_sig = sem("s_sig")
        s_gm = sem("s_gm")
        s_pload = sem("s_pload")
        s_phi = sem("s_phi")
        s_p = sem("s_p")
        s_dve = sem("s_dve")
        s_ft = sem("s_ft")
        s_misc = sem("s_misc")
        s_load = sem("s_load")
        s_head = [sem("s_head0"), sem("s_head1")]
        s_phi2 = sem("s_phi2")
        s_ops = sem("s_ops")
        s_qk = sem("s_qk")
        s_ttr = sem("s_ttr")
        s_exp = sem("s_exp")
        s_tr = sem("s_tr")
        s_ptA = sem("s_ptA")
        s_ptD = sem("s_ptD")
        s_pv = sem("s_pv")
        s_ox = sem("s_ox")
        s_mg = sem("s_mg")
        s_rl = sem("s_rl")
        s_cf = sem("s_cf")
        s_o = sem("s_o")
        s_oh = sem("s_oh")
        s_bd = sem("s_bd")
        s_cb = sem("s_cb")
        s_cu = sem("s_cu")
        s_gl = sem("s_gl")
        s_ge = sem("s_ge")
        s_md = sem("s_md")
        s_cmp = sem("s_cmp")
        s_cl = sem("s_cl")
        s_cz = sem("s_cz")
        s_out = sem("s_out")

        N_CONST = 7
        block = ctx.enter_context(nc.Block())

        rounds = [("x", 8), ("cq", 2), ("ckv", 1), ("m0", 8), ("h0", 8), ("n0", 8), ("g0", 8), ("x1", 8),
                  ("m1", 8), ("h1", 8), ("n1", 8), ("g1", 8)]
        rnd, q0 = {}, 0
        for no, (name, n) in enumerate(rounds):
            rnd[name] = (no, q0, n)
            q0 += n
        GAIN = {"x": 0, "x1": 1, "m0": 2, "m1": 3, "h0": 4, "h1": 5, "n0": 6, "n1": 7, "g0": 8, "g1": 9}
        applies, x0 = {}, 0
        for name, n in (("x", 8), ("cq", 3), ("h0", 8), ("g0", 8), ("x1", 8), ("h1", 8), ("g1", 8)):
            applies[name] = x0
            x0 += n
        resids = {"m0": 0, "n0": 8, "ga0": 16, "m1": 24, "n1": 32, "ga1": 40}
        gate_base = [resids["ga0"], resids["ga1"]]
        tcount = {"m0": 0, "n0": 8, "m1": 16, "n1": 24}
        TASKS_EVEN = phases["mla"][1][-1][-1].c1
        TASKS_ODD = phases["nsa"][1][-1][-1].c1
        COPIES = {name: rows[-1][-1].ogroups[-1]["rel"][1] for name, (_, rows) in phases.items()}
        segs_first = {n: segs[g].iters[0][0] for n, g in
                      {"x": "in0a", "h0": "mlpa0", "g0": "gate0", "x1": "in1p", "h1": "mlpa1", "g1": "gate1"}.items()}
        seg_end = {n: s.iters[-1][-1].tiles_end for n, s in segs.items()}

        def chunk_of(x, name, pos, it):
            c = {"fox": it * 2 + (4 + pos), "mla": it, "dil": it, "nsa": it + 2}[name]
            return x[:, bass.ds(c, 1)].rearrange("p o s -> p (o s)")

        def run(eng, n, body):
            if n > 1:
                with eng.Fori(0, n) as it:
                    body(it)
            else:
                body(0)

        @block.sync
        def _(sp):
            for m in range(4):
                sp.dma_start(H[:, 2 * m:2 * m + 2], ins["xT"][2 * m:2 * m + 2].rearrange("c p s -> p c s"))\
                    .then_inc(s_h[m], 16)
            for dst, key in ((IDENT, "ident"), (GAINS, "gains"), (QKVG, "qkvg"), (CONST, "const")):
                sp.dma_start(dst[:], ins[key]).then_inc(s_const, 16)
            sp.dma_start(POS[:], bass.AP(ins["positions"].tensor, 0, [[0, P], [1, S]])).then_inc(s_const, 16)
            sp.dma_start(KR[:, 0:P], ins["mask"]).then_inc(s_const, 16)
            sp.dma_start(T5[0:32, :], ins["t5"]).then_inc(s_const, 16)

            def weights(name):
                seg = segs[name]

                def body(it):
                    for pos in range(len(seg.iters[0])):
                        us = [row[pos] for row in seg.iters]
                        slot = us[0].no % 2
                        need(sp, s_split, [u.no - 1 for u in us], it)
                        sp.dma_start(RAW[:, slot], ins["w"][bass.ds(at(us[0].no, len(seg.iters[0]), it), 1)]
                                     .rearrange("o p n -> p (o n)")).then_inc(s_raw[slot], 16)
                run(sp, seg.n, body)

            def attention(name):
                n, rows = phases[name]

                def body(it):
                    for pos, j in enumerate(rows[0]):
                        js = [row[pos] for row in rows]
                        slot = j.slot
                        pair = at(j.first, j.step, it)

                        def load(dst, src):
                            sp.dma_start(dst, src).then_inc(s_load, 16)

                        def rows_of(t, idx, lo=0, hi=P):
                            return t[bass.ds(idx, 1), lo:hi].rearrange("o p s -> (o p) s")

                        def bias_free():
                            need(sp, s_ttr, [k.prev.c1["task"] if k.prev else TASK0 for k in js], it)

                        if j.vgroups:
                            need(sp, s_ptA, [k.v_before for k in js], it)
                        if kind_ops(j):
                            need(sp, s_ops, [k.c0["ops"] for k in js], it)
                        if name == "fox":
                            load(RV[:], rows_of(y_fox, pair))
                            bias_free()
                            load(BIAS[:, slot], y_f[bass.ds(pair * 2, 2)].rearrange("(o h) s -> o (h s)", o=1)
                                 .to_broadcast([P, 2 * S]))
                        elif name == "mla":
                            load(RQ[0:96], rows_of(y_q, pair, 0, 96))
                            load(RK[0:64], rows_of(y_kv, pair, 0, 64))
                            load(RK[64:96], y_kr)
                            load(RV[0:64], rows_of(y_kv, pair, 64, 128))
                        elif name == "dil":
                            g = DILATED.index(j.kind)
                            w = D16_W if g == 2 else DIL_W
                            load(RV[:], rows_of(y_odd, pair + 2 * g))
                            bias_free()
                            load(BIASD[:, slot, :, 0:w],
                                 b_tile[j.kind][bass.ds(pair * 2, 2)].rearrange("h p u -> p h u"))
                        elif j.kind != "cmp":
                            c = 7 if j.kind == "sel" else 8
                            w = SEL_W if j.kind == "sel" else WIN_W
                            for r in (0, 64):
                                load(RK[r:r + 64], y_odd[c, 0:64])
                                load(RV[r:r + 64], y_odd[c, 64:128])
                            bias_free()
                            load(BIAS[:, slot, 0:2 * w].rearrange("p (h u) -> p h u", h=2),
                                 b_tile[j.kind][bass.ds(pair * 2, 2)].rearrange("h p u -> p h u"))
                        if name == "mla":
                            continue
                        y, q, k_ = {"fox": (y_foxs, 0, 4), "dil": (y_odds, 0, 6), "nsa": (y_odds, 12, None)}[name]
                        g = 2 * DILATED.index(j.kind) if name == "dil" else 0
                        for e in range(2):
                            need(sp, s_qk, [k.c0["task"] - NB * (1 - e) for k in js], it)
                            rows_e = slice(e * HD, (e + 1) * HD)
                            for half in range(2):
                                src = y[bass.ds(pair + q + g, 1), 1 - half, rows_e].rearrange("o p s -> (o p) s")
                                sp.dma_start(QK[half * HD:(half + 1) * HD, e, 0].bitcast(F32), src).then_inc(s_head[e], 16)
                            if k_ is None:
                                continue
                            for r in (0, 64):
                                for half in range(2):
                                    src = y[bass.ds(pair + k_ + g, 1), 1 - half, rows_e].rearrange("o p s -> (o p) s")
                                    sp.dma_start(QK[r:r + HD, e, 2 + half].bitcast(F32), src).then_inc(s_head[e], 16)
                run(sp, n, body)

            def store_out(name):
                for c in range(DC):
                    sp.wait_ge(s_res, resids[name] + c + 1)
                    sp.dma_start(out[c], H[:, c]).then_inc(s_out, 16)
                sp.wait_ge(s_out, 16 * DC)

            def p_load(l):
                sp.wait_ge(s_tile, segs[f"mlpz{l}"].iters[0][HID_GROUP - 1].tiles_end)
                sp.dma_start(PRAW[:], ins["pT"][l].rearrange("c p s -> p c s")).then_inc(s_pload, 16)

            for name in ("in0a", "in0p", "in0b", "in0c", "up0"):
                weights(name)
            last = tiles[seg_end["up0"] - 1]
            sp.wait_ge(s_store[0], 16 * last.store[0])
            sp.wait_ge(s_store[1], 16 * last.store[1])
            sp.wait_ge(s_misc, 32)
            sp.wait_ge(s_tile, seg_end["up0"])
            sp.wait_ge(s_evD, last.dve)
            attention("fox")
            sp.wait_ge(s_ttr, phases["fox"][1][-1][-1].c1["task"])
            sp.dma_start(BIAS[:, 0, 0:S], ins["mlamask"]).then_inc(s_const, 16)
            attention("mla")
            weights("out0")
            for name in ("mlpa0", "mlp0", "mlpz0"):
                weights(name)
            p_load(0)
            weights("ple0")
            weights("gate0")
            if stop == "l0":
                store_out("ga0")
                return
            for name in ("in1p", "in1a", "in1b", "in1c"):
                weights(name)
            last = tiles[seg_end["in1c"] - 1]
            sp.wait_ge(s_store[0], 16 * last.store[0])
            sp.wait_ge(s_store[1], 16 * last.store[1])
            sp.dma_start(ONEHOT[:], ins["onehot"]).then_inc(s_cl, 16)
            for which in range(2):
                src = y_odd[6, 64 * which:64 * which + 64]
                sp.dma_start(CMPX[0:64, which, 0:S], src).then_inc(s_cl, 16)
                sp.dma_start(CMPX[64:128, which, 0:S - 1], src[:, 1:S]).then_inc(s_cl, 16)
            sp.dma_start(POSC[:], ins["posc"]).then_inc(s_cl, 16)
            sp.dma_start(GTT[:], y_odd[9, 0:12]).then_inc(s_cl, 16)
            sp.dma_start(CMPMASK[:], ins["cmpmask"]).then_inc(s_cl, 16)
            sp.dma_start(W2K[:], ins["w2k"]).then_inc(s_cl, 16)
            sp.dma_start(W2V[:], ins["w2v"]).then_inc(s_cl, 16)
            weights("cmp")
            sp.wait_ge(s_evA, extras["cmp"][2].act)
            sp.dma_start(b_rows, BRS[:]).then_inc(s_bd, 16)
            sp.wait_ge(s_bd, 16)

            def skew(kind, head0, width):
                src = bass.AP(b_rows.tensor, head0 * BROW_N + BROW[kind] + P - 1, [[BROW_N, 4], [-1, P], [1, width]])
                sp.dma_start(b_tile[kind], src).then_inc(s_bd, 16)

            skew("sel", 12, SEL_W)
            skew("win", 12, WIN_W)
            skew("d1", 0, DIL_W)
            skew("d4", 4, DIL_W)
            skew("d16", 8, D16_W)
            sp.wait_ge(s_bd, 16 * 6)
            kc = extras["out1"][0]
            sp.wait_ge(s_evA, kc.act)
            sp.wait_ge(s_evD, kc.dve)
            attention("dil")
            sp.wait_ge(s_ox, 2)
            attention("nsa")
            weights("out1")
            for name in ("mlpa1", "mlp1", "mlpz1"):
                weights(name)
            p_load(1)
            weights("ple1")
            weights("gate1")
            store_out("ga1")


        @block.gpsimd
        def _(pool):
            for s in (s_ops, s_phi2):
                pool.sem_inc(s, 2)
            nc.gpsimd.memset(ONES[:], 1.0).then_inc(s_ones, 1)
            pool.wait_ge(s_ones, 1)
            nc.gpsimd.memset(T5[32:33, :], NEG).then_inc(s_ones, 1)
            pool.wait_ge(s_ones, 2)
            pool.wait_ge(s_const, 16 * N_CONST)
            nc.gpsimd.tensor_copy(IDR[:], IDENT[:]).then_inc(s_ones, 1)
            nc.gpsimd.tensor_copy(MKR[:], KR[:, 0:P]).then_inc(s_ones, 1)

            def weights(name):
                seg = segs[name]

                def body(it):
                    for pos in range(len(seg.iters[0])):
                        us = [row[pos] for row in seg.iters]
                        slot = us[0].no % 2
                        need(pool, s_raw[slot], [16 * (u.no // 2 + 1) for u in us], it)
                        need(pool, s_tile, [units[u.no - 2].tiles_end if u.no > 1 else 0 for u in us], it)
                        if name == "cmp" and pos in (2, 3, 4, 6, 7):
                            pool.wait_ge(s_cu, pos - 1 if pos < 5 else pos - 2)
                        nc.gpsimd.tensor_copy(WH[:, slot], RAW[:, slot]).then_inc(s_whi, 1)
                        need(pool, s_whi, [u.no + 1 for u in us], it)
                        nc.gpsimd.tensor_tensor(WL[:, slot], RAW[:, slot], WH[:, slot].bitcast(F32),
                                                ALU.subtract).then_inc(s_split, 1)
                run(pool, seg.n, body)

            def attention(name):
                n, rows = phases[name]

                def body(it):
                    for pos, j in enumerate(rows[0]):
                        js = [row[pos] for row in rows]
                        pairs = {"mla": [(0, RQ), (2, RK)], "sel": [(2, RK)], "win": [(2, RK)]}.get(j.kind, [])
                        if not pairs:
                            continue
                        need(pool, s_load, [16 * k.c1["load"] for k in js], it)
                        need(pool, s_qk, [k.kfree for k in js], it)
                        for part, raw in pairs:
                            nc.gpsimd.tensor_copy(QK[:, j.slot, part], raw[:]).then_inc(s_phi2, 1)
                        for m, (part, raw) in enumerate(pairs):
                            need(pool, s_phi2, [k.c0["ops"] + m + 1 for k in js], it)
                            nc.gpsimd.tensor_tensor(QK[:, j.slot, part + 1], raw[:],
                                                    QK[:, j.slot, part].bitcast(F32), ALU.subtract).then_inc(s_ops, 1)
                run(pool, n, body)

            for name in ("in0a", "in0p", "in0b", "in0c", "up0"):
                weights(name)
            last = tiles[seg_end["up0"] - 1]
            pool.wait_ge(s_evD, last.dve)
            pool.wait_ge(s_misc, 32)
            pool.wait_ge(s_split, segs["up0"].iters[0][-1].no + 1)
            nc.gpsimd.memset(RQ[96:128], 0.0).then_inc(s_ones, 1)
            pool.wait_ge(s_ones, 5)
            nc.gpsimd.memset(RK[96:128], 0.0).then_inc(s_ones, 1)
            pool.wait_ge(s_ones, 6)
            attention("mla")
            weights("out0")
            for name in ("mlpa0", "mlp0", "mlpz0"):
                weights(name)
            weights("ple0")
            weights("gate0")
            if stop == "l0":
                return
            for name in ("in1p", "in1a", "in1b", "in1c"):
                weights(name)
            pool.wait_ge(s_tile, seg_end["in1c"])
            nc.gpsimd.memset(CMPX[0:64, :, S:S + 32], 0.0).then_inc(s_cz, 1)
            pool.wait_ge(s_cz, 1)
            nc.gpsimd.memset(CMPX[64:128, :, S - 1:S + 32], 0.0).then_inc(s_cz, 1)
            pool.wait_ge(s_cz, 2)
            weights("cmp")
            attention("nsa")
            pool.wait_ge(s_cu, 6)
            weights("out1")
            for name in ("mlpa1", "mlp1", "mlpz1"):
                weights(name)
            weights("ple1")
            weights("gate1")

        @block.tensor
        def _(pe):
            def operands(src):
                return {"x": (XH, XL), "hid": (HH, HL), "cq": (CQH[:, 0:2], CQL[:, 0:2]),
                        "ckv": (CQH[:, 2:3], CQL[:, 2:3]), "p": (XH[:, 6:8], XL[:, 6:8]),
                        "x1": (X1H, X1L)}[src]

            def evacuated(ts, it):
                for s, what in ((s_evA, "act"), (s_evD, "dve")):
                    vals = [tiles[t.no - 2].released()[what] if t.no > 1 else 0 for t in ts]
                    need(pe, s, vals, it)

            def three_pass(acc, k0, kn, ws, wl_, xh, xl, first, last):
                mm = None
                for k in range(k0, kn):
                    for w, x in ((ws, xh), (ws, xl), (wl_, xh)):
                        for h in range(2):
                            mm = nc.tensor.matmul(acc[:, h * HALF:(h + 1) * HALF], w(k), x[:, k, h * HALF:(h + 1) * HALF],
                                                  start=first and k == k0 and w is ws and x is xh,
                                                  stop=last and k == kn - 1 and w is wl_)
                return mm

            def weights(name, ready=None, after=None):
                seg = segs[name]

                def body(it):
                    for pos in range(len(seg.iters[0])):
                        us = [row[pos] for row in seg.iters]
                        u, slot = us[0], us[0].no % 2
                        need(pe, s_split, [v.no + 1 for v in us], it)
                        xh, xl = operands(u.src)
                        for m in range(len(u.tiles)):
                            ts = [v.tiles[m] for v in us]
                            evacuated(ts, it)
                            for k in range(u.k):
                                if ready:
                                    ready(pe, k, it, us, m)
                                col = (m * u.k + k) * P
                                mm = three_pass(ACC[:, ts[0].pair], k, k + 1,
                                                lambda _: WH[:, slot, col:col + P],
                                                lambda _: WL[:, slot, col:col + P], xh, xl,
                                                k == 0, k == u.k - 1)
                            mm.then_inc(s_tile, 1)
                            if after:
                                after(ts[0])
                run(pe, seg.n, body)

            def stats(name, chunks):
                no, q, n = rnd[name]
                for c in chunks:
                    if c == 0 and no:
                        pe.wait_ge(s_rt, no)
                    pe.wait_ge(s_sq, q + c + 1)
                    for h in range(2):
                        mm = nc.tensor.matmul(OP[:, h], ONES[:], Q[:, (q + c) % 2, h * HALF:(h + 1) * HALF],
                                              start=c == 0, stop=c == n - 1)
                    mm.then_inc(s_st, 1)

            def first_unit(name, skip=()):
                def ready(pe, k, it, us, m):
                    if us[0] is segs_first[name]:
                        if k not in skip:
                            stats(name, [k])
                        pe.wait_ge(s_x, applies[name] + k + 1)
                    hid_ready(pe, k, it, us, m)
                return ready

            def sums(name, kind, lag, n=DC):
                def after(t):
                    if t.kind == kind and lag <= t.idx < n:
                        stats(name, [t.idx - lag])
                return after

            def ring_free(gs, it, eng=pe):
                prev = [pt_groups[g["tr"] - 5] if g["tr"] > 4 else None for g in gs]
                who = {p[0] for p in prev if p}
                assert len(who) <= 1, prev
                if who:
                    need(eng, s_ptA if who == {"A"} else s_ptD, [p[1] if p else 2 for p in prev], it)

            def attention(name):
                n, rows = phases[name]

                def turn_v(it, js):
                    j = js[0]
                    for g, vg in enumerate(j.vgroups):
                        if g == 0:
                            need(pe, s_load, [16 * k.c1["load"] for k in js], it)
                        ring_free([k.vgroups[g] for k in js], it)
                        r = HD if j.kind == "mla" else P
                        for b in range(4):
                            c, t0 = {"d4": 4, "d16": 8}.get(j.kind, 1), token(j.kind, 4 * g + b)
                            tr = nc.tensor.transpose(TR[:, vg["ring"], b * r:(b + 1) * r],
                                                     RV[0:r, t0:t0 + c * (P - 1) + 1:c], IDENT[0:r, 0:r])
                        tr.then_inc(s_tr, 1)

                def logits(it, js, n):
                    j = js[0]
                    slot, kind, t = j.slot, j.kind, j.tasks[n]
                    e, i, b = t["e"], t["i"], t["T"] % 2
                    need(pe, s_ttr, [k.tasks[n]["T"] - 1 for k in js], it)
                    w = j.width(i)
                    if kind_ops(j) and n == 0:
                        need(pe, s_ops, [k.c1["ops"] for k in js], it)
                    if kind != "mla" and i == 0:
                        need(pe, s_head[e], [16 * k.c1["hload"] for k in js], it)
                    c = {"d4": 4, "d16": 8}.get(kind, 1)
                    span = lambda x, b0, m: x[:, token(kind, b0):token(kind, b0) + c * (m - 1) + 1:c]
                    qs = slot if kind == "mla" else e
                    ks = slot if kind in ("mla", "sel", "win") else e
                    q, ql = (span(QK[:, qs, m], i, P) for m in range(2))
                    if kind == "cmp":
                        kh, kl = KCH[:], KCL[:]
                    else:
                        kh, kl = (span(QK[:, ks, 2 + m], t["blocks"][0], w) for m in range(2))
                    passes = [(q, kh), (ql, kh), (q, kl)] if kind == "mla" else [(q, kh), (q, kl)]
                    for c0 in range(0, w, HALF):
                        c1 = min(w, c0 + HALF)
                        masked = kind == "fox" and c1 == w
                        for m, (x, k) in enumerate(passes):
                            mm = nc.tensor.matmul(ACC[:, b, c0:c1], x, k[:, c0:c1], start=m == 0,
                                                  stop=m == len(passes) - 1 and not masked)
                        if masked:
                            mm = nc.tensor.matmul(ACC[:, b, w - P:w], IDR[:], MKR[:], start=False, stop=True)
                    mm.then_inc(s_qk, 1)

                def turn(it, js, n):
                    t = js[0].tasks[n]
                    need(pe, s_exp, [k.tasks[n]["T"] + 1 for k in js], it)
                    for m, g in enumerate(t["groups"]):
                        ring_free([k.tasks[n]["groups"][m] for k in js], it)
                        for x in range(g["g0"], g["g1"]):
                            w = HD if js[0].kind == "cmp" else P
                            y = x - g["g0"]
                            tr = nc.tensor.transpose(TR[0:w, g["ring"], y * P:(y + 1) * P],
                                                     PB[:, t["T"] % 2, x * w:(x + 1) * w], IDENT[:])
                        tr.then_inc(s_tr, 1)

                def values(it, js, n):
                    j = js[0]
                    t = j.tasks[n]
                    e, b = t["e"], t["T"] % 2
                    if n == 0 and j.vgroups:
                        need(pe, s_ptA, [k.vgroups[1]["rel"][1] for k in js], it)
                    need(pe, s_o, [k.tasks[n]["T"] - 1 for k in js], it)
                    for m, g in enumerate(t["groups"]):
                        need(pe, s_ptA if g["eng"] == "A" else s_ptD,
                             [k.tasks[n]["groups"][m]["rel"][1] for k in js], it)
                        pr = (g["pv"] - 1) % 2
                        for x in range(g["g0"], g["g1"]):
                            y = x - g["g0"]
                            if j.kind == "cmp":
                                lhs, rhs = PT[0:HD, pr, 0:P], VC[:]
                            else:
                                lhs = PT[:, pr, y * P:(y + 1) * P]
                                rhs = V[:, j.slot, t["blocks"][x], HD * e:HD * e + HD]
                            mm = nc.tensor.matmul(OP[:, b, 0:HD], lhs, rhs, start=x == 0,
                                                  stop=x == len(t["blocks"]) - 1)
                        mm.then_inc(s_pv, 1)

                def turn_output(it, js):
                    for m, g in enumerate(js[0].ogroups):
                        if m == 0:
                            need(pe, s_o, [k.c1["task"] for k in js], it)
                        ring_free([k.ogroups[m] for k in js], it)
                        src = {"o": OT, "u": OT, "l": OL, "m": OM}[g["what"]]
                        for y in range(4):
                            tr = nc.tensor.transpose(TR[:, g["ring"], y * P:(y + 1) * P], src[:, 4 * g["g"] + y],
                                                     IDENT[:])
                        tr.then_inc(s_tr, 1)

                def body(it):
                    job = lambda p: [row[p] for row in rows]
                    for st in pipeline(rows[0]):
                        if st["start"] is not None:
                            turn_v(it, job(st["start"]))
                        if st["logits"]:
                            logits(it, job(st["logits"][0]), st["logits"][1])
                        if st["values"]:
                            values(it, job(st["values"][0]), st["values"][1])
                        if st["turn"]:
                            turn(it, job(st["turn"][0]), st["turn"][1])
                        if st["end"] is not None:
                            turn_output(it, job(st["end"]))
                run(pe, n, body)

            def hid_ready(pe, k, it, us, m):
                if us[0].src == "hid" and us[0].tiles[0].idx == 0 and m == 0:
                    need(pe, s_hid, [T_SLOTS + u.tiles[0].up - HID_GROUP + k + 1 for u in us], it)

            def layer_end(l):
                weights(f"out{l}", after=sums(f"m{l}", "out", 1))
                stats(f"m{l}", [7])
                weights(f"mlpa{l}", first_unit(f"h{l}"))
                weights(f"mlp{l}", hid_ready)
                weights(f"mlpz{l}", hid_ready, sums(f"n{l}", "down", 1))
                pe.wait_ge(s_p, l + 1)

                def beside_ple(t):
                    if t.idx == 0:
                        stats(f"n{l}", [7])
                    if t.idx >= 5:
                        stats(f"g{l}", [t.idx - 5])
                weights(f"ple{l}", after=beside_ple)
                weights(f"gate{l}", first_unit(f"g{l}", (0, 1, 2)),
                        sums("x1", "gate", 1) if l == 0 else None)

            for s, n in ((s_tr, 2), (s_pv, 2), (s_qk, TASK0)):
                pe.sem_inc(s, n)
            pe.wait_ge(s_ones, 4)
            weights("in0a", first_unit("x"))
            stats("cq", range(2))
            weights("in0p", after=lambda t: stats("ckv", [0]) if t.idx == 0 else None)
            weights("in0b")
            weights("in0c")
            pe.wait_ge(s_x, applies["cq"] + 3)
            weights("up0")
            last = tiles[seg_end["up0"] - 1]
            pe.wait_ge(s_evA, last.act)
            pe.wait_ge(s_evD, last.dve)
            pe.wait_ge(s_rt, 3)
            attention("fox")
            attention("mla")
            pe.wait_ge(s_ttr, TASKS_EVEN["task"])
            pe.wait_ge(s_ptD, COPIES["mla"])
            pe.wait_ge(s_o, TASKS_EVEN["task"])
            layer_end(0)
            if stop == "l0":
                return
            weights("in1p", first_unit("x1", range(7)))
            for name in ("in1a", "in1b", "in1c"):
                weights(name)

            pe.wait_ge(s_cl, 16 * 10)
            for g in range(3):
                t = extras["cmp"][g]
                evacuated([t], 0)
                for h in range(2):
                    c0 = g * S + h * HALF
                    c1 = min(BROW_N, c0 + HALF)
                    mm = nc.tensor.matmul(ACC[0:16, t.pair, h * HALF:h * HALF + c1 - c0], T5[:], ONEHOT[:, c0:c1],
                                          start=True, stop=True)
                mm.then_inc(s_tile, 1)
            t = extras["cmp"][3]
            evacuated([t], 0)
            for i in range(NB):
                tr = nc.tensor.transpose(ACC[:, t.pair, i * 12:(i + 1) * 12], GTT[:, i * P:(i + 1) * P],
                                         IDENT[0:12, 0:12])
            tr.then_inc(s_tile, 1)
            for pos, u in enumerate(segs["cmp"].iters[0]):
                which, slot = pos // 4, u.no % 2
                t = segs["cmp"].iters[0][4 * which + 3].tiles[0]
                if pos % 4 == 0:
                    evacuated([t], 0)
                if pos == 0:
                    pe.wait_ge(s_cmp, 2)
                pe.wait_ge(s_split, u.no + 1)
                for mm4 in range(4):
                    m = 4 * (pos % 4) + mm4
                    for c in range(2):
                        for n3, (w, x) in enumerate(((WH, CBH), (WH, CBL), (WL, CBH))):
                            mm = nc.tensor.matmul(ACC[:, t.pair, c * HALF:c * HALF + HD],
                                                  w[:, slot, mm4 * 256 + c * P:mm4 * 256 + (c + 1) * P],
                                                  x[:, which, m], start=m == 0 and n3 == 0,
                                                  stop=m == 15 and n3 == 2)
                mm.then_inc(s_tile if pos % 4 == 3 else s_cu, 1)
            t = extras["out1"][0]
            evacuated([t], 0)
            pe.wait_ge(s_gl, GELU_STEPS)
            for c in range(2):
                nc.tensor.matmul(ACC[:, t.pair, 0:HD], W2K[:, c], HIDU[:, 0, c], start=c == 0, stop=c == 1)
            for c in range(2):
                mm = nc.tensor.matmul(ACC[0:HD, t.pair, HALF:HALF + HD], HIDU[:, 1, c], W2V[:, c],
                                      start=c == 0, stop=c == 1)
            mm.then_inc(s_tile, 1)
            pe.wait_ge(s_evA, t.act)
            pe.wait_ge(s_evD, t.dve)
            pe.wait_ge(s_rt, rnd["x1"][0] + 1)
            attention("dil")
            attention("nsa")
            pe.wait_ge(s_ttr, TASKS_ODD["task"])
            pe.wait_ge(s_ox, 2)
            pe.wait_ge(s_ptD, COPIES["nsa"])
            pe.wait_ge(s_o, TASKS_ODD["task"])
            layer_end(1)

        @block.scalar
        def _(act):
            def square(name, c, src):
                q = rnd[name][1] + c
                if q > 1:
                    act.wait_ge(s_st, q - 1)
                nc.scalar.activation(Q[:, q % 2], src, ACT.Square).then_inc(s_sq, 1)

            def root(name, dst):
                _, q, n = rnd[name]
                act.wait_ge(s_st, q + n)
                nc.scalar.activation(dst[:], OP[:].rearrange("p h s -> p (h s)"), ACT.Sqrt, bias=CONST[:, 0:1],
                                     scale=1.0 / (n * P)).then_inc(s_rt, 1)

            def high(name, c, dst):
                nc.scalar.activation(dst[:, c], H[:, c], ACT.Copy, scale=GAINS[:, GAIN[name], c:c + 1])\
                    .then_inc(s_xh, 1)

            def tile_loop(name, fn):
                seg = segs[name]

                def body(it):
                    for pos in range(len(seg.iters[0])):
                        us = [row[pos] for row in seg.iters]
                        for m in range(len(us[0].tiles)):
                            fn([u.tiles[m] for u in us], it)
                run(act, seg.n, body)

            def wide(t):
                return ACC[:, t.pair]

            def store(ts, it):
                t = ts[0]
                step = ts[1].idx - ts[0].idx if len(ts) > 1 else 0
                own = t.kind in ("uq", "ukv")
                if own:
                    need(act, s_tile, [x.no + 1 for x in ts], it)
                    need(act, s_store[t.pair], [16 * x.slot_before[t.pair] for x in ts], it)
                    rows = HD if t.kind == "uq" else P
                    nc.scalar.activation(Q[0:rows, t.pair], ACC[0:rows, t.pair], ACT.Copy).then_inc(s_evA, 1)
                    need(act, s_evA, [x.act for x in ts], it)
                    if t.kind == "uq":
                        act.wait_ge(s_rope, ROPE_KEY_STEPS + 2 * t.idx + 2)
                else:
                    need(act, s_evD, [x.dve for x in ts], it)
                if t.kind in SPLIT:
                    nc.scalar.activation(QR[:, t.pair], TL[:, t.pair].bitcast(F32), ACT.Copy).then_inc(s_hi, 1)
                    need(act, s_lo, [x.split for x in ts], it)
                    y = y_foxs if t.kind == "foxs" else y_odds
                    act.dma_start(y[bass.ds(at(t.idx, step, it), 1)].rearrange("o h p s -> p (o h) s"),
                                  HALVES[:, :, t.pair].bitcast(F32)).then_inc(s_store[t.pair], 16)
                    return
                dst = {"fox": y_fox, "odd": y_odd, "uq": y_q, "ukv": y_kv}[t.kind]
                rows = 96 if t.kind == "uq" else P
                src = Q[0:rows, t.pair] if own else QR[:, t.pair].bitcast(F32)
                act.dma_start(dst[bass.ds(at(t.idx, step, it), 1), 0:rows].rearrange("o p s -> (o p) s"),
                              src).then_inc(s_store[t.pair], 16)

            def mlp(ts, it):
                t = ts[0]
                if t.kind != "up":
                    return
                x = T[:, (t.up - 1) % 2]
                need(act, s_evD, [y.dve for y in ts], it)
                nc.scalar.activation(HH[:, t.idx], x, ACT.Square).then_inc(s_hhi, 1)
                need(act, s_hhi, [y.up for y in ts], it)
                nc.scalar.activation(x, x, ACT.Square).then_inc(s_sqh, 1)

            def attention(name):
                n, rows = phases[name]

                def copy_v(it, js):
                    j = js[0]
                    for g, vg in enumerate(j.vgroups):
                        need(act, s_tr, [k.vgroups[g]["tr"] for k in js], it)
                        if g == 0:
                            need(act, s_pv, [k.prev.pv_end if k.prev else 2 for k in js], it)
                        r = HD if j.kind == "mla" else P
                        nc.scalar.activation(V[:, j.slot, 4 * g:4 * g + 4, 0:r],
                                             TR[:, vg["ring"], 0:4 * r].rearrange("p (b f) -> p b f", b=4),
                                             ACT.Copy).then_inc(s_ptA, 1)

                def copies(it, js, n):
                    for m, g in enumerate(js[0].tasks[n]["groups"]):
                        if g["eng"] != "A":
                            continue
                        gs = [k.tasks[n]["groups"][m] for k in js]
                        need(act, s_tr, [x["tr"] for x in gs], it)
                        need(act, s_pv, [x["pv"] - 2 for x in gs], it)
                        w = (g["g1"] - g["g0"]) * P
                        nc.scalar.activation(PT[:, (g["pv"] - 1) % 2, 0:w], TR[:, g["ring"], 0:w],
                                             ACT.Copy).then_inc(s_ptA, 1)

                def probabilities(it, js, n):
                    t = js[0].tasks[n]
                    need(act, s_ttr, [k.tasks[n]["T"] + 1 for k in js], it)
                    x = PB[:, t["T"] % 2, 0:js[0].width(t["i"])]
                    nc.scalar.activation(x, x, ACT.Exp, bias=NM[:, n:n + 1], scale=-1.0,
                                         accum_out=L[:, n:n + 1]).then_inc(s_exp, 1)

                def outputs(it, js, pos):
                    for m, g in enumerate(js[0].ogroups):
                        if g["what"] != "o":
                            continue
                        need(act, s_tr, [k.ogroups[m]["tr"] for k in js], it)
                        nc.scalar.activation(chunk_of(XH, name, pos, it)[:, g["g"] * HALF:(g["g"] + 1) * HALF],
                                             TR[:, g["ring"]], ACT.Copy).then_inc(s_oh, 1)
                    if js[0].kind == "d16":
                        need(act, s_md, [MERGE_STEPS * k + 5 for k in range(len(rows))], it)
                        nc.scalar.activation(DM[:], DM[:], ACT.Exp, scale=-1.0).then_inc(s_mg, 1)

                def body(it):
                    job = lambda p: [row[p] for row in rows]
                    for st in pipeline(rows[0]):
                        if st["start"] is not None:
                            copy_v(it, job(st["start"]))
                        if st["turn"]:
                            copies(it, job(st["turn"][0]), st["turn"][1])
                        if st["logits"]:
                            probabilities(it, job(st["logits"][0]), st["logits"][1])
                        if st["end"] is not None:
                            outputs(it, job(st["end"]), st["end"])
                run(act, n, body)

            for s, n in ((s_exp, TASK0), (s_ptA, 2), (s_oh, 2)):
                act.sem_inc(s, n)
            for s in s_store:
                act.sem_inc(s, 16)
            act.wait_ge(s_const, 16 * N_CONST)
            for c in range(DC):
                act.wait_ge(s_h[c // 2], 16)
                square("x", c, H[:, c])
                high("x", c, XH)
            root("x", R)
            for c in range(3):
                act.wait_ge(s_evD, segs["in0a"].iters[0][c].tiles[0].dve)
                square("cq" if c < 2 else "ckv", c % 2, CQ[:, c])
                if c == 1:
                    act.wait_ge(s_dve, DVE_ANGLE)
                    root("cq", RC)
            for c in range(3):
                if c == 2:
                    act.wait_ge(s_cqn, 2)
                    root("ckv", RC)
                act.wait_ge(s_cqn, c + 1)
                nc.scalar.activation(CQH[:, c], CQ[:, c], ACT.Copy, scale=QKVG[:, c:c + 1]).then_inc(s_xh, 1)
            tile_loop("in0p", store)
            act.wait_ge(s_dve, DVE_ANGLE)
            nc.scalar.activation(CS[:], ANG[:, 0], ACT.Sin).then_inc(s_ft, 1)
            act.wait_ge(s_dve, DVE_FZ)
            nc.scalar.activation(KT[64:72], ANG[64:72, 1], ACT.Abs).then_inc(s_ft, 1)
            act.wait_ge(s_ft, 2)
            nc.scalar.activation(KT[64:72], KT[64:72], ACT.Exp, scale=-1.0).then_inc(s_ft, 1)
            act.wait_ge(s_ft, 3)
            nc.scalar.activation(KT[64:72], KT[64:72], ACT.Ln, bias=1.0).then_inc(s_ft, 1)
            act.wait_ge(s_rope, ROPE_KEY_STEPS)
            act.dma_start(y_kr, KR[0:32]).then_inc(s_misc, 16)
            act.wait_ge(s_dve, DVE_ALL)
            act.dma_start(y_f, ANG[64:72, 0]).then_inc(s_misc, 16)
            tile_loop("in0b", store)
            tile_loop("in0c", store)
            tile_loop("up0", store)
            attention("fox")
            attention("mla")

            def layer_end(l):
                for u in segs[f"out{l}"].iters[0]:
                    for t in u.tiles:
                        act.wait_ge(s_tile, t.no + 1)
                        nc.scalar.activation(M[:, t.idx], wide(t), ACT.Copy).then_inc(s_evA, 1)
                        act.wait_ge(s_evA, t.act)
                        square(f"m{l}", t.idx, M[:, t.idx])
                root(f"m{l}", R)
                for c in range(DC):
                    act.wait_ge(s_res, resids[f"m{l}"] + c + 1)
                    square(f"h{l}", c, H[:, c])
                    high(f"h{l}", c, XH)
                root(f"h{l}", R)
                for name in ("mlpa", "mlp", "mlpz"):
                    tile_loop(f"{name}{l}", mlp)
                downs = [t for u in segs[f"mlpz{l}"].iters[0] for t in u.tiles if t.kind == "down"]
                for c, t in enumerate(downs):
                    act.wait_ge(s_evD, t.dve)
                    square(f"n{l}", c, M[:, c])
                    if c == 3:
                        act.wait_ge(s_pload, 16 * (l + 1))
                        nc.scalar.activation(XH[:, 6:8], PRAW[:], ACT.Copy).then_inc(s_phi, 1)

                def projected(t):
                    act.wait_ge(s_tile, t.no + 1)
                    nc.scalar.activation(PP[:, t.idx], wide(t), ACT.Copy).then_inc(s_evA, 1)

                def stream(c):
                    act.wait_ge(s_res, resids[f"n{l}"] + c + 1)
                    square(f"g{l}", c, H[:, c])
                    if c == 4:
                        act.wait_ge(s_p, l + 1)
                    if c == 6:
                        act.wait_ge(s_tile, seg_end[f"ple{l}"])
                    high(f"g{l}", c, XH)

                for t in (t for u in segs[f"ple{l}"].iters[0] for t in u.tiles):
                    projected(t)
                    if t.idx == 0:
                        root(f"n{l}", R)
                    if t.idx >= 4:
                        stream(t.idx - 4)
                for c in range(4, DC):
                    stream(c)
                root(f"g{l}", R)
                for t in (u.tiles[0] for u in segs[f"gate{l}"].iters[0]):
                    x = T[:, (t.gate - 1) % 2]
                    act.wait_ge(s_evD, t.dve)
                    nc.scalar.activation(x, x, ACT.Sigmoid).then_inc(s_sig, 1)
                    if l == 0:
                        act.wait_ge(s_res, resids["ga0"] + t.idx + 1)
                        square("x1", t.idx, H[:, t.idx])
                        high("x1", t.idx, X1H)

            layer_end(0)
            if stop == "l0":
                return
            root("x1", R)
            for name in ("in1p", "in1a", "in1b", "in1c"):
                tile_loop(name, store)
            for g in range(3):
                t = extras["cmp"][g]
                c1 = min(BROW_N, (g + 1) * S)
                act.wait_ge(s_tile, t.no + 1)
                nc.scalar.activation(BRS[:, g * S:c1], ACC[0:16, t.pair, 0:c1 - g * S], ACT.Copy).then_inc(s_evA, 1)
            t = extras["cmp"][3]
            act.wait_ge(s_tile, t.no + 1)
            nc.scalar.activation(GT[:], ACC[:, t.pair, 0:NB * 12].rearrange("p (b g) -> p b g", g=12),
                                 ACT.Sigmoid).then_inc(s_evA, 1)
            for which in range(2):
                t = segs["cmp"].iters[0][4 * which + 3].tiles[0]
                act.wait_ge(s_tile, t.no + 1)
                nc.scalar.activation(HIDF[:, which], ACC[:, t.pair].rearrange("p (c s) -> p c s", c=2)[:, :, 0:HD],
                                     ACT.Copy).then_inc(s_evA, 1)
            act.wait_ge(s_gl, 3)
            nc.scalar.activation(HIDT[:], HIDT[:], ACT.Exp, scale=-2.0 * math.sqrt(2.0 / math.pi)).then_inc(s_ge, 1)
            t = extras["out1"][0]
            act.wait_ge(s_tile, t.no + 1)
            nc.scalar.activation(VC[:], ACC[0:HD, t.pair, HALF:HALF + HD], ACT.Copy)
            nc.scalar.activation(KCH[:], ACC[:, t.pair, 0:HD], ACT.Copy).then_inc(s_evA, 1)
            attention("dil")
            attention("nsa")
            layer_end(1)

        @block.vector
        def _(dve):
            V_ = nc.vector
            steps = [0]

            def link(ins):
                steps[0] += 1
                ins.then_inc(s_dve, 1)
                dve.wait_ge(s_dve, steps[0])

            def inverse_rms(name, r):
                no = rnd[name][0]
                dve.wait_ge(s_rt, no + 1)
                V_.reciprocal(r[:], r[:]).then_inc(s_R, 1)
                dve.wait_ge(s_R, no + 1)

            def low(x, src, gain, hi, lo):
                dve.wait_ge(s_xh, x + 1)
                V_.scalar_tensor_tensor(out=lo, in0=src, scalar=gain, in1=hi.bitcast(F32), op0=ALU.mult,
                                        op1=ALU.subtract).then_inc(s_x, 1)

            def low_h(name, c, hi=XH, lo=XL):
                low(applies[name] + c, H[:, c], GAINS[:, GAIN[name], c:c + 1], hi[:, c], lo[:, c])

            def residual(name, then):
                inverse_rms(name, R)
                for c in range(8):
                    t0 = tcount[name] + c
                    if c > 1:
                        dve.wait_ge(s_res, resids[name] + c - 1)
                    V_.scalar_tensor_tensor(out=T[:, t0 % 2], in0=M[:, c], scalar=GAINS[:, GAIN[name], c:c + 1],
                                            in1=R[:], op0=ALU.mult, op1=ALU.mult).then_inc(s_T, 1)
                    dve.wait_ge(s_T, t0 + 1)
                    V_.tensor_tensor(H[:, c], H[:, c], T[:, t0 % 2], ALU.add).then_inc(s_res, 1)
                    if c:
                        low_h(then, c - 1)
                low_h(then, 7)

            def tile_loop(name, fn):
                seg = segs[name]

                def body(it):
                    for pos in range(len(seg.iters[0])):
                        us = [row[pos] for row in seg.iters]
                        for m in range(len(us[0].tiles)):
                            fn([u.tiles[m] for u in us], it)
                run(dve, seg.n, body)

            def mlp(ts, it):
                t = ts[0]
                need(dve, s_tile, [y.no + 1 for y in ts], it)
                if t.kind == "up":
                    x = T[:, (t.up - 1) % 2]
                    need(dve, s_hid, [T_SLOTS + y.up - 2 for y in ts], it)
                    V_.scalar_tensor_tensor(out=x, in0=ACC[:, t.pair], scalar=0.0, in1=R[:], op0=ALU.max,
                                            op1=ALU.mult).then_inc(s_evD, 1)
                    need(dve, s_sqh, [y.up for y in ts], it)
                    V_.tensor_tensor(HL[:, t.idx], x, HH[:, t.idx].bitcast(F32), ALU.subtract).then_inc(s_hid, 1)
                else:
                    need(dve, s_evD, [y.dve - DC - HID_GROUP for y in ts], it)
                    V_.tensor_tensor(M[:, t.idx], M[:, t.idx], ACC[:, t.pair], ALU.add).then_inc(s_evD, 1)

            def project(ts, it):
                t = ts[0]
                need(dve, s_tile, [x.no + 1 for x in ts], it)
                if t.kind in ("cq", "misc"):
                    dst = CQ[:, t.idx] if t.kind == "cq" else MISC1[:, 0]
                    V_.tensor_tensor(dst, ACC[:, t.pair], R[:], ALU.mult).then_inc(s_evD, 1)
                    return
                need(dve, s_store[t.pair], [16 * x.slot_before[t.pair] for x in ts], it)
                dst = (TL if t.kind in SPLIT else QR)[:, t.pair].bitcast(F32)
                V_.tensor_tensor(dst, ACC[:, t.pair], R[:], ALU.mult).then_inc(s_evD, 1)

            def low_half(ts, it):
                t = ts[0]
                need(dve, s_hi, [x.split for x in ts], it)
                V_.tensor_tensor(TL[:, t.pair], TL[:, t.pair].bitcast(F32), QR[:, t.pair].bitcast(F32),
                                 ALU.subtract).then_inc(s_lo, 1)

            def projection(ts, it):
                project(ts, it)
                if ts[0].kind in SPLIT:
                    low_half(ts, it)

            def rotate(ts, it):
                t = ts[0]
                if t.kind != "uq":
                    return
                dve.wait_ge(s_tile, t.no + 1)
                dve.wait_ge(s_store[t.pair], 16 * t.slot_before[t.pair])
                dve.wait_ge(s_rope, ROPE_KEY_STEPS + 2 * t.idx)
                V_.tensor_tensor(KT[64:96], ACC[96:128, t.pair], CS[96:128], ALU.mult).then_inc(s_rope, 1)
                V_.tensor_tensor(Q[64:96, t.pair], ACC[64:96, t.pair], CS[64:96], ALU.mult).then_inc(s_evD, 1)
                dve.wait_ge(s_rope, ROPE_KEY_STEPS + 2 * t.idx + 1)
                dve.wait_ge(s_evD, t.dve)
                V_.tensor_tensor(Q[64:96, t.pair], Q[64:96, t.pair], KT[64:96], ALU.add).then_inc(s_rope, 1)

            def attention(name):
                n_it, rows = phases[name]

                def bias(j, t):
                    slot, kind = j.slot, j.kind
                    e, i, w = t["e"], t["i"], j.width(t["i"])
                    if kind == "fox":
                        return BIAS[:, slot, e * S:e * S + w]
                    if kind == "mla":
                        return BIAS[:, 0, S - P - i * P:S]
                    if kind == "sel":
                        return BIAS[:, slot, e * S + S - P - i * P:(e + 1) * S]
                    if kind == "win":
                        return BIAS[:, slot, (e + 1) * WIN_W - w:(e + 1) * WIN_W]
                    if kind == "cmp":
                        return CMPMASK[:, i * HD:(i + 1) * HD]
                    wt = D16_W if kind == "d16" else DIL_W
                    return BIASD[:, slot, e, wt - w:wt]

                def copies(it, js, n):
                    for m, g in enumerate(js[0].tasks[n]["groups"]):
                        if g["eng"] != "D":
                            continue
                        gs = [k.tasks[n]["groups"][m] for k in js]
                        need(dve, s_tr, [x["tr"] for x in gs], it)
                        need(dve, s_pv, [x["pv"] - 2 for x in gs], it)
                        w, r = (g["g1"] - g["g0"]) * P, HD if js[0].kind == "cmp" else P
                        V_.tensor_copy(PT[0:r, (g["pv"] - 1) % 2, 0:w], TR[0:r, g["ring"], 0:w]).then_inc(s_ptD, 1)

                def scores(it, js, n):
                    j, t = js[0], js[0].tasks[n]
                    w, b = j.width(t["i"]), t["T"] % 2
                    need(dve, s_qk, [k.tasks[n]["T"] + 1 for k in js], it)
                    if n == 0 and j.kind != "cmp":
                        need(dve, s_load, [16 * k.c1["load"] for k in js], it)
                    need(dve, s_tr, [k.tasks[n]["tr_before"] for k in js], it)
                    V_.tensor_tensor_reduce(PB[:, b, 0:w], ACC[:, b, 0:w], bias(j, t),
                                            -MLA_SCALE if j.kind == "mla" else -1.0 / ISCALE, 3e38,
                                            ALU.add, ALU.min, NM[:, n:n + 1]).then_inc(s_ttr, 1)

                def output(it, js, n, pos):
                    kind, t = js[0].kind, js[0].tasks[n]
                    e, i, b = t["e"], t["i"], t["T"] % 2
                    need(dve, s_pv, [k.tasks[n]["groups"][-1]["pv"] for k in js], it)
                    if n == 0:
                        need(dve, s_tr, [k.ot_before for k in js], it)
                    f = HD * (pos if kind == "mla" else e)
                    dst = OT[:, i, f:f + HD]
                    if kind in DILATED:
                        V_.tensor_copy(OL[:, i, f:f + HD], L[:, n:n + 1].to_broadcast([P, HD]))
                        V_.tensor_copy(OM[:, i, f:f + HD], NM[:, n:n + 1].to_broadcast([P, HD]))
                        V_.tensor_copy(dst, OP[:, b, 0:HD]).then_inc(s_o, 1)
                        return
                    V_.reciprocal(RL[:, n:n + 1], L[:, n:n + 1]).then_inc(s_rl, 1)
                    need(dve, s_rl, [k.c0["rl"] + n + 1 for k in js], it)
                    if kind not in NSA:
                        V_.tensor_scalar(dst, OP[:, b, 0:HD], RL[:, n:n + 1], None, ALU.mult).then_inc(s_o, 1)
                        return
                    col = at(e * 3 + NSA.index(kind), 6, it)
                    V_.tensor_tensor(CF[:, n:n + 1], RL[:, n:n + 1], GT[:, i, bass.ds(col, 1)], ALU.mult)\
                        .then_inc(s_cf, 1)
                    need(dve, s_cf, [k.c0["cf"] + n + 1 for k in js], it)
                    if kind == "cmp":
                        V_.tensor_scalar(dst, OP[:, b, 0:HD], CF[:, n:n + 1], None, ALU.mult).then_inc(s_o, 1)
                    else:
                        need(dve, s_o, [k.tasks[n]["T"] - 15 for k in js], it)
                        V_.scalar_tensor_tensor(out=dst, in0=OP[:, b, 0:HD], scalar=CF[:, n:n + 1], in1=dst,
                                                op0=ALU.mult, op1=ALU.add).then_inc(s_o, 1)

                def outputs(it, js, pos):
                    kind = js[0].kind
                    for m, g in enumerate(js[0].ogroups):
                        need(dve, s_tr, [k.ogroups[m]["tr"] for k in js], it)
                        cols = slice(g["g"] * HALF, (g["g"] + 1) * HALF)
                        if g["what"] == "o":
                            need(dve, s_oh, [k.c0["oh"] + m + 1 for k in js], it)
                            V_.tensor_tensor(chunk_of(XL, name, pos, it)[:, cols], TR[:, g["ring"]],
                                             chunk_of(XH, name, pos, it)[:, cols].bitcast(F32),
                                             ALU.subtract).then_inc(s_ptD, 1)
                            continue
                        dst = {"u": DU, "l": DL, "m": DM}[g["what"]]
                        c = {"d1": 1, "d4": 4, "d16": 8}[kind]
                        d = dst[:, DILATED.index(kind)]
                        src = TR[:, g["ring"]]
                        if c == 1:
                            d = d[:, cols]
                        else:
                            d = d.rearrange("p (a c) -> p c a", c=c)[:, g["g"] * c // 2:(g["g"] + 1) * c // 2, :]
                            src = src.rearrange("p (c a) -> p c a", c=c // 2)
                        V_.tensor_copy(d, src).then_inc(s_ptD, 1)
                    if kind == "d16":
                        merge([k.ogroups[-1]["rel"][1] for k in js], it)

                def body(it):
                    job = lambda p: [row[p] for row in rows]
                    for st in pipeline(rows[0]):
                        if st["turn"]:
                            copies(it, job(st["turn"][0]), st["turn"][1])
                        if st["logits"]:
                            scores(it, job(st["logits"][0]), st["logits"][1])
                        if st["end"] is not None:
                            outputs(it, job(st["end"]), st["end"])
                        if st["values"]:
                            output(it, job(st["values"][0]), st["values"][1], st["values"][0])

                def merge(evacuated, it):
                    m = [0]

                    def step(ins):
                        m[0] += 1
                        ins.then_inc(s_md, 1)

                    def done():
                        need(dve, s_md, [MERGE_STEPS * k + m[0] for k in range(n_it)], it)

                    mm = OM[:].rearrange("p b f -> p (b f)")
                    need(dve, s_ptD, evacuated, it)
                    step(V_.tensor_tensor(mm, DM[:, 0], DM[:, 1], ALU.min))
                    done()
                    step(V_.tensor_tensor(mm, mm, DM[:, 2], ALU.min))
                    done()
                    for g in range(3):
                        step(V_.tensor_tensor(DM[:, g], DM[:, g], mm, ALU.subtract))
                    need(dve, s_mg, [k + 1 for k in range(n_it)], it)
                    step(V_.tensor_tensor(DU[:], DU[:], DM[:], ALU.mult))
                    step(V_.tensor_tensor(DL[:], DL[:], DM[:], ALU.mult))
                    done()
                    for g in (1, 2):
                        step(V_.tensor_tensor(DU[:, 0], DU[:, 0], DU[:, g], ALU.add))
                        step(V_.tensor_tensor(DL[:, 0], DL[:, 0], DL[:, g], ALU.add))
                        done()
                    step(V_.reciprocal(DL[:, 0], DL[:, 0]))
                    done()
                    step(V_.tensor_tensor(DU[:, 0], DU[:, 0], DL[:, 0], ALU.mult))
                    done()
                    xh, xl = chunk_of(XH, "dil", 0, it), chunk_of(XL, "dil", 0, it)
                    step(V_.tensor_copy(xh, DU[:, 0]))
                    done()
                    assert m[0] == MERGE_STEPS
                    V_.tensor_tensor(xl, DU[:, 0], xh.bitcast(F32), ALU.subtract).then_inc(s_ox, 1)

                run(dve, n_it, body)

            two_pi = 2 * math.pi
            c1 = 6.28125
            c2 = float(np.float32(np.round((two_pi - c1) * 2 ** 20) / 2 ** 20))
            c3 = float(np.float32(two_pi - c1 - c2))
            magic = float(3 << 22)
            for s, n in ((s_evD, 2), (s_ttr, TASK0), (s_o, TASK0), (s_ptD, 2), (s_rl, 2), (s_cf, 2)):
                dve.sem_inc(s, n)
            dve.wait_ge(s_const, 16 * N_CONST)
            V_.memset(RL[:, 0:1], 0.0).then_inc(s_hid, T_SLOTS)
            for c in range(DC):
                low_h("x", c)
            inverse_rms("x", R)
            low_rank = [[u.tiles[0]] for u in segs["in0a"].iters[0]]
            project(low_rank[0], 0)
            link(V_.tensor_copy(ANG[:, 0], POS[:]))
            link(V_.tensor_scalar(ANG[:, 1], ANG[:, 0], CONST[:, 1:2], None, ALU.mult))
            link(V_.tensor_scalar(ANG[:, 2], ANG[:, 1], 1.0 / two_pi, CONST[:, 2:3], ALU.mult, ALU.add))
            link(V_.tensor_scalar(ANG[:, 2], ANG[:, 2], magic, None, ALU.add))
            link(V_.tensor_scalar(ANG[:, 2], ANG[:, 2], -magic, None, ALU.add))
            link(V_.scalar_tensor_tensor(out=ANG[:, 0], in0=ANG[:, 2], scalar=-c1, in1=ANG[:, 1], op0=ALU.mult, op1=ALU.add))
            link(V_.scalar_tensor_tensor(out=ANG[:, 1], in0=ANG[:, 2], scalar=-c2, in1=ANG[:, 0], op0=ALU.mult, op1=ALU.add))
            link(V_.scalar_tensor_tensor(out=ANG[:, 0], in0=ANG[:, 2], scalar=-c3, in1=ANG[:, 1], op0=ALU.mult, op1=ALU.add))
            link(V_.tensor_scalar(ANG[:, 0], ANG[:, 0], CONST[:, 3:4], None, ALU.add))
            link(V_.tensor_scalar(ANG[:, 0], ANG[:, 0], 3.1415925, -3.1415925, ALU.min, ALU.max))
            assert steps[0] == DVE_ANGLE
            for t in low_rank[1:]:
                project(t, 0)

            def norm_cq(c):
                V_.tensor_tensor(CQ[:, c], CQ[:, c], RC[:], ALU.mult).then_inc(s_cqn, 1)

            def low_cq(c):
                low(applies["cq"] + c, CQ[:, c], QKVG[:, c:c + 1], CQH[:, c], CQL[:, c])

            inverse_rms("cq", RC)
            norm_cq(0)
            norm_cq(1)
            low_cq(0)
            low_cq(1)
            first = [[u.tiles[0]] for u in segs["in0p"].iters[0]]
            project(first[0], 0)
            inverse_rms("ckv", RC)
            norm_cq(2)
            low_cq(2)
            low_half(first[0], 0)
            projection(first[1], 0)
            t = segs["in0a"].iters[0][3].tiles[0]
            dve.wait_ge(s_evD, t.dve)
            f0, f1, f2 = ANG[64:72, 0], ANG[64:72, 1], KT[64:72]
            link(V_.tensor_scalar(f1, MISC[64:72], CONST[64:72, 5:6], None, ALU.add))
            assert steps[0] == DVE_FZ
            dve.wait_ge(s_ft, 1)
            link(V_.tensor_scalar(CS[:], CS[:], CONST[:, 4:5], None, ALU.mult))
            link(V_.tensor_scalar(f0, f1, 0.0, None, ALU.min))
            dve.wait_ge(s_ft, 4)
            link(V_.tensor_tensor(f0, f0, f2, ALU.subtract))
            link(V_.memset(f1, 1.0))
            link(V_.tensor_tensor_scan(f2, f1, f0, 0.0, ALU.mult, ALU.add))
            link(V_.tensor_scalar(f0, f2, -ISCALE, None, ALU.mult))
            assert steps[0] == DVE_ALL, steps
            dve.wait_ge(s_ones, 4)
            V_.tensor_tensor(KT[0:32], MISC[32:64], CS[32:64], ALU.mult).then_inc(s_rope, 1)
            V_.tensor_tensor(KR[0:32], MISC[0:32], CS[0:32], ALU.mult).then_inc(s_rope, 1)
            dve.wait_ge(s_rope, 2)
            V_.tensor_tensor(KR[0:32], KR[0:32], KT[0:32], ALU.add).then_inc(s_rope, 1)
            tile_loop("in0b", projection)
            tile_loop("in0c", projection)
            tile_loop("up0", rotate)
            attention("fox")
            attention("mla")

            def layer_end(l):
                residual(f"m{l}", f"h{l}")
                link(V_.memset(M[:], 0.0))
                inverse_rms(f"h{l}", R)
                for name in ("mlpa", "mlp"):
                    tile_loop(f"{name}{l}", mlp)
                for t in (t for u in segs[f"mlpz{l}"].iters[0] for t in u.tiles):
                    mlp([t], 0)
                    if t.kind == "down" and t.idx == 4:
                        dve.wait_ge(s_phi, l + 1)
                        V_.tensor_tensor(XL[:, 6:8], PRAW[:], XH[:, 6:8].bitcast(F32), ALU.subtract).then_inc(s_p, 1)
                dve.wait_ge(s_hid, T_SLOTS + t.up)
                residual(f"n{l}", f"g{l}")
                inverse_rms(f"g{l}", R)
                for t in (u.tiles[0] for u in segs[f"gate{l}"].iters[0]):
                    x = T[:, (t.gate - 1) % 2]
                    dve.wait_ge(s_tile, t.no + 1)
                    dve.wait_ge(s_res, resids[f"ga{l}"] + max(t.idx - 1, 0))
                    V_.tensor_tensor(x, ACC[:, t.pair], R[:], ALU.mult).then_inc(s_evD, 1)
                    dve.wait_ge(s_sig, t.gate)
                    V_.tensor_tensor(x, x, PP[:, t.idx], ALU.mult).then_inc(s_gm, 1)
                    dve.wait_ge(s_gm, t.gate)
                    V_.tensor_tensor(H[:, t.idx], H[:, t.idx], x, ALU.add).then_inc(s_res, 1)
                    if l == 0:
                        low_h("x1", t.idx, X1H, X1L)

            layer_end(0)
            if stop == "l0":
                return
            inverse_rms("x1", R)
            for name in ("in1p", "in1a", "in1b", "in1c"):
                tile_loop(name, projection)
            dve.wait_ge(s_cl, 16 * 10)
            dve.wait_ge(s_cz, 2)
            for which in range(2):
                for m in range(16):
                    last = V_.tensor_scalar(CBF[:, which, m], CMPX[:, which, 2 * m:2 * m + 16 * 63 + 1:16],
                                            POSC[:, m, which:which + 1], None, ALU.add)
            last.then_inc(s_cb, 1)
            dve.wait_ge(s_cb, 1)
            V_.tensor_copy(CBH[:], CBF[:]).then_inc(s_cmp, 1)
            dve.wait_ge(s_cmp, 1)
            V_.tensor_tensor(CBL[:], CBF[:], CBH[:].bitcast(F32), ALU.subtract).then_inc(s_cmp, 1)
            t = extras["cmp"][3]
            dve.wait_ge(s_evA, t.act)
            g = GT[:, 0].rearrange("p (h b) -> p h b", b=3)[:, :, 0]
            V_.tensor_scalar(g, g, CONST[:, 6:7], None, ALU.mult).then_inc(s_cmp, 1)
            t = segs["cmp"].iters[0][7].tiles[0]
            dve.wait_ge(s_evA, t.act)
            n = [0]

            def gelu(ins):
                n[0] += 1
                ins.then_inc(s_gl, 1)
                dve.wait_ge(s_gl, n[0])

            gelu(V_.tensor_tensor(HIDT[:], HIDF[:], HIDF[:], ALU.mult))
            gelu(V_.tensor_scalar(HIDT[:], HIDT[:], 0.044715, 1.0, ALU.mult, ALU.add))
            gelu(V_.tensor_tensor(HIDT[:], HIDT[:], HIDF[:], ALU.mult))
            dve.wait_ge(s_ge, 1)
            gelu(V_.tensor_scalar(HIDT[:], HIDT[:], 1.0, None, ALU.add))
            gelu(V_.reciprocal(HIDT[:], HIDT[:]))
            gelu(V_.tensor_tensor(HIDU[:], HIDF[:], HIDT[:], ALU.mult))
            assert n[0] == GELU_STEPS
            t = extras["out1"][0]
            dve.wait_ge(s_evA, t.act)
            V_.tensor_tensor(KCL[:], ACC[:, t.pair, 0:HD], KCH[:].bitcast(F32), ALU.subtract).then_inc(s_evD, 1)
            attention("dil")
            attention("nsa")
            layer_end(1)


def t5_bucket(dist):
    n = np.maximum(dist, 0)
    ratio = np.log(np.maximum(n, 1).astype(np.float32) / np.float32(16)) / np.float32(math.log(2048 / 16))
    large = np.minimum(16 + (ratio * np.float32(16)).astype(np.int32), 31)
    return np.where(n < 16, n, large)


def onehot_rows():
    oh = np.zeros((33, BROW_N), np.float32)

    def fill(kind, width, top, ok, step=1):
        x = np.arange(width)
        d = top - x
        good = ok(d)
        b = np.where(good, t5_bucket(d * step), 32)
        oh[b, BROW[kind] + x] = ISCALE

    fill("sel", 1152, S - 1, lambda d: d >= 0)
    fill("win", 768, WIN_W - 1, lambda d: (d >= 0) & (d < 512))
    fill("d1", 384, DIL_W - 1, lambda d: (d >= 0) & (d <= 128))
    fill("d4", 384, DIL_W - 1, lambda d: (d >= 0) & (d <= 128), 4)
    fill("d16", 256, D16_W - 1, lambda d: (d >= 0) & (d % 2 == 0), 8)
    return oh


def constants():
    c = {"ident": np.eye(P, dtype=np.float32), "onehot": onehot_rows()}
    q, k = np.arange(P)[:, None], np.arange(P)[None]
    c["mask"] = np.where(k > q, np.float32(NEG * ISCALE), np.float32(0))
    u = np.arange(S)[None]
    c["mlamask"] = np.where(u - (S - P) > q, np.float32(NEG), np.float32(0))
    t = np.arange(S).reshape(NB, P).T[:, :, None]
    n = np.arange(HD)[None, None]
    ok = (16 * n + 31 <= t) & (n < N_CMP)
    c["cmpmask"] = np.where(ok, np.float32(0), np.float32(NEG * ISCALE)).reshape(P, NB * HD).copy()
    k = np.zeros((P, 8), np.float32)
    inv = (10000.0 ** (-np.arange(0, 32, 2, dtype=np.float32) / np.float32(32))).astype(np.float32)
    row = np.arange(P)
    k[:, 0] = EPS
    k[:, 1] = inv[row % 16]
    cos = (row // 32) % 2 == 0
    k[:, 2] = np.where(cos, 0.25, 0.0)
    k[:, 3] = np.where(cos, math.pi / 2, 0.0)
    k[:, 4] = np.where(cos, 1.0, np.where(row % 32 < 16, -1.0, 1.0))
    k[:, 6] = (row >= 31).astype(np.float32)
    c["const"] = k
    return c


def weight_stream(a):
    f = lambda w: np.asarray(w)[0]
    out = []

    def full(w, cols):
        x = np.zeros((D, P), np.float32)
        cols = np.asarray(cols)
        x[:, cols >= 0] = w[:, cols[cols >= 0]]
        out.append(x.reshape(DC, P, P).transpose(1, 0, 2).reshape(P, D))

    def span(w, kc, c0, tiles):
        x = w[:, c0:c0 + tiles * P].reshape(kc, P, tiles, P)
        out.append(x.transpose(1, 2, 0, 3).reshape(P, D))

    r = lambda c0, n=P: list(range(c0, c0 + n))
    w = f(a["ev_w_in"])
    for c in range(3):
        full(w, r(c * P))
    kr = 384
    full(w, r(kr, 32) + r(kr + 16, 16) + r(kr, 16) + r(kr + 32 + 3 * 512, 8) + [-1] * 56)
    for c in range(12):
        full(w, r(kr + 32 + c * P))
    uq = f(a["ev_w_uq"]).reshape(256, 8, 96)
    uq = np.concatenate([uq, uq[:, :, 80:96], uq[:, :, 64:80]], axis=2).reshape(256, 1024)
    span(uq, 2, 0, 4)
    span(uq, 2, 512, 4)
    span(f(a["ev_w_ukv"]), 1, 0, 8)
    for c in range(8):
        full(f(a["ev_w_out"]), r(c * P))

    def rest(l):
        up, down = np.asarray(a["w_mlp_up"])[l], np.asarray(a["w_mlp_down"])[l]
        for g in range(N_GROUPS):
            for c in range(HID_GROUP):
                full(up, r((g * HID_GROUP + c) * P))
            for j in range(DC // 2):
                span(down[g * 512:(g + 1) * 512], 4, 2 * j * P, 2)
        for h in range(2):
            span(np.asarray(a["w_ple_proj"])[l], 2, 512 * h, 4)
        for c in range(8):
            full(np.asarray(a["w_ple_gate"])[l], r(c * P))

    rest(0)
    w = f(a["od_w_in"])
    for c in range(23):
        full(w, r(c * P))
    full(w, r(23 * P, 12) + [-1] * 116)
    for key in ("od_cmp_w1_k", "od_cmp_w1_v"):
        x = f(a[key]).reshape(4, 4, P, 256)
        for q in range(4):
            out.append(x[q].transpose(1, 0, 2).reshape(P, D))
    for c in range(4):
        span(f(a["od_w_out"]), 4, 2 * c * P, 2)
    rest(1)
    return np.stack(out)


def layout(a):
    a = {k: np.asarray(v) for k, v in a.items()}
    cols = lambda g: g.reshape(-1, P).T
    m = constants()
    m["xT"] = a["x"][0].T.reshape(DC, P, S)
    m["pT"] = a["p"][:, 0].transpose(0, 2, 1).reshape(2, 2, P, S)
    m["positions"] = a["positions"].reshape(1, S)
    m["w"] = weight_stream(a)
    gains = [a[k][l] for k in ("norm_mix_pre", "norm_mix_post", "norm_mlp_pre", "norm_mlp_post", "ple_norm")
             for l in range(2)]
    m["gains"] = np.stack([cols(g) for g in gains], axis=1)
    m["qkvg"] = np.concatenate([cols(a["ev_q_norm"][0]), cols(a["ev_kv_norm"][0])], axis=1)
    m["const"][64:72, 5] = a["ev_forget_bias"][0]
    m["t5"] = a["t5_bias"]
    pos = np.stack([a["od_cmp_pos_k"][0], a["od_cmp_pos_v"][0]])
    m["posc"] = pos.reshape(2, 16, P).transpose(2, 1, 0)
    k2 = a["od_cmp_w2_k"][0].reshape(2, P, HD).transpose(1, 0, 2)
    m["w2k"] = np.concatenate([k2, k2], axis=2)
    m["w2v"] = a["od_cmp_w2_v"][0].reshape(2, P, HD).transpose(1, 0, 2)
    return {k: np.ascontiguousarray(v) for k, v in m.items()}


STOP = None


def kernel(**inputs):
    import concourse.bacc as bacc
    from concourse.bass_utils import run_bass_kernel_spmd

    nc = bacc.Bacc("TRN2", target_bir_lowering=False, num_devices=1)
    arrays = layout(inputs)
    ins = {k: nc.dram_tensor(f"in_{k}", v.shape, mybir.dt.from_np(v.dtype), kind="ExternalInput").ap()
           for k, v in arrays.items()}
    out = nc.dram_tensor("out", (DC, P, S), F32, kind="ExternalOutput").ap()
    program(nc, ins, out, STOP)
    r = run_bass_kernel_spmd(nc, [{f"in_{k}": v for k, v in arrays.items()}], core_ids=[0])
    y = np.asarray(r.results[0]["out"])
    return np.ascontiguousarray(y.reshape(D, S).T)[None]
```

```python
import math
from contextlib import ExitStack

import numpy as np

import concourse.bass as bass
from concourse import mybir

F32 = mybir.dt.float32
F32R = mybir.dt.float32r
I32 = mybir.dt.int32
ALU = mybir.AluOpType
ACT = mybir.ActivationFunctionType

P = 128
S = 1024
D = 1024
DC = D // P
NB = S // P
HALF = 512
HD = 64
KB = 1024
EPS = 1e-6
NEG = -1e30
ISCALE = 8.0
MLA_SCALE = 96 ** -0.5
HID_GROUP = 4
N_GROUPS = 4 * D // P // HID_GROUP
N_CMP = 63
WIN_BLOCKS = 4

SEL_W, WIN_W, DIL_W, D16_W = S, (WIN_BLOCKS + 1) * P, 2 * P, P
BROW = {"sel": 0, "win": 1152, "d1": 1920, "d4": 2304, "d16": 2688}
BROW_N = 2944


def unit_plan():
    full = lambda kind, idx, step=0, src="x": (8, src, [(kind, idx, step)])
    mlp = [full("up", c) for c in range(HID_GROUP)]
    mlp += [(4, "hid", [("down", 2 * j, 0), ("down", 2 * j + 1, 0)]) for j in range(DC // 2)]
    segs = []

    def rest(l):
        segs.append((f"mlpa{l}", 1, mlp))
        segs.append((f"mlp{l}", N_GROUPS - 2, mlp))
        segs.append((f"mlpz{l}", 1, mlp))
        segs.append((f"ple{l}", 1, [(2, "p", [("ple", 4 * a + j, 0) for j in range(4)]) for a in range(2)]))
        segs.append((f"gate{l}", 1, [full("gate", c) for c in range(DC)]))

    segs.append(("in0a", 1, [full("cq", 0), full("cq", 1), full("cq", 2), full("misc", 0)]))
    segs.append(("in0p", 1, [full("foxs", 0), full("foxs", 1)]))
    segs.append(("in0b", 3, [full("foxs", 2, 2), full("foxs", 3, 2)]))
    segs.append(("in0c", 2, [full("fox", 0, 2), full("fox", 1, 2)]))
    segs.append(("up0", 1, [(2, "cq", [("uq", 4 * a + j, 0) for j in range(4)]) for a in range(2)]
                 + [(1, "ckv", [("ukv", j, 0) for j in range(8)])]))
    segs.append(("out0", 1, [full("out", c) for c in range(DC)]))
    rest(0)
    segs.append(("in1p", 1, [full("odds", 0, 0, "x1"), full("odds", 1, 0, "x1"), full("odd", 6, 0, "x1"),
                             full("odd", 7, 0, "x1")]))
    segs.append(("in1a", 5, [full("odds", c, 2, "x1") for c in (2, 3)]))
    segs.append(("in1b", 3, [full("odd", c, 2, "x1") for c in (0, 1)]))
    segs.append(("in1c", 1, [full(kind, c, 0, "x1") for kind, c in (("odds", 12), ("odds", 13), ("oddk", 14),
                                                                    ("oddk", 15))]))
    segs.append(("out1", 1, [(4, "x", [("out", 2 * a, 0), ("out", 2 * a + 1, 0)]) for a in range(4)]))
    rest(1)
    return segs


EXTRA = {"in0a": [("brow", 0), ("brow", 1), ("brow", 2)], "in1c": [("gt", 0)], "out1": [("kc", 0)]}
GELU_STEPS = 6
T_SLOTS = 2
MERGE_STEPS = 11
POOL_STEPS = 7
ROPE_KEY_STEPS = 3
DVE_ANGLE = 10
DVE_FZ = 11
DVE_ALL = 17
ACT_RELEASES = {"gt", "kc", "uq", "ukv", "out", "ple", "brow"}
DVE_RELEASES = {"cq", "misc", "fox", "foxs", "odd", "odds", "oddk", "up", "down", "gate", "uq", "kc"}
SPLIT = {"foxs", "odds", "oddk"}
STORED = {"fox", "odd", "uq", "ukv"} | SPLIT


class Tile:

    def __init__(self, kind, idx, no, prev):
        self.kind, self.idx, self.no, self.pair = kind, idx, no, no % 2
        self.act = (prev.act if prev else 0) + (kind in ACT_RELEASES)
        self.dve = (prev.dve if prev else 2) + (kind in DVE_RELEASES)
        self.store = list(prev.store) if prev else [1, 1]
        self.up = (prev.up if prev else 0) + (kind == "up")
        self.down = (prev.down if prev else 0) + (kind == "down")
        self.gate = (prev.gate if prev else 0) + (kind == "gate")
        self.split = (prev.split if prev else 0) + (kind in SPLIT)
        self.slot_before = list(self.store)
        if kind in STORED:
            self.store[self.pair] += 1


    def released(self):
        return {"act": self.act, "dve": self.dve}


class Unit:
    def __init__(self, no, k, src, tiles, tiles_end):
        self.no, self.k, self.src, self.tiles, self.tiles_end = no, k, src, tiles, tiles_end


class Seg:
    def __init__(self, name, n, iters):
        self.name, self.n, self.iters = name, n, iters


def build_segments(extra_before):
    segs, extras, tiles, units = {}, {}, [], []

    def tile(kind, idx):
        tiles.append(Tile(kind, idx, len(tiles), tiles[-1] if tiles else None))
        return tiles[-1]

    for name, n, body in unit_plan():
        extras[name] = [tile(*x) for x in extra_before.get(name, [])]
        iters = []
        for it in range(n):
            row = []
            for pos, (k, src, kinds) in enumerate(body):
                made = [tile(kind, i0 + it * step) for kind, i0, step in kinds]
                end = len(tiles)
                units.append(Unit(len(units), k, src, made, end))
                row.append(units[-1])
            iters.append(row)
        segs[name] = Seg(name, n, iters)
    return segs, extras, tiles, units


def need(eng, sem, vals, it):
    if len(vals) == 1:
        if vals[0] > 0:
            eng.wait_ge(sem, vals[0])
        return
    if len(vals) == 2:
        slope = vals[1] - vals[0]
    else:
        slope = vals[2] - vals[1]
        assert all(vals[k + 1] - vals[k] == slope for k in range(1, len(vals) - 1)), vals
    first = vals[1] - slope
    assert first >= (slope > 0), vals
    if first < vals[0]:
        eng.wait_ge(sem, vals[0])
    if slope == 0:
        if first > 0:
            eng.wait_ge(sem, first)
        return
    eng.wait_ge(sem, it * slope + first)
    eng.nop(nofuse=True)


def at(idx0, step, it):
    return idx0 if step == 0 or isinstance(it, int) and it == 0 else it * step + idx0


TASK0 = 2 * NB
DILATED = ("d1", "d4", "d16")
NSA = ("cmp", "sel", "win")


class Job:

    def __init__(self, kind, pair, slot, prev_same_slot, c0):
        self.kind, self.pair, self.slot, self.prev = kind, pair, slot, prev_same_slot
        self.c0 = dict(c0)
        self.heads = 1 if kind == "mla" else 2
        self.nt = NB * self.heads
        self.vgroups = [] if kind == "cmp" else [dict(g=g, eng="A") for g in range(2)]
        self.tasks = []
        for n in range(self.nt):
            e, i = divmod(n, NB)
            blocks = self.blocks(i)
            t = dict(n=n, e=e, i=i, blocks=blocks, T=c0["task"] + n, groups=[])
            for g0 in range(0, len(blocks), 4):
                eng = "D" if (len(blocks) <= 4 or g0 > 0) else "A"
                t["groups"].append(dict(g0=g0, g1=min(len(blocks), g0 + 4), eng=eng))
            self.tasks.append(t)
        kinds = {"fox": ["o"], "mla": ["o"] if pair % 2 else [], "d1": ["u", "l", "m"],
                 "d4": ["u", "l", "m"], "d16": ["u", "l", "m"], "win": ["o"]}.get(kind, [])
        self.ogroups = [dict(what=what, g=g, eng="D") for what in kinds for g in range(2)]
        n_ops = 2 if kind == "mla" else 0
        loads = {"fox": 1, "mla": 4, "d1": 1, "d4": 1, "d16": 1, "sel": 2, "win": 2, "cmp": 0}[kind]
        hloads = {"mla": 0, "cmp": 2}.get(kind, 6)
        self.kfree = c0["task"] - NB
        self.c1 = dict(task=c0["task"] + self.nt, ops=c0["ops"] + n_ops, load=c0["load"] + loads,
                       hload=c0["hload"] + hloads, bias=c0["bias"] + (kind not in ("mla", "cmp")), rl=c0["rl"] + (0 if kind in DILATED else self.nt),
                       cf=c0["cf"] + (self.nt if kind in NSA else 0),
                       oh=c0["oh"] + sum(g["what"] == "o" for g in self.ogroups))

    def blocks(self, i):
        k = self.kind
        if k in ("fox", "mla", "sel"):
            return list(range(i + 1))
        if k == "win":
            return list(range(max(0, i - WIN_BLOCKS), i + 1))
        if k == "d1":
            return list(range(max(0, i - 1), i + 1))
        if k == "d4":
            return [i - 1, i] if i % 2 else [i]
        return [i] if k == "d16" else [0]

    def width(self, i):
        return HD if self.kind == "cmp" else P * len(self.blocks(i))


def token(kind, block):
    if kind == "d4":
        return block // 2 + 4 * P * (block % 2)
    return block if kind == "d16" else block * P


def pipeline(row):
    flat = [(p, n) for p, j in enumerate(row) for n in range(j.nt)]
    ends = {sum(j.nt for j in row[:p + 1]) - 1: p for p in range(len(row))}
    get = lambda k: flat[k] if 0 <= k < len(flat) else None
    return [dict(start=get(k)[0] if get(k) and get(k)[1] == 0 else None, logits=get(k), turn=get(k - 2),
                 values=get(k - 3), end=ends.get(k - 4)) for k in range(len(flat) + 4)]


def build_jobs():
    c = dict(task=TASK0, ops=2, load=0, hload=0, bias=0, rl=2, cf=2, oh=2)
    last = {0: None, 1: None}
    phases, flat, pv = {}, [], 2
    bodies = {
        "fox": (2, [("fox", 2, 0, 0), ("fox", 2, 1, 1)]),
        "mla": (4, [("mla", 2, 0, 0), ("mla", 2, 1, 1)]),
        "dil": (2, [("d1", 1, 0, 0), ("d4", 1, 0, 1), ("d16", 1, 0, 0)]),
        "nsa": (2, [("cmp", 1, 0, 0), ("sel", 1, 0, 1), ("win", 1, 0, 0)]),
    }
    groups = []
    for name, (n, body) in bodies.items():
        rows = []
        for it in range(n):
            row = []
            for kind, step, first, slot in body:
                j = Job(kind, first + step * it, slot, last[slot], c)
                j.step, j.first = step, first
                for t in j.tasks:
                    for g in t["groups"]:
                        pv += 1
                        g["pv"] = pv
                last[slot] = j
                c = j.c1
                row.append(j)
                flat.append(j)
            rows.append(row)
        phases[name] = (n, rows)
    n = dict(tr=2, A=2, D=2, pv=2, vA=2, ot=2)

    def group(g):
        n["tr"] += 1
        n[g["eng"]] += 1
        g.update(tr=n["tr"], ring=(n["tr"] - 1) % 2, rel=(g["eng"], n[g["eng"]]))
        groups.append(g["rel"])

    for _, rows in phases.values():
        for row in rows:
            for st in pipeline(row):
                if st["start"] is not None:
                    j = row[st["start"]]
                    j.v_before = n["vA"]
                    for g in j.vgroups:
                        group(g)
                    if j.vgroups:
                        n["vA"] = n["A"]
                if st["values"]:
                    t = row[st["values"][0]].tasks[st["values"][1]]
                    for g in t["groups"]:
                        n["pv"] += 1
                        assert g["pv"] == n["pv"]
                if st["turn"]:
                    j = row[st["turn"][0]]
                    t = j.tasks[st["turn"][1]]
                    for g in t["groups"]:
                        group(g)
                    t["done"] = n["tr"]
                if st["end"] is not None:
                    for g in row[st["end"]].ogroups:
                        group(g)
                    if row[st["end"]].ogroups:
                        n["ot"] = n["tr"]
                if st["values"] and st["values"][1] == 0:
                    row[st["values"][0]].ot_before = n["ot"]
    done = [2] * 4
    for j in flat:
        for t in j.tasks:
            wide = j.kind in DILATED + NSA and not (j is phases["dil"][1][0][0] and t["n"] < 4)
            t["tr_before"] = done[-4 if wide else -2]
            done.append(t["done"])
        j.pv_end = j.tasks[-1]["groups"][-1]["pv"]
    flat[-1].counts = n
    return phases, flat, groups


def program(nc, ins, out):
    segs, extras, tiles, units = build_segments(EXTRA)
    phases, jobs, pt_groups = build_jobs()

    ctx = ExitStack()
    with ctx:
        nc_base = 16512 // 32 * 32

        def sb(name, shape, kb, dt=F32):
            return nc.alloc_sbuf_tensor_at(name, shape, dt, offset=nc_base + int(kb * KB))

        def sem(name):
            return ctx.enter_context(nc.semaphore(name))

        H = sb("H", [P, DC, S], 0)
        XH = sb("XH", [P, DC, S], 32, F32R)
        XL = sb("XL", [P, DC, S], 64, F32R)
        HH = sb("HH", [P, HID_GROUP, S], 96, F32R)
        HL = sb("HL", [P, HID_GROUP, S], 112, F32R)
        PP = sb("PP", [P, DC, S], 96)
        M = sb("M", [P, DC, S], 128)
        T = sb("T", [P, 2, S], 160)
        HALVES = sb("HALVES", [P, 2, 2, S], 160, F32R)
        TL, QR = HALVES[:, 0], HALVES[:, 1]
        Q = sb("Q", [P, 2, S], 168)
        R = sb("R", [P, S], 176)
        RAW = sb("RAW", [P, 2, S], 180)
        WH = sb("WH", [P, 2, S], 188, F32R)
        WL = sb("WL", [P, 2, S], 196, F32R)
        CQ = sb("CQ", [P, 3, S], 96)
        CQH = sb("CQH", [P, 3, S], 108, F32R)
        CQL = sb("CQL", [P, 3, S], 120, F32R)
        MISC1 = sb("MISC", [P, 1, S], 132)
        MISC = MISC1[:, 0]
        CS = sb("CS", [P, S], 136)
        ANG = sb("ANG", [P, 3, S], 140)
        POS = sb("POS", [P, S], 152, I32)
        KR = sb("KR", [P, S], 156)
        KT = sb("KT", [P, S], 152)
        RC = sb("RC", [P, S], 148)
        PRAW = sb("PRAW", [P, 2, S], 48)
        X1H = sb("X1H", [P, DC, S], 128, F32R)
        X1L = sb("X1L", [P, DC, S], 96, F32R)
        QK = sb("QK", [P, 2, 4, S], 96, F32R)
        V = sb("V", [P, 2, NB, P], 128)
        RQ = sb("RQ", [P, S], 136)
        RK = sb("RK", [P, S], 140)
        RV = sb("RV", [P, S], 144)
        PB = sb("PB", [P, 2, S], 148)
        PBX = sb("PBX", [P, 2, S], 136)
        PT = sb("PT", [P, 2, HALF], 156)
        BIAS = sb("BIAS", [P, 2, 2 * S], 160)
        OT = sb("OT", [P, NB, P], 176)
        BIASD = sb("BIASD", [P, 2, 2, DIL_W], 160)
        DU = sb("DU", [P, 3, S], 48)
        DL = sb("DL", [P, 3, S], 80)
        DM = sb("DM", [P, 3, S], 164)
        OL = sb("OL", [P, NB, P], 60)
        OM = sb("OM", [P, NB, P], 92)
        CMPMASK = sb("CMPMASK", [P, NB * HD], 116)
        CMPX = sb("CMPX", [P, 2, S + 32], 32)
        CBF = sb("CBF", [P, 2, 16, HD], 41)
        HIDF = sb("HIDF", [P, 2, 2, HD], 49)
        HIDT = sb("HIDT", [P, 2, 2, HD], 50)
        HIDU = sb("HIDU", [P, 2, 2, HD], 51)
        W2K = sb("W2K", [P, 2, P], 52)
        W2V = sb("W2V", [P, 2, HD], 53)
        POSC = sb("POSC", [P, 16, 2], 54)
        GTT = sb("GTT", [12, S], 55)
        W1 = sb("W1", [P, 8, S], 64)
        BRS = sb("BRS", [16, BROW_N], 108)
        ONEHOT = sb("ONEHOT", [33, BROW_N], 120)
        o = 204.0
        IDENT = sb("IDENT", [P, P], o)
        ONES = sb("ONES", [P, P], o + 0.5)
        IDR = sb("IDR", [P, P], o + 1, F32R)
        MKR = sb("MKR", [P, P], o + 1.5, F32R)
        GAINS = sb("GAINS", [P, 10, DC], o + 2)
        QKVG = sb("QKVG", [P, 3], o + 2.3125)
        CONST = sb("CONST", [P, 8], o + 2.34375)
        NM = sb("NM", [P, 16], o + 2.375)
        L = sb("L", [P, 16], o + 2.4375)
        RL = sb("RL", [P, 16], o + 2.5)
        CF = sb("CF", [P, 16], o + 2.5625)
        GT = sb("GT", [P, NB, 12], o + 2.625)
        KCH = sb("KCH", [P, HD], o + 3, F32R)
        KCL = sb("KCL", [P, HD], o + 3.25, F32R)
        VC = sb("VC", [HD, HD], o + 3.5)
        T5 = sb("T5", [33, 16], o + 3.75)

        ps = lambda name, shape: ctx.enter_context(nc.psum_tensor(name, shape, F32))
        ACC = ps("ACC", [P, 2, S])
        TR = ps("TR", [P, 2, HALF])
        OP = ps("OP", [P, 2, HALF])

        dram = lambda name, shape: nc.dram_tensor(name, shape, F32, kind="Internal").ap()
        y_foxs = dram("y_foxs", (8, 2, P, S))
        y_fox = dram("y_fox", (4, P, S))
        y_q = dram("y_q", (8, P, S))
        y_kv = dram("y_kv", (8, P, S))
        y_kr = dram("y_kr", (32, S))
        y_f = dram("y_f", (8, S))
        y_odds = dram("y_odds", (16, 2, P, S))
        y_odd = dram("y_odd", (8, P, S))
        y_v = dram("y_v", (2, HD, S))
        b_rows = dram("b_rows", (16, BROW_N))
        b_tile = {"sel": dram("b_sel", (4, P, SEL_W)), "win": dram("b_win", (4, P, WIN_W)),
                  "d1": dram("b_d1", (4, P, DIL_W)), "d4": dram("b_d4", (4, P, DIL_W)),
                  "d16": dram("b_d16", (4, P, D16_W))}

        s_const = sem("s_const")
        s_mask = sem("s_mask")
        s_pos = sem("s_pos")
        s_ones = sem("s_ones")
        s_h = [sem(f"s_h{m}") for m in range(4)]
        s_raw = [sem("s_raw0"), sem("s_raw1")]
        s_whi = sem("s_whi")
        s_split = sem("s_split")
        s_tile = sem("s_tile")
        s_evA = sem("s_evA")
        s_evD = sem("s_evD")
        s_store = [sem("s_store0"), sem("s_store1")]
        s_hi = sem("s_hi")
        s_lo = sem("s_lo")
        s_cqn = sem("s_cqn")
        s_hhi = sem("s_hhi")
        s_sqh = sem("s_sqh")
        s_hid = sem("s_hid")
        s_rope = sem("s_rope")
        s_sq = sem("s_sq")
        s_st = sem("s_st")
        s_rt = sem("s_rt")
        s_R = sem("s_R")
        s_T = sem("s_T")
        s_xh = sem("s_xh")
        s_x = sem("s_x")
        s_res = sem("s_res")
        s_sig = sem("s_sig")
        s_gm = sem("s_gm")
        s_pload = sem("s_pload")
        s_phi = sem("s_phi")
        s_p = sem("s_p")
        s_dve = sem("s_dve")
        s_ft = sem("s_ft")
        s_misc = sem("s_misc")
        s_load = sem("s_load")
        s_bias = sem("s_bias")
        s_head = [sem("s_head0"), sem("s_head1")]
        s_phi2 = sem("s_phi2")
        s_ops = sem("s_ops")
        s_qk = sem("s_qk")
        s_ttr = sem("s_ttr")
        s_exp = sem("s_exp")
        s_tr = sem("s_tr")
        s_ptA = sem("s_ptA")
        s_ptD = sem("s_ptD")
        s_pv = sem("s_pv")
        s_ox = sem("s_ox")
        s_pm = sem("s_pm")
        s_mg = sem("s_mg")
        s_rl = sem("s_rl")
        s_cf = sem("s_cf")
        s_o = sem("s_o")
        s_oh = sem("s_oh")
        s_bd = sem("s_bd")
        s_vst = sem("s_vst")
        s_cb = sem("s_cb")
        s_w1 = sem("s_w1")
        s_cu = sem("s_cu")
        s_t5 = sem("s_t5")
        s_hidf = sem("s_hidf")
        s_gl = sem("s_gl")
        s_ge = sem("s_ge")
        s_md = sem("s_md")
        s_cmp = sem("s_cmp")
        s_cl = sem("s_cl")
        s_cz = sem("s_cz")
        s_out = sem("s_out")

        N_CONST = 5
        block = ctx.enter_context(nc.Block())

        rounds = [("x", 8), ("cq", 2), ("ckv", 1), ("m0", 8), ("h0", 8), ("n0", 8), ("g0", 8), ("x1", 8),
                  ("m1", 8), ("h1", 8), ("n1", 8), ("g1", 8)]
        rnd, q0 = {}, 0
        for no, (name, n) in enumerate(rounds):
            rnd[name] = (no, q0, n)
            q0 += n
        GAIN = {"x": 0, "x1": 1, "m0": 2, "m1": 3, "h0": 4, "h1": 5, "n0": 6, "n1": 7, "g0": 8, "g1": 9}
        applies, x0 = {}, 0
        for name, n in (("x", 8), ("cq", 3), ("h0", 8), ("g0", 8), ("x1", 8), ("h1", 8), ("g1", 8)):
            applies[name] = x0
            x0 += n
        resids = {"m0": 0, "n0": 8, "ga0": 16, "m1": 24, "n1": 32, "ga1": 40}
        tcount = {"m0": 0, "n0": 8, "m1": 16, "n1": 24}
        TASKS_EVEN = phases["mla"][1][-1][-1].c1
        TASKS_ODD = phases["nsa"][1][-1][-1].c1
        COPIES = {name: rows[-1][-1].ogroups[-1]["rel"][1] for name, (_, rows) in phases.items()}
        segs_first = {n: segs[g].iters[0][0] for n, g in
                      {"x": "in0a", "h0": "mlpa0", "g0": "gate0", "x1": "in1p", "h1": "mlpa1", "g1": "gate1"}.items()}
        seg_end = {n: s.iters[-1][-1].tiles_end for n, s in segs.items()}

        def prob(j, t):
            if j.kind in DILATED + NSA:
                return (PB if t["T"] % 4 < 2 else PBX)[:, t["T"] % 2]
            return PB[:, t["T"] % 2]

        def chunk_of(x, name, pos, it):
            c = {"fox": it * 2 + (4 + pos), "mla": it, "dil": it, "nsa": it + 2}[name]
            return x[:, bass.ds(c, 1)].rearrange("p o s -> p (o s)")

        def run(eng, n, body):
            if n > 1:
                with eng.Fori(0, n) as it:
                    body(it)
            else:
                body(0)

        def load_h(eng, m):
            eng.dma_start(H[:, 2 * m:2 * m + 2], ins["xT"][2 * m:2 * m + 2].rearrange("c p s -> p c s"))\
                .then_inc(s_h[m], 16)

        @block.sync
        def _(sp):
            sp.dma_start(T5[0:32, :], ins["t5"]).then_inc(s_t5, 16)
            sp.dma_start(ONEHOT[:], ins["onehot"]).then_inc(s_t5, 16)
            for dst, key in ((GAINS, "gains"), (CONST, "const"), (IDENT, "ident"), (QKVG, "qkvg")):
                sp.dma_start(dst[:], ins[key]).then_inc(s_const, 16)
            sp.dma_start(KR[:, 0:P], ins["mask"]).then_inc(s_const, 16)
            load_h(sp, 0)

            def weights(name):
                seg = segs[name]

                def body(it):
                    for pos in range(len(seg.iters[0])):
                        us = [row[pos] for row in seg.iters]
                        slot = us[0].no % 2
                        need(sp, s_split, [u.no - 1 for u in us], it)
                        sp.dma_start(RAW[:, slot], ins["w"][bass.ds(at(us[0].no, len(seg.iters[0]), it), 1)]
                                     .rearrange("o p n -> p (o n)")).then_inc(s_raw[slot], 16)
                run(sp, seg.n, body)

            def attention(name):
                n, rows = phases[name]

                def staged():
                    last = tiles[seg_end["up0" if name == "fox" else "in1c"] - 1]
                    sp.wait_ge(s_store[0], 16 * last.store[0])
                    sp.wait_ge(s_store[1], 16 * last.store[1])

                def body(it):
                    for pos, j in enumerate(rows[0]):
                        js = [row[pos] for row in rows]
                        slot = j.slot
                        pair = at(j.first, j.step, it)

                        def load(dst, src):
                            sp.dma_start(dst, src).then_inc(s_load, 16)

                        def rows_of(t, idx, lo=0, hi=P):
                            return t[bass.ds(idx, 1), lo:hi].rearrange("o p s -> (o p) s")

                        def load_bias(dst, src):
                            need(sp, s_ttr, [k.prev.c1["task"] if k.prev else TASK0 for k in js], it)
                            if name == "fox" and pos == 1 or j.kind == "d1":
                                staged()
                            if j.kind == "sel":
                                sp.wait_ge(s_ox, 1 + 2)
                            sp.dma_start(dst, src).then_inc(s_bias, 16)

                        if j.vgroups:
                            need(sp, s_ptA, [k.v_before for k in js], it)
                        if j.kind == "mla":
                            need(sp, s_ops, [k.c0["ops"] for k in js], it)
                        if name == "fox":
                            load(RV[:], rows_of(y_fox, pair))
                            biases = (BIAS[:, slot], y_f[bass.ds(pair * 2, 2)]
                                      .rearrange("(o h) s -> o (h s)", o=1).to_broadcast([P, 2 * S]))
                        elif name == "mla":
                            load(RQ[0:96], rows_of(y_q, pair, 0, 96))
                            load(RK[0:64], rows_of(y_kv, pair, 0, 64))
                            load(RK[64:96], y_kr)
                            load(RV[0:64], rows_of(y_kv, pair, 64, 128))
                        elif name == "dil":
                            g = DILATED.index(j.kind)
                            w = D16_W if g == 2 else DIL_W
                            load(RV[:], rows_of(y_odd, pair + 2 * g))
                            biases = (BIASD[:, slot, :, 0:w],
                                      b_tile[j.kind][bass.ds(pair * 2, 2)].rearrange("h p u -> p h u"))
                        elif j.kind != "cmp":
                            w = SEL_W if j.kind == "sel" else WIN_W
                            for r in (0, 64):
                                load(RV[r:r + 64], y_v[0 if j.kind == "sel" else 1])
                            biases = (BIAS[:, slot, 0:2 * w].rearrange("p (h u) -> p h u", h=2),
                                      b_tile[j.kind][bass.ds(pair * 2, 2)].rearrange("h p u -> p h u"))
                        if name == "mla":
                            continue
                        y, q, k_ = {"fox": (y_foxs, 0, 4), "dil": (y_odds, 0, 6), "nsa": (y_odds, 12, None)}[name]
                        g = 2 * DILATED.index(j.kind) if name == "dil" else 0
                        for e in range(2):
                            if e == 1 and j.kind != "cmp":
                                load_bias(*biases)
                            need(sp, s_qk, [k.c0["task"] - NB * (1 - e) for k in js], it)
                            rows_e = slice(e * HD, (e + 1) * HD)
                            for half in range(2):
                                src = y[bass.ds(pair + q + g, 1), 1 - half, rows_e].rearrange("o p s -> (o p) s")
                                sp.dma_start(QK[half * HD:(half + 1) * HD, e, 0].bitcast(F32), src).then_inc(s_head[e], 16)
                            if j.kind == "cmp":
                                continue
                            for r in (0, 64):
                                for half in range(2):
                                    if name == "nsa":
                                        src = y[14 if j.kind == "sel" else 15, 1 - half, 0:HD]
                                    else:
                                        src = y[bass.ds(pair + k_ + g, 1), 1 - half, rows_e]\
                                            .rearrange("o p s -> (o p) s")
                                    sp.dma_start(QK[r:r + HD, e, 2 + half].bitcast(F32), src).then_inc(s_head[e], 16)
                run(sp, n, body)

            def store_out(name):
                for c in range(DC):
                    sp.wait_ge(s_res, resids[name] + c + 1)
                    sp.dma_start(out[c], H[:, c]).then_inc(s_out, 16)
                sp.wait_ge(s_out, 16 * DC)

            def p_load(l):
                sp.wait_ge(s_tile, segs[f"mlpz{l}"].iters[0][HID_GROUP - 1].tiles_end)
                sp.dma_start(PRAW[:], ins["pT"][l].rearrange("c p s -> p c s")).then_inc(s_pload, 16)

            weights("in0a")
            sp.wait_ge(s_evA, extras["in0a"][2].act)
            sp.dma_start(b_rows, BRS[:]).then_inc(s_bd, 16)
            sp.wait_ge(s_bd, 16)

            def skew(kind, head0, width):
                src = bass.AP(b_rows.tensor, head0 * BROW_N + BROW[kind] + P - 1, [[BROW_N, 4], [-1, P], [1, width]])
                sp.dma_start(b_tile[kind], src).then_inc(s_bd, 16)

            skew("sel", 12, SEL_W)
            skew("win", 12, WIN_W)
            skew("d1", 0, DIL_W)
            skew("d4", 4, DIL_W)
            skew("d16", 8, D16_W)
            for name in ("in0p", "in0b", "in0c", "up0"):
                weights(name)
            last = tiles[seg_end["in0c"] - 1]
            sp.wait_ge(s_store[0], 16 * last.store[0])
            sp.wait_ge(s_store[1], 16 * last.store[1])
            sp.wait_ge(s_misc, 32)
            sp.wait_ge(s_tile, seg_end["up0"])
            sp.wait_ge(s_evD, tiles[seg_end["up0"] - 1].dve)
            attention("fox")
            sp.wait_ge(s_ttr, phases["fox"][1][-1][-1].c1["task"])
            sp.dma_start(BIAS[:, 0, 0:S], ins["mlamask"]).then_inc(s_mask, 16)
            attention("mla")
            weights("out0")
            for name in ("mlpa0", "mlp0", "mlpz0"):
                weights(name)
            p_load(0)
            weights("ple0")
            weights("gate0")
            weights("in1p")
            weights("in1a")
            for t in (u.tiles[0] for u in segs["in1p"].iters[0][2:4]):
                sp.wait_ge(s_store[t.pair], 16 * t.store[t.pair])
            for which in range(2):
                src = y_odd[6, 64 * which:64 * which + 64]
                sp.dma_start(CMPX[0:64, which, 0:S], src).then_inc(s_cl, 16)
                sp.dma_start(CMPX[64:128, which, 0:S - 1], src[:, 1:S]).then_inc(s_cl, 16)
            sp.dma_start(POSC[:], ins["posc"]).then_inc(s_cl, 16)
            sp.dma_start(GTT[:], y_odd[7, 0:12]).then_inc(s_cl, 16)
            sp.dma_start(W2K[:], ins["w2k"]).then_inc(s_cl, 16)
            sp.dma_start(W2V[:], ins["w2v"]).then_inc(s_cl, 16)
            for which in range(2):
                sp.dma_start(W1[:, 4 * which:4 * which + 4], ins["w1"][which]).then_inc(s_w1, 16)
            weights("in1b")
            weights("in1c")
            sp.wait_ge(s_tile, seg_end["in1c"])
            last = segs["in1b"].iters[-1][-1].tiles[-1]
            sp.wait_ge(s_store[0], 16 * last.store[0])
            sp.wait_ge(s_store[1], 16 * last.store[1])
            sp.wait_ge(s_bd, 16 * 6)
            attention("dil")
            sp.dma_start(CMPMASK[:], ins["cmpmask"]).then_inc(s_bd, 16)
            sp.wait_ge(s_vst, 32)
            attention("nsa")
            weights("out1")
            for name in ("mlpa1", "mlp1", "mlpz1"):
                weights(name)
            p_load(1)
            weights("ple1")
            weights("gate1")
            store_out("ga1")


        @block.gpsimd
        def _(pool):
            for s, n in ((s_ops, 2), (s_phi2, 2), (s_ox, 1)):
                pool.sem_inc(s, n)
            nc.gpsimd.memset(ONES[:], 1.0).then_inc(s_ones, 1)
            pool.wait_ge(s_ones, 1)
            nc.gpsimd.memset(T5[32:33, :], NEG).then_inc(s_ones, 1)
            pool.wait_ge(s_ones, 2)
            pool.wait_ge(s_const, 16 * N_CONST)
            nc.gpsimd.tensor_copy(IDR[:], IDENT[:]).then_inc(s_ones, 1)
            nc.gpsimd.tensor_copy(MKR[:], KR[:, 0:P]).then_inc(s_ones, 1)

            def weights(name):
                seg = segs[name]

                def body(it):
                    for pos in range(len(seg.iters[0])):
                        us = [row[pos] for row in seg.iters]
                        slot = us[0].no % 2
                        need(pool, s_raw[slot], [16 * (u.no // 2 + 1) for u in us], it)
                        need(pool, s_tile, [units[u.no - 2].tiles_end if u.no > 1 else 0 for u in us], it)
                        nc.gpsimd.tensor_copy(WH[:, slot], RAW[:, slot]).then_inc(s_whi, 1)
                        need(pool, s_whi, [u.no + 1 for u in us], it)
                        nc.gpsimd.tensor_tensor(WL[:, slot], RAW[:, slot], WH[:, slot].bitcast(F32),
                                                ALU.subtract).then_inc(s_split, 1)
                run(pool, seg.n, body)

            def attention(name):
                n, rows = phases[name]

                def body(it):
                    for pos, j in enumerate(rows[0]):
                        js = [row[pos] for row in rows]
                        pairs = [(0, RQ), (2, RK)]
                        need(pool, s_load, [16 * k.c1["load"] for k in js], it)
                        need(pool, s_qk, [k.kfree for k in js], it)
                        for part, raw in pairs:
                            nc.gpsimd.tensor_copy(QK[:, j.slot, part], raw[:]).then_inc(s_phi2, 1)
                        for m, (part, raw) in enumerate(pairs):
                            need(pool, s_phi2, [k.c0["ops"] + m + 1 for k in js], it)
                            nc.gpsimd.tensor_tensor(QK[:, j.slot, part + 1], raw[:],
                                                    QK[:, j.slot, part].bitcast(F32), ALU.subtract).then_inc(s_ops, 1)
                run(pool, n, body)

            def merge(it):
                n, m = 2, [0]

                def step(ins):
                    m[0] += 1
                    ins.then_inc(s_pm, 1)
                    need(pool, s_pm, [POOL_STEPS * k + m[0] for k in range(n)], it)

                for g in range(3):
                    need(pool, s_mg, [3 * k + g + 1 for k in range(n)], it)
                    step(nc.gpsimd.tensor_tensor(DU[:, g], DU[:, g], DM[:, g], ALU.mult))
                for g in (1, 2):
                    step(nc.gpsimd.tensor_tensor(DU[:, 0], DU[:, 0], DU[:, g], ALU.add))
                need(pool, s_md, [MERGE_STEPS * (k + 1) for k in range(n)], it)
                step(nc.gpsimd.tensor_tensor(DU[:, 0], DU[:, 0], DL[:, 0], ALU.mult))
                xh, xl = (x[:, bass.ds(it, 1)].rearrange("p o s -> p (o s)") for x in (XH, XL))
                step(nc.gpsimd.tensor_copy(xh, DU[:, 0]))
                assert m[0] == POOL_STEPS
                nc.gpsimd.tensor_tensor(xl, DU[:, 0], xh.bitcast(F32), ALU.subtract).then_inc(s_ox, 1)

            for name in ("in0a", "in0p", "in0b", "in0c", "up0"):
                weights(name)
            last = tiles[seg_end["up0"] - 1]
            pool.wait_ge(s_evD, last.dve)
            pool.wait_ge(s_misc, 32)
            pool.wait_ge(s_split, segs["up0"].iters[0][-1].no + 1)
            nc.gpsimd.memset(RQ[96:128], 0.0).then_inc(s_ones, 1)
            pool.wait_ge(s_ones, 5)
            nc.gpsimd.memset(RK[96:128], 0.0).then_inc(s_ones, 1)
            pool.wait_ge(s_ones, 6)
            attention("mla")
            weights("out0")
            for name in ("mlpa0", "mlp0", "mlpz0"):
                weights(name)
            weights("ple0")
            weights("gate0")
            weights("in1p")
            pool.wait_ge(s_tile, seg_end["gate0"])
            pool.wait_ge(s_split, segs["in1p"].iters[0][-1].no + 1)
            nc.gpsimd.memset(CMPX[0:64, :, S:S + 32], 0.0).then_inc(s_cz, 1)
            pool.wait_ge(s_cz, 1)
            nc.gpsimd.memset(CMPX[64:128, :, S - 1:S + 32], 0.0).then_inc(s_cz, 1)
            pool.wait_ge(s_cz, 2)
            for name in ("in1a", "in1b", "in1c"):
                weights(name)
            run(pool, 2, merge)
            weights("out1")
            for name in ("mlpa1", "mlp1", "mlpz1"):
                weights(name)
            weights("ple1")
            weights("gate1")

        @block.tensor
        def _(pe):
            def operands(src):
                return {"x": (XH, XL), "hid": (HH, HL), "cq": (CQH[:, 0:2], CQL[:, 0:2]),
                        "ckv": (CQH[:, 2:3], CQL[:, 2:3]), "p": (XH[:, 6:8], XL[:, 6:8]),
                        "x1": (X1H, X1L)}[src]

            def evacuated(ts, it):
                for s, what in ((s_evA, "act"), (s_evD, "dve")):
                    vals = [tiles[t.no - 2].released()[what] if t.no > 1 else 0 for t in ts]
                    need(pe, s, vals, it)

            def three_pass(acc, k0, kn, ws, wl_, xh, xl, first, last):
                mm = None
                for k in range(k0, kn):
                    for w, x in ((ws, xh), (ws, xl), (wl_, xh)):
                        for h in range(2):
                            mm = nc.tensor.matmul(acc[:, h * HALF:(h + 1) * HALF], w(k), x[:, k, h * HALF:(h + 1) * HALF],
                                                  start=first and k == k0 and w is ws and x is xh,
                                                  stop=last and k == kn - 1 and w is wl_)
                return mm

            def compress():
                pe.wait_ge(s_w1, 16 * 2)
                pe.wait_ge(s_cb, 1)
                pe.wait_ge(s_rt, rnd["x1"][0] + 1)
                for which, acc in ((0, OP), (1, TR)):
                    for c in range(2):
                        for m in range(16):
                            col = (m % 4) * 256 + c * P
                            mm = nc.tensor.matmul(acc[:, c, 0:HD], W1[:, 4 * which + m // 4, col:col + P],
                                                  CBF[:, which, m], start=m == 0, stop=m == 15)
                mm.then_inc(s_cu, 1)

            def weights(name, ready=None, after=None):
                seg = segs[name]

                def body(it):
                    for pos in range(len(seg.iters[0])):
                        us = [row[pos] for row in seg.iters]
                        u, slot = us[0], us[0].no % 2
                        need(pe, s_split, [v.no + 1 for v in us], it)
                        xh, xl = operands(u.src)
                        for m in range(len(u.tiles)):
                            ts = [v.tiles[m] for v in us]
                            evacuated(ts, it)
                            for k in range(u.k):
                                if ready:
                                    ready(pe, k, it, us, m)
                                col = (m * u.k + k) * P
                                mm = three_pass(ACC[:, ts[0].pair], k, k + 1,
                                                lambda _: WH[:, slot, col:col + P],
                                                lambda _: WL[:, slot, col:col + P], xh, xl,
                                                k == 0, k == u.k - 1)
                            mm.then_inc(s_tile, 1)
                            if after:
                                after(ts[0])
                run(pe, seg.n, body)

            def stats(name, chunks):
                no, q, n = rnd[name]
                for c in chunks:
                    if c == 0 and no:
                        pe.wait_ge(s_rt, no)
                    pe.wait_ge(s_sq, q + c + 1)
                    for h in range(2):
                        mm = nc.tensor.matmul(OP[:, h], ONES[:], Q[:, (q + c) % 2, h * HALF:(h + 1) * HALF],
                                              start=c == 0, stop=c == n - 1)
                    mm.then_inc(s_st, 1)

            def first_unit(name, skip=(), then=None):
                def ready(pe, k, it, us, m):
                    if us[0] is segs_first[name]:
                        if k and k - 1 not in skip:
                            stats(name, [k - 1])
                        pe.wait_ge(s_x, applies[name] + k + 1)
                    hid_ready(pe, k, it, us, m)

                def after(t):
                    if t is segs_first[name].tiles[0]:
                        stats(name, [7])
                    if then:
                        then(t)
                return dict(ready=ready, after=after)

            def sums(name, kind, lag, n=DC):
                def after(t):
                    if t.kind == kind and lag <= t.idx < n:
                        stats(name, [t.idx - lag])
                return after

            def ring_free(gs, it, eng=pe):
                prev = [pt_groups[g["tr"] - 5] if g["tr"] > 4 else None for g in gs]
                who = {p[0] for p in prev if p}
                assert len(who) <= 1, prev
                if who:
                    need(eng, s_ptA if who == {"A"} else s_ptD, [p[1] if p else 2 for p in prev], it)

            def attention(name):
                n, rows = phases[name]

                def turn_v(it, js):
                    j = js[0]
                    for g, vg in enumerate(j.vgroups):
                        if g == 0:
                            need(pe, s_load, [16 * k.c1["load"] for k in js], it)
                        ring_free([k.vgroups[g] for k in js], it)
                        r = HD if j.kind == "mla" else P
                        for b in range(4):
                            c, t0 = {"d4": 4, "d16": 8}.get(j.kind, 1), token(j.kind, 4 * g + b)
                            tr = nc.tensor.transpose(TR[:, vg["ring"], b * r:(b + 1) * r],
                                                     RV[0:r, t0:t0 + c * (P - 1) + 1:c], IDENT[0:r, 0:r])
                        tr.then_inc(s_tr, 1)

                def logits(it, js, n):
                    j = js[0]
                    slot, kind, t = j.slot, j.kind, j.tasks[n]
                    e, i, b = t["e"], t["i"], t["T"] % 2
                    need(pe, s_ttr, [k.tasks[n]["T"] - 1 for k in js], it)
                    w = j.width(i)
                    if j.kind == "mla" and n == 0:
                        need(pe, s_ops, [k.c1["ops"] for k in js], it)
                    if kind != "mla" and i == 0:
                        need(pe, s_head[e], [16 * k.c1["hload"] for k in js], it)
                    c = {"d4": 4, "d16": 8}.get(kind, 1)
                    span = lambda x, b0, m: x[:, token(kind, b0):token(kind, b0) + c * (m - 1) + 1:c]
                    qs = slot if kind == "mla" else e
                    ks = slot if kind == "mla" else e
                    q, ql = (span(QK[:, qs, m], i, P) for m in range(2))
                    if kind == "cmp":
                        kh, kl = KCH[:], KCL[:]
                    else:
                        kh, kl = (span(QK[:, ks, 2 + m], t["blocks"][0], w) for m in range(2))
                    passes = [(q, kh), (ql, kh), (q, kl)] if kind == "mla" else [(q, kh), (q, kl)]
                    for c0 in range(0, w, HALF):
                        c1 = min(w, c0 + HALF)
                        masked = kind == "fox" and c1 == w
                        for m, (x, k) in enumerate(passes):
                            mm = nc.tensor.matmul(ACC[:, b, c0:c1], x, k[:, c0:c1], start=m == 0,
                                                  stop=m == len(passes) - 1 and not masked)
                        if masked:
                            mm = nc.tensor.matmul(ACC[:, b, w - P:w], IDR[:], MKR[:], start=False, stop=True)
                    mm.then_inc(s_qk, 1)

                def turn(it, js, n):
                    t = js[0].tasks[n]
                    need(pe, s_exp, [k.tasks[n]["T"] + 1 for k in js], it)
                    for m, g in enumerate(t["groups"]):
                        ring_free([k.tasks[n]["groups"][m] for k in js], it)
                        for x in range(g["g0"], g["g1"]):
                            w = HD if js[0].kind == "cmp" else P
                            y = x - g["g0"]
                            tr = nc.tensor.transpose(TR[0:w, g["ring"], y * P:(y + 1) * P],
                                                     prob(js[0], t)[:, x * w:(x + 1) * w], IDENT[:])
                        tr.then_inc(s_tr, 1)

                def values(it, js, n):
                    j = js[0]
                    t = j.tasks[n]
                    e, b = t["e"], t["T"] % 2
                    if n == 0 and j.vgroups:
                        need(pe, s_ptA, [k.vgroups[1]["rel"][1] for k in js], it)
                    need(pe, s_o, [k.tasks[n]["T"] - 1 for k in js], it)
                    for m, g in enumerate(t["groups"]):
                        need(pe, s_ptA if g["eng"] == "A" else s_ptD,
                             [k.tasks[n]["groups"][m]["rel"][1] for k in js], it)
                        pr = (g["pv"] - 1) % 2
                        for x in range(g["g0"], g["g1"]):
                            y = x - g["g0"]
                            if j.kind == "cmp":
                                lhs, rhs = PT[0:HD, pr, 0:P], VC[:]
                            else:
                                lhs = PT[:, pr, y * P:(y + 1) * P]
                                rhs = V[:, j.slot, t["blocks"][x], HD * e:HD * e + HD]
                            mm = nc.tensor.matmul(OP[:, b, 0:HD], lhs, rhs, start=x == 0,
                                                  stop=x == len(t["blocks"]) - 1)
                        mm.then_inc(s_pv, 1)

                def turn_output(it, js):
                    for m, g in enumerate(js[0].ogroups):
                        if m == 0:
                            need(pe, s_o, [k.c1["task"] for k in js], it)
                        ring_free([k.ogroups[m] for k in js], it)
                        src = {"o": OT, "u": OT, "l": OL, "m": OM}[g["what"]]
                        for y in range(4):
                            tr = nc.tensor.transpose(TR[:, g["ring"], y * P:(y + 1) * P], src[:, 4 * g["g"] + y],
                                                     IDENT[:])
                        tr.then_inc(s_tr, 1)

                def body(it):
                    job = lambda p: [row[p] for row in rows]
                    for st in pipeline(rows[0]):
                        if st["start"] is not None:
                            turn_v(it, job(st["start"]))
                        if st["logits"]:
                            logits(it, job(st["logits"][0]), st["logits"][1])
                        if st["turn"]:
                            turn(it, job(st["turn"][0]), st["turn"][1])
                        if st["values"]:
                            values(it, job(st["values"][0]), st["values"][1])
                        if st["end"] is not None:
                            turn_output(it, job(st["end"]))
                run(pe, n, body)

            def hid_ready(pe, k, it, us, m):
                if us[0].src == "hid" and us[0].tiles[0].idx == 0 and m == 0:
                    need(pe, s_hid, [T_SLOTS + u.tiles[0].up - HID_GROUP + k + 1 for u in us], it)

            def layer_end(l):
                weights(f"out{l}", after=sums(f"m{l}", "out", 1))
                stats(f"m{l}", [7])
                weights(f"mlpa{l}", **first_unit(f"h{l}"))
                weights(f"mlp{l}", hid_ready)
                weights(f"mlpz{l}", hid_ready, sums(f"n{l}", "down", 1))
                pe.wait_ge(s_p, l + 1)

                def beside_ple(t):
                    if t.idx == 0:
                        stats(f"n{l}", [7])
                    if t.idx >= 5:
                        stats(f"g{l}", [t.idx - 5])
                weights(f"ple{l}", after=beside_ple)
                weights(f"gate{l}", **first_unit(f"g{l}", (0, 1, 2), sums("x1", "gate", 1) if l == 0 else None))

            for s, n in ((s_tr, 2), (s_pv, 2), (s_qk, TASK0)):
                pe.sem_inc(s, n)
            pe.wait_ge(s_t5, 32)
            pe.wait_ge(s_ones, 2)
            for g in range(3):
                t = extras["in0a"][g]
                evacuated([t], 0)
                for h in range(2):
                    c0 = g * S + h * HALF
                    c1 = min(BROW_N, c0 + HALF)
                    mm = nc.tensor.matmul(ACC[0:16, t.pair, h * HALF:h * HALF + c1 - c0], T5[:], ONEHOT[:, c0:c1],
                                          start=True, stop=True)
                mm.then_inc(s_tile, 1)
            pe.wait_ge(s_ones, 4)
            weights("in0a", **first_unit("x"))
            stats("cq", range(2))
            weights("in0p", after=lambda t: stats("ckv", [0]) if t.idx == 0 else None)
            weights("in0b")
            weights("in0c")
            pe.wait_ge(s_x, applies["cq"] + 3)
            weights("up0")
            last = tiles[seg_end["up0"] - 1]
            pe.wait_ge(s_evA, last.act)
            pe.wait_ge(s_evD, last.dve)
            pe.wait_ge(s_rt, 3)
            attention("fox")
            attention("mla")
            pe.wait_ge(s_ttr, TASKS_EVEN["task"])
            pe.wait_ge(s_ptD, COPIES["mla"])
            pe.wait_ge(s_o, TASKS_EVEN["task"])
            layer_end(0)
            weights("in1p", **first_unit("x1", range(7)))
            for name in ("in1a", "in1b"):
                weights(name)
            pe.wait_ge(s_cl, 16 * 8)
            t = extras["in1c"][0]
            evacuated([t], 0)
            for i in range(NB):
                tr = nc.tensor.transpose(ACC[:, t.pair, i * 12:(i + 1) * 12], GTT[:, i * P:(i + 1) * P],
                                         IDENT[0:12, 0:12])
            tr.then_inc(s_tile, 1)
            compress()
            weights("in1c")
            t = extras["out1"][0]
            evacuated([t], 0)
            pe.wait_ge(s_gl, GELU_STEPS)
            for c in range(2):
                nc.tensor.matmul(ACC[:, t.pair, 0:HD], W2K[:, c], HIDU[:, 0, c], start=c == 0, stop=c == 1)
            for c in range(2):
                mm = nc.tensor.matmul(ACC[0:HD, t.pair, HALF:HALF + HD], HIDU[:, 1, c], W2V[:, c],
                                      start=c == 0, stop=c == 1)
            mm.then_inc(s_tile, 1)
            pe.wait_ge(s_evA, t.act)
            pe.wait_ge(s_evD, t.dve)
            attention("dil")
            attention("nsa")
            pe.wait_ge(s_ttr, TASKS_ODD["task"])
            pe.wait_ge(s_ox, 1 + 2)
            pe.wait_ge(s_ptD, COPIES["nsa"])
            pe.wait_ge(s_o, TASKS_ODD["task"])
            layer_end(1)

        @block.scalar
        def _(act):
            def square(name, c, src):
                q = rnd[name][1] + c
                if q > 1:
                    act.wait_ge(s_st, q - 1)
                nc.scalar.activation(Q[:, q % 2], src, ACT.Square).then_inc(s_sq, 1)

            def root(name, dst):
                _, q, n = rnd[name]
                act.wait_ge(s_st, q + n)
                nc.scalar.activation(dst[:], OP[:].rearrange("p h s -> p (h s)"), ACT.Sqrt, bias=CONST[:, 0:1],
                                     scale=1.0 / (n * P)).then_inc(s_rt, 1)

            def high(name, c, dst):
                nc.scalar.activation(dst[:, c], H[:, c], ACT.Copy, scale=GAINS[:, GAIN[name], c:c + 1])\
                    .then_inc(s_xh, 1)

            def tile_loop(name, fn):
                seg = segs[name]

                def body(it):
                    for pos in range(len(seg.iters[0])):
                        us = [row[pos] for row in seg.iters]
                        for m in range(len(us[0].tiles)):
                            fn([u.tiles[m] for u in us], it)
                run(act, seg.n, body)

            def wide(t):
                return ACC[:, t.pair]

            def store(ts, it):
                t = ts[0]
                step = ts[1].idx - ts[0].idx if len(ts) > 1 else 0
                own = t.kind in ("uq", "ukv")
                if own:
                    need(act, s_tile, [x.no + 1 for x in ts], it)
                    need(act, s_store[t.pair], [16 * x.slot_before[t.pair] for x in ts], it)
                    rows = HD if t.kind == "uq" else P
                    nc.scalar.activation(Q[0:rows, t.pair], ACC[0:rows, t.pair], ACT.Copy).then_inc(s_evA, 1)
                    need(act, s_evA, [x.act for x in ts], it)
                    if t.kind == "uq":
                        act.wait_ge(s_rope, ROPE_KEY_STEPS + 2 * t.idx + 2)
                else:
                    need(act, s_evD, [x.dve for x in ts], it)
                if t.kind == "oddk":
                    act.dma_start(y_v[t.idx - 14], TL[HD:P, t.pair].bitcast(F32)).then_inc(s_vst, 16)
                if t.kind in SPLIT:
                    nc.scalar.activation(QR[:, t.pair], TL[:, t.pair].bitcast(F32), ACT.Copy).then_inc(s_hi, 1)
                    need(act, s_lo, [x.split for x in ts], it)
                    y = y_foxs if t.kind == "foxs" else y_odds
                    act.dma_start(y[bass.ds(at(t.idx, step, it), 1)].rearrange("o h p s -> p (o h) s"),
                                  HALVES[:, :, t.pair].bitcast(F32)).then_inc(s_store[t.pair], 16)
                    return
                dst = {"fox": y_fox, "odd": y_odd, "uq": y_q, "ukv": y_kv}[t.kind]
                rows = 96 if t.kind == "uq" else P
                src = Q[0:rows, t.pair] if own else QR[:, t.pair].bitcast(F32)
                act.dma_start(dst[bass.ds(at(t.idx, step, it), 1), 0:rows].rearrange("o p s -> (o p) s"),
                              src).then_inc(s_store[t.pair], 16)

            def mlp(ts, it):
                t = ts[0]
                if t.kind != "up":
                    return
                x = T[:, (t.up - 1) % 2]
                need(act, s_evD, [y.dve for y in ts], it)
                nc.scalar.activation(HH[:, t.idx], x, ACT.Square).then_inc(s_hhi, 1)
                need(act, s_hhi, [y.up for y in ts], it)
                nc.scalar.activation(x, x, ACT.Square).then_inc(s_sqh, 1)

            def attention(name):
                n, rows = phases[name]

                def copy_v(it, js):
                    j = js[0]
                    for g, vg in enumerate(j.vgroups):
                        need(act, s_tr, [k.vgroups[g]["tr"] for k in js], it)
                        if g == 0:
                            need(act, s_pv, [k.prev.pv_end if k.prev else 2 for k in js], it)
                        r = HD if j.kind == "mla" else P
                        nc.scalar.activation(V[:, j.slot, 4 * g:4 * g + 4, 0:r],
                                             TR[:, vg["ring"], 0:4 * r].rearrange("p (b f) -> p b f", b=4),
                                             ACT.Copy).then_inc(s_ptA, 1)

                def copies(it, js, n):
                    for m, g in enumerate(js[0].tasks[n]["groups"]):
                        if g["eng"] != "A":
                            continue
                        gs = [k.tasks[n]["groups"][m] for k in js]
                        need(act, s_tr, [x["tr"] for x in gs], it)
                        need(act, s_pv, [x["pv"] - 2 for x in gs], it)
                        w = (g["g1"] - g["g0"]) * P
                        nc.scalar.activation(PT[:, (g["pv"] - 1) % 2, 0:w], TR[:, g["ring"], 0:w],
                                             ACT.Copy).then_inc(s_ptA, 1)

                def probabilities(it, js, n):
                    t = js[0].tasks[n]
                    need(act, s_ttr, [k.tasks[n]["T"] + 1 for k in js], it)
                    x = prob(js[0], t)[:, 0:js[0].width(t["i"])]
                    nc.scalar.activation(x, x, ACT.Exp, bias=NM[:, n:n + 1], scale=-1.0,
                                         accum_out=L[:, n:n + 1]).then_inc(s_exp, 1)

                def outputs(it, js, pos):
                    for m, g in enumerate(js[0].ogroups):
                        if g["what"] != "o":
                            continue
                        need(act, s_tr, [k.ogroups[m]["tr"] for k in js], it)
                        nc.scalar.activation(chunk_of(XH, name, pos, it)[:, g["g"] * HALF:(g["g"] + 1) * HALF],
                                             TR[:, g["ring"]], ACT.Copy).then_inc(s_oh, 1)
                    if js[0].kind == "d16":
                        for g in range(3):
                            need(act, s_md, [MERGE_STEPS * k + 3 + g for k in range(len(rows))], it)
                            nc.scalar.activation(DM[:, g], DM[:, g], ACT.Exp, scale=-1.0).then_inc(s_mg, 1)

                def body(it):
                    job = lambda p: [row[p] for row in rows]
                    for st in pipeline(rows[0]):
                        if st["start"] is not None:
                            copy_v(it, job(st["start"]))
                        if st["turn"]:
                            copies(it, job(st["turn"][0]), st["turn"][1])
                        if st["logits"]:
                            probabilities(it, job(st["logits"][0]), st["logits"][1])
                        if st["end"] is not None:
                            outputs(it, job(st["end"]), st["end"])
                run(act, n, body)

            for m in range(1, 4):
                load_h(act, m)
            act.dma_start(POS[:], bass.AP(ins["positions"].tensor, 0, [[0, P], [1, S]])).then_inc(s_pos, 16)
            for s, n in ((s_exp, TASK0), (s_ptA, 2), (s_oh, 2)):
                act.sem_inc(s, n)
            for s in s_store:
                act.sem_inc(s, 16)
            act.wait_ge(s_const, 16 * N_CONST)
            for g in range(3):
                t = extras["in0a"][g]
                c1 = min(BROW_N, (g + 1) * S)
                act.wait_ge(s_tile, t.no + 1)
                nc.scalar.activation(BRS[:, g * S:c1], ACC[0:16, t.pair, 0:c1 - g * S], ACT.Copy).then_inc(s_evA, 1)
            for c in range(DC):
                act.wait_ge(s_h[c // 2], 16)
                high("x", c, XH)
                square("x", c, H[:, c])
            root("x", R)
            for c in range(3):
                act.wait_ge(s_evD, segs["in0a"].iters[0][c].tiles[0].dve)
                square("cq" if c < 2 else "ckv", c % 2, CQ[:, c])
                if c == 1:
                    act.wait_ge(s_dve, DVE_ANGLE)
                    root("cq", RC)
            act.wait_ge(s_bd, 16)
            for c in range(3):
                if c == 2:
                    act.wait_ge(s_cqn, 2)
                    root("ckv", RC)
                act.wait_ge(s_cqn, c + 1)
                nc.scalar.activation(CQH[:, c], CQ[:, c], ACT.Copy, scale=QKVG[:, c:c + 1]).then_inc(s_xh, 1)
            tile_loop("in0p", store)
            act.wait_ge(s_dve, DVE_ANGLE)
            nc.scalar.activation(CS[:], ANG[:, 0], ACT.Sin).then_inc(s_ft, 1)
            act.wait_ge(s_dve, DVE_FZ)
            nc.scalar.activation(KT[64:72], ANG[64:72, 1], ACT.Abs).then_inc(s_ft, 1)
            act.wait_ge(s_ft, 2)
            nc.scalar.activation(KT[64:72], KT[64:72], ACT.Exp, scale=-1.0).then_inc(s_ft, 1)
            act.wait_ge(s_ft, 3)
            nc.scalar.activation(KT[64:72], KT[64:72], ACT.Ln, bias=1.0).then_inc(s_ft, 1)
            act.wait_ge(s_rope, ROPE_KEY_STEPS)
            act.dma_start(y_kr, KR[0:32]).then_inc(s_misc, 16)
            act.wait_ge(s_dve, DVE_ALL)
            act.dma_start(y_f, ANG[64:72, 0]).then_inc(s_misc, 16)
            tile_loop("in0b", store)
            tile_loop("in0c", store)
            tile_loop("up0", store)
            attention("fox")
            attention("mla")

            def layer_end(l):
                for u in segs[f"out{l}"].iters[0]:
                    for t in u.tiles:
                        act.wait_ge(s_tile, t.no + 1)
                        square(f"m{l}", t.idx, wide(t))
                        nc.scalar.activation(M[:, t.idx], wide(t), ACT.Copy).then_inc(s_evA, 1)
                root(f"m{l}", R)
                for c in range(DC):
                    act.wait_ge(s_res, resids[f"m{l}"] + c + 1)
                    high(f"h{l}", c, XH)
                    square(f"h{l}", c, H[:, c])
                root(f"h{l}", R)
                for name in ("mlpa", "mlp", "mlpz"):
                    tile_loop(f"{name}{l}", mlp)
                downs = [t for u in segs[f"mlpz{l}"].iters[0] for t in u.tiles if t.kind == "down"]
                for c, t in enumerate(downs):
                    act.wait_ge(s_evD, t.dve)
                    square(f"n{l}", c, M[:, c])
                    if c == 3:
                        act.wait_ge(s_pload, 16 * (l + 1))
                        nc.scalar.activation(XH[:, 6:8], PRAW[:], ACT.Copy).then_inc(s_phi, 1)

                def projected(t):
                    act.wait_ge(s_tile, t.no + 1)
                    nc.scalar.activation(PP[:, t.idx], wide(t), ACT.Copy).then_inc(s_evA, 1)

                def stream(c):
                    act.wait_ge(s_res, resids[f"n{l}"] + c + 1)
                    if c == 4:
                        act.wait_ge(s_p, l + 1)
                    if c == 6:
                        act.wait_ge(s_tile, seg_end[f"ple{l}"])
                    high(f"g{l}", c, XH)
                    square(f"g{l}", c, H[:, c])

                for t in (t for u in segs[f"ple{l}"].iters[0] for t in u.tiles):
                    projected(t)
                    if t.idx == 0:
                        root(f"n{l}", R)
                    if t.idx >= 4:
                        stream(t.idx - 4)
                for c in range(4, DC):
                    stream(c)
                root(f"g{l}", R)
                for t in (u.tiles[0] for u in segs[f"gate{l}"].iters[0]):
                    x = T[:, (t.gate - 1) % 2]
                    act.wait_ge(s_evD, t.dve)
                    nc.scalar.activation(x, x, ACT.Sigmoid).then_inc(s_sig, 1)
                    if l == 0:
                        act.wait_ge(s_res, resids["ga0"] + t.idx + 1)
                        high("x1", t.idx, X1H)
                        square("x1", t.idx, H[:, t.idx])

            layer_end(0)
            root("x1", R)
            for name in ("in1p", "in1a", "in1b"):
                tile_loop(name, store)
            t = extras["in1c"][0]
            act.wait_ge(s_tile, t.no + 1)
            nc.scalar.activation(GT[:], ACC[:, t.pair, 0:NB * 12].rearrange("p (b g) -> p b g", g=12),
                                 ACT.Sigmoid).then_inc(s_evA, 1)
            in1c = [t for u in segs["in1c"].iters[0] for t in u.tiles]
            act.wait_ge(s_cu, 1)
            for which, src in ((0, OP), (1, TR)):
                nc.scalar.activation(HIDF[:, which], src[:, :, 0:HD], ACT.Copy).then_inc(s_hidf, 1)
            act.wait_ge(s_gl, 3)
            nc.scalar.activation(HIDT[:], HIDT[:], ACT.Exp, scale=-2.0 * math.sqrt(2.0 / math.pi)).then_inc(s_ge, 1)
            for t in in1c:
                store([t], 0)
            t = extras["out1"][0]
            act.wait_ge(s_tile, t.no + 1)
            nc.scalar.activation(VC[:], ACC[0:HD, t.pair, HALF:HALF + HD], ACT.Copy)
            nc.scalar.activation(KCH[:], ACC[:, t.pair, 0:HD], ACT.Copy).then_inc(s_evA, 1)
            attention("dil")
            attention("nsa")
            layer_end(1)

        @block.vector
        def _(dve):
            V_ = nc.vector
            steps = [0]

            def link(ins):
                steps[0] += 1
                ins.then_inc(s_dve, 1)
                dve.wait_ge(s_dve, steps[0])

            def inverse_rms(name, r):
                no = rnd[name][0]
                dve.wait_ge(s_rt, no + 1)
                V_.reciprocal(r[:], r[:]).then_inc(s_R, 1)
                dve.wait_ge(s_R, no + 1)

            def low(x, src, gain, hi, lo):
                dve.wait_ge(s_xh, x + 1)
                V_.scalar_tensor_tensor(out=lo, in0=src, scalar=gain, in1=hi.bitcast(F32), op0=ALU.mult,
                                        op1=ALU.subtract).then_inc(s_x, 1)

            def low_h(name, c, hi=XH, lo=XL):
                low(applies[name] + c, H[:, c], GAINS[:, GAIN[name], c:c + 1], hi[:, c], lo[:, c])

            def residual(name, then):
                inverse_rms(name, R)
                if name[0] == "m":
                    dve.wait_ge(s_evA, tiles[seg_end[f"out{name[1]}"] - 1].act)
                for c in range(8):
                    t0 = tcount[name] + c
                    if c > 1:
                        dve.wait_ge(s_res, resids[name] + c - 1)
                    V_.scalar_tensor_tensor(out=T[:, t0 % 2], in0=M[:, c], scalar=GAINS[:, GAIN[name], c:c + 1],
                                            in1=R[:], op0=ALU.mult, op1=ALU.mult).then_inc(s_T, 1)
                    dve.wait_ge(s_T, t0 + 1)
                    V_.tensor_tensor(H[:, c], H[:, c], T[:, t0 % 2], ALU.add).then_inc(s_res, 1)
                    if c:
                        low_h(then, c - 1)
                low_h(then, 7)

            def tile_loop(name, fn):
                seg = segs[name]

                def body(it):
                    for pos in range(len(seg.iters[0])):
                        us = [row[pos] for row in seg.iters]
                        for m in range(len(us[0].tiles)):
                            fn([u.tiles[m] for u in us], it)
                run(dve, seg.n, body)

            def mlp(ts, it):
                t = ts[0]
                need(dve, s_tile, [y.no + 1 for y in ts], it)
                if t.kind == "up":
                    x = T[:, (t.up - 1) % 2]
                    need(dve, s_hid, [T_SLOTS + y.up - 2 for y in ts], it)
                    V_.scalar_tensor_tensor(out=x, in0=ACC[:, t.pair], scalar=0.0, in1=R[:], op0=ALU.max,
                                            op1=ALU.mult).then_inc(s_evD, 1)
                    need(dve, s_sqh, [y.up for y in ts], it)
                    V_.tensor_tensor(HL[:, t.idx], x, HH[:, t.idx].bitcast(F32), ALU.subtract).then_inc(s_hid, 1)
                else:
                    need(dve, s_evD, [y.dve - DC - HID_GROUP for y in ts], it)
                    V_.tensor_tensor(M[:, t.idx], M[:, t.idx], ACC[:, t.pair], ALU.add).then_inc(s_evD, 1)

            def project(ts, it):
                t = ts[0]
                need(dve, s_tile, [x.no + 1 for x in ts], it)
                if t.kind in ("cq", "misc"):
                    dst = CQ[:, t.idx] if t.kind == "cq" else MISC1[:, 0]
                    V_.tensor_tensor(dst, ACC[:, t.pair], R[:], ALU.mult).then_inc(s_evD, 1)
                    return
                need(dve, s_store[t.pair], [16 * x.slot_before[t.pair] for x in ts], it)
                dst = (TL if t.kind in SPLIT else QR)[:, t.pair].bitcast(F32)
                V_.tensor_tensor(dst, ACC[:, t.pair], R[:], ALU.mult).then_inc(s_evD, 1)

            def low_half(ts, it):
                t = ts[0]
                need(dve, s_hi, [x.split for x in ts], it)
                if t.kind == "oddk":
                    dve.wait_ge(s_vst, 16 * (t.idx - 13))
                V_.tensor_tensor(TL[:, t.pair], TL[:, t.pair].bitcast(F32), QR[:, t.pair].bitcast(F32),
                                 ALU.subtract).then_inc(s_lo, 1)

            def projection(ts, it):
                project(ts, it)
                if ts[0].kind in SPLIT:
                    low_half(ts, it)

            def rotate(ts, it):
                t = ts[0]
                if t.kind != "uq":
                    return
                dve.wait_ge(s_tile, t.no + 1)
                dve.wait_ge(s_store[t.pair], 16 * t.slot_before[t.pair])
                dve.wait_ge(s_rope, ROPE_KEY_STEPS + 2 * t.idx)
                V_.tensor_tensor(KT[64:96], ACC[96:128, t.pair], CS[96:128], ALU.mult).then_inc(s_rope, 1)
                V_.tensor_tensor(Q[64:96, t.pair], ACC[64:96, t.pair], CS[64:96], ALU.mult).then_inc(s_evD, 1)
                dve.wait_ge(s_rope, ROPE_KEY_STEPS + 2 * t.idx + 1)
                dve.wait_ge(s_evD, t.dve)
                V_.tensor_tensor(Q[64:96, t.pair], Q[64:96, t.pair], KT[64:96], ALU.add).then_inc(s_rope, 1)

            def attention(name):
                n_it, rows = phases[name]

                def bias(j, t):
                    slot, kind = j.slot, j.kind
                    e, i, w = t["e"], t["i"], j.width(t["i"])
                    if kind == "fox":
                        return BIAS[:, slot, e * S:e * S + w]
                    if kind == "mla":
                        return BIAS[:, 0, S - P - i * P:S]
                    if kind == "sel":
                        return BIAS[:, slot, e * S + S - P - i * P:(e + 1) * S]
                    if kind == "win":
                        return BIAS[:, slot, (e + 1) * WIN_W - w:(e + 1) * WIN_W]
                    if kind == "cmp":
                        return CMPMASK[:, i * HD:(i + 1) * HD]
                    wt = D16_W if kind == "d16" else DIL_W
                    return BIASD[:, slot, e, wt - w:wt]

                def copies(it, js, n):
                    for m, g in enumerate(js[0].tasks[n]["groups"]):
                        if g["eng"] != "D":
                            continue
                        gs = [k.tasks[n]["groups"][m] for k in js]
                        need(dve, s_tr, [x["tr"] for x in gs], it)
                        need(dve, s_pv, [x["pv"] - 2 for x in gs], it)
                        w, r = (g["g1"] - g["g0"]) * P, HD if js[0].kind == "cmp" else P
                        V_.tensor_copy(PT[0:r, (g["pv"] - 1) % 2, 0:w], TR[0:r, g["ring"], 0:w]).then_inc(s_ptD, 1)

                def scores(it, js, n):
                    j, t = js[0], js[0].tasks[n]
                    w, b = j.width(t["i"]), t["T"] % 2
                    need(dve, s_qk, [k.tasks[n]["T"] + 1 for k in js], it)
                    if n == 0 and j.kind == "mla" and j.slot == 0:
                        dve.wait_ge(s_mask, 16)
                    elif n == 0 and j.kind not in ("mla", "cmp"):
                        need(dve, s_bias, [16 * k.c1["bias"] for k in js], it)
                    need(dve, s_tr, [k.tasks[n]["tr_before"] for k in js], it)
                    V_.tensor_tensor_reduce(prob(j, t)[:, 0:w], ACC[:, b, 0:w], bias(j, t),
                                            -MLA_SCALE if j.kind == "mla" else -1.0 / ISCALE, 3e38,
                                            ALU.add, ALU.min, NM[:, n:n + 1]).then_inc(s_ttr, 1)

                def output(it, js, n, pos):
                    kind, t = js[0].kind, js[0].tasks[n]
                    e, i, b = t["e"], t["i"], t["T"] % 2
                    need(dve, s_pv, [k.tasks[n]["groups"][-1]["pv"] for k in js], it)
                    if n == 0:
                        need(dve, s_tr, [k.ot_before for k in js], it)
                    f = HD * (pos if kind == "mla" else e)
                    dst = OT[:, i, f:f + HD]
                    if kind in DILATED:
                        V_.tensor_copy(OL[:, i, f:f + HD], L[:, n:n + 1].to_broadcast([P, HD]))
                        V_.tensor_copy(OM[:, i, f:f + HD], NM[:, n:n + 1].to_broadcast([P, HD]))
                        V_.tensor_copy(dst, OP[:, b, 0:HD]).then_inc(s_o, 1)
                        return
                    V_.reciprocal(RL[:, n:n + 1], L[:, n:n + 1]).then_inc(s_rl, 1)
                    need(dve, s_rl, [k.c0["rl"] + n + 1 for k in js], it)
                    if kind not in NSA:
                        V_.tensor_scalar(dst, OP[:, b, 0:HD], RL[:, n:n + 1], None, ALU.mult).then_inc(s_o, 1)
                        return
                    col = at(e * 3 + NSA.index(kind), 6, it)
                    V_.tensor_tensor(CF[:, n:n + 1], RL[:, n:n + 1], GT[:, i, bass.ds(col, 1)], ALU.mult)\
                        .then_inc(s_cf, 1)
                    need(dve, s_cf, [k.c0["cf"] + n + 1 for k in js], it)
                    if kind == "cmp":
                        V_.tensor_scalar(dst, OP[:, b, 0:HD], CF[:, n:n + 1], None, ALU.mult).then_inc(s_o, 1)
                    else:
                        need(dve, s_o, [k.tasks[n]["T"] - 15 for k in js], it)
                        V_.scalar_tensor_tensor(out=dst, in0=OP[:, b, 0:HD], scalar=CF[:, n:n + 1], in1=dst,
                                                op0=ALU.mult, op1=ALU.add).then_inc(s_o, 1)

                def outputs(it, js, pos):
                    kind = js[0].kind
                    if kind == "d1":
                        need(dve, s_ox, [1 + k for k in range(n_it)], it)
                    for m, g in enumerate(js[0].ogroups):
                        need(dve, s_tr, [k.ogroups[m]["tr"] for k in js], it)
                        cols = slice(g["g"] * HALF, (g["g"] + 1) * HALF)
                        if g["what"] == "o":
                            need(dve, s_oh, [k.c0["oh"] + m + 1 for k in js], it)
                            V_.tensor_tensor(chunk_of(XL, name, pos, it)[:, cols], TR[:, g["ring"]],
                                             chunk_of(XH, name, pos, it)[:, cols].bitcast(F32),
                                             ALU.subtract).then_inc(s_ptD, 1)
                            continue
                        dst = {"u": DU, "l": DL, "m": DM}[g["what"]]
                        c = {"d1": 1, "d4": 4, "d16": 8}[kind]
                        d = dst[:, DILATED.index(kind)]
                        src = TR[:, g["ring"]]
                        if c == 1:
                            d = d[:, cols]
                        else:
                            d = d.rearrange("p (a c) -> p c a", c=c)[:, g["g"] * c // 2:(g["g"] + 1) * c // 2, :]
                            src = src.rearrange("p (c a) -> p c a", c=c // 2)
                        V_.tensor_copy(d, src).then_inc(s_ptD, 1)
                    if kind == "d16":
                        merge([k.ogroups[-1]["rel"][1] for k in js], it)

                def body(it):
                    job = lambda p: [row[p] for row in rows]
                    for st in pipeline(rows[0]):
                        if st["turn"] and name == "mla":
                            copies(it, job(st["turn"][0]), st["turn"][1])
                        if st["logits"]:
                            scores(it, job(st["logits"][0]), st["logits"][1])
                        if st["turn"] and name != "mla":
                            copies(it, job(st["turn"][0]), st["turn"][1])
                        if st["end"] is not None:
                            outputs(it, job(st["end"]), st["end"])
                        if st["values"]:
                            output(it, job(st["values"][0]), st["values"][1], st["values"][0])

                def merge(evacuated, it):
                    mm = OM[:].rearrange("p b f -> p (b f)")
                    need(dve, s_ptD, evacuated, it)
                    V_.tensor_tensor(mm, DM[:, 0], DM[:, 1], ALU.min).then_inc(s_md, 1)
                    need(dve, s_md, [MERGE_STEPS * k + 1 for k in range(n_it)], it)
                    V_.tensor_tensor(mm, mm, DM[:, 2], ALU.min).then_inc(s_md, 1)
                    need(dve, s_md, [MERGE_STEPS * k + 2 for k in range(n_it)], it)
                    for g in range(3):
                        V_.tensor_tensor(DM[:, g], DM[:, g], mm, ALU.subtract).then_inc(s_md, 1)
                    for g in range(3):
                        need(dve, s_mg, [3 * k + g + 1 for k in range(n_it)], it)
                        V_.tensor_tensor(DL[:, g], DL[:, g], DM[:, g], ALU.mult).then_inc(s_md, 1)
                    need(dve, s_md, [MERGE_STEPS * k + 7 for k in range(n_it)], it)
                    V_.tensor_tensor(DL[:, 0], DL[:, 0], DL[:, 1], ALU.add).then_inc(s_md, 1)
                    need(dve, s_md, [MERGE_STEPS * k + 9 for k in range(n_it)], it)
                    V_.tensor_tensor(DL[:, 0], DL[:, 0], DL[:, 2], ALU.add).then_inc(s_md, 1)
                    need(dve, s_md, [MERGE_STEPS * k + 10 for k in range(n_it)], it)
                    V_.reciprocal(DL[:, 0], DL[:, 0]).then_inc(s_md, 1)

                run(dve, n_it, body)

            two_pi = 2 * math.pi
            c1 = 6.28125
            c2 = float(np.float32(np.round((two_pi - c1) * 2 ** 20) / 2 ** 20))
            c3 = float(np.float32(two_pi - c1 - c2))
            magic = float(3 << 22)
            for s, n in ((s_evD, 2), (s_ttr, TASK0), (s_o, TASK0), (s_ptD, 2), (s_rl, 2), (s_cf, 2)):
                dve.sem_inc(s, n)
            dve.wait_ge(s_const, 16 * N_CONST)
            V_.memset(RL[:, 0:1], 0.0).then_inc(s_hid, T_SLOTS)
            for c in range(DC):
                low_h("x", c)
            inverse_rms("x", R)
            low_rank = [[u.tiles[0]] for u in segs["in0a"].iters[0]]
            project(low_rank[0], 0)
            dve.wait_ge(s_pos, 16)
            link(V_.tensor_copy(ANG[:, 0], POS[:]))
            link(V_.tensor_scalar(ANG[:, 1], ANG[:, 0], CONST[:, 1:2], None, ALU.mult))
            link(V_.tensor_scalar(ANG[:, 2], ANG[:, 1], 1.0 / two_pi, CONST[:, 2:3], ALU.mult, ALU.add))
            link(V_.tensor_scalar(ANG[:, 2], ANG[:, 2], magic, None, ALU.add))
            link(V_.tensor_scalar(ANG[:, 2], ANG[:, 2], -magic, None, ALU.add))
            link(V_.scalar_tensor_tensor(out=ANG[:, 0], in0=ANG[:, 2], scalar=-c1, in1=ANG[:, 1], op0=ALU.mult, op1=ALU.add))
            link(V_.scalar_tensor_tensor(out=ANG[:, 1], in0=ANG[:, 2], scalar=-c2, in1=ANG[:, 0], op0=ALU.mult, op1=ALU.add))
            link(V_.scalar_tensor_tensor(out=ANG[:, 0], in0=ANG[:, 2], scalar=-c3, in1=ANG[:, 1], op0=ALU.mult, op1=ALU.add))
            link(V_.tensor_scalar(ANG[:, 0], ANG[:, 0], CONST[:, 3:4], None, ALU.add))
            link(V_.tensor_scalar(ANG[:, 0], ANG[:, 0], 3.1415925, -3.1415925, ALU.min, ALU.max))
            assert steps[0] == DVE_ANGLE
            for t in low_rank[1:]:
                project(t, 0)

            def norm_cq(c):
                V_.tensor_tensor(CQ[:, c], CQ[:, c], RC[:], ALU.mult).then_inc(s_cqn, 1)

            def low_cq(c):
                low(applies["cq"] + c, CQ[:, c], QKVG[:, c:c + 1], CQH[:, c], CQL[:, c])

            inverse_rms("cq", RC)
            norm_cq(0)
            norm_cq(1)
            low_cq(0)
            low_cq(1)
            first = [[u.tiles[0]] for u in segs["in0p"].iters[0]]
            project(first[0], 0)
            inverse_rms("ckv", RC)
            norm_cq(2)
            low_cq(2)
            low_half(first[0], 0)
            projection(first[1], 0)
            t = segs["in0a"].iters[0][3].tiles[0]
            dve.wait_ge(s_evD, t.dve)
            f0, f1, f2 = ANG[64:72, 0], ANG[64:72, 1], KT[64:72]
            link(V_.tensor_scalar(f1, MISC[64:72], CONST[64:72, 5:6], None, ALU.add))
            assert steps[0] == DVE_FZ
            dve.wait_ge(s_ft, 1)
            link(V_.tensor_scalar(CS[:], CS[:], CONST[:, 4:5], None, ALU.mult))
            link(V_.tensor_scalar(f0, f1, 0.0, None, ALU.min))
            dve.wait_ge(s_ft, 4)
            link(V_.tensor_tensor(f0, f0, f2, ALU.subtract))
            link(V_.memset(f1, 1.0))
            link(V_.tensor_tensor_scan(f2, f1, f0, 0.0, ALU.mult, ALU.add))
            link(V_.tensor_scalar(f0, f2, -ISCALE, None, ALU.mult))
            assert steps[0] == DVE_ALL, steps
            dve.wait_ge(s_ones, 4)
            V_.tensor_tensor(KT[0:32], MISC[32:64], CS[32:64], ALU.mult).then_inc(s_rope, 1)
            V_.tensor_tensor(KR[0:32], MISC[0:32], CS[0:32], ALU.mult).then_inc(s_rope, 1)
            dve.wait_ge(s_rope, 2)
            V_.tensor_tensor(KR[0:32], KR[0:32], KT[0:32], ALU.add).then_inc(s_rope, 1)
            tile_loop("in0b", projection)
            tile_loop("in0c", projection)
            tile_loop("up0", rotate)
            attention("fox")
            attention("mla")

            def layer_end(l):
                residual(f"m{l}", f"h{l}")
                link(V_.memset(M[:], 0.0))
                inverse_rms(f"h{l}", R)
                for name in ("mlpa", "mlp"):
                    tile_loop(f"{name}{l}", mlp)
                for t in (t for u in segs[f"mlpz{l}"].iters[0] for t in u.tiles):
                    mlp([t], 0)
                    if t.kind == "down" and t.idx == 4:
                        dve.wait_ge(s_phi, l + 1)
                        V_.tensor_tensor(XL[:, 6:8], PRAW[:], XH[:, 6:8].bitcast(F32), ALU.subtract).then_inc(s_p, 1)
                dve.wait_ge(s_hid, T_SLOTS + t.up)
                residual(f"n{l}", f"g{l}")
                inverse_rms(f"g{l}", R)
                for t in (u.tiles[0] for u in segs[f"gate{l}"].iters[0]):
                    x = T[:, (t.gate - 1) % 2]
                    dve.wait_ge(s_tile, t.no + 1)
                    dve.wait_ge(s_res, resids[f"ga{l}"] + max(t.idx - 1, 0))
                    V_.tensor_tensor(x, ACC[:, t.pair], R[:], ALU.mult).then_inc(s_evD, 1)
                    dve.wait_ge(s_sig, t.gate)
                    V_.tensor_tensor(x, x, PP[:, t.idx], ALU.mult).then_inc(s_gm, 1)
                    dve.wait_ge(s_gm, t.gate)
                    V_.tensor_tensor(H[:, t.idx], H[:, t.idx], x, ALU.add).then_inc(s_res, 1)
                    if l == 0:
                        low_h("x1", t.idx, X1H, X1L)

            layer_end(0)
            inverse_rms("x1", R)
            for name in ("in1p", "in1a"):
                tile_loop(name, projection)
            dve.wait_ge(s_cl, 16 * 8)
            dve.wait_ge(s_cz, 2)
            for which in range(2):
                for m in range(16):
                    last = V_.tensor_scalar(CBF[:, which, m], CMPX[:, which, 2 * m:2 * m + 16 * 63 + 1:16],
                                            POSC[:, m, which:which + 1], None, ALU.add)
            last.then_inc(s_cb, 1)
            tile_loop("in1b", projection)
            in1c = [t for u in segs["in1c"].iters[0] for t in u.tiles]
            dve.wait_ge(s_evA, extras["in1c"][0].act)
            g = GT[:, 0].rearrange("p (h b) -> p h b", b=3)[:, :, 0]
            V_.tensor_scalar(g, g, CONST[:, 6:7], None, ALU.mult).then_inc(s_cmp, 1)
            dve.wait_ge(s_hidf, 2)
            n = [0]

            def gelu(ins):
                n[0] += 1
                ins.then_inc(s_gl, 1)
                dve.wait_ge(s_gl, n[0])

            gelu(V_.tensor_tensor(HIDT[:], HIDF[:], HIDF[:], ALU.mult))
            gelu(V_.tensor_scalar(HIDT[:], HIDT[:], 0.044715, 1.0, ALU.mult, ALU.add))
            gelu(V_.tensor_tensor(HIDT[:], HIDT[:], HIDF[:], ALU.mult))
            dve.wait_ge(s_ge, 1)
            gelu(V_.tensor_scalar(HIDT[:], HIDT[:], 1.0, None, ALU.add))
            gelu(V_.reciprocal(HIDT[:], HIDT[:]))
            gelu(V_.tensor_tensor(HIDU[:], HIDF[:], HIDT[:], ALU.mult))
            assert n[0] == GELU_STEPS
            for t in in1c:
                projection([t], 0)
            t = extras["out1"][0]
            dve.wait_ge(s_evA, t.act)
            V_.tensor_tensor(KCL[:], ACC[:, t.pair, 0:HD], KCH[:].bitcast(F32), ALU.subtract).then_inc(s_evD, 1)
            attention("dil")
            dve.wait_ge(s_bd, 16 * 7)
            attention("nsa")
            layer_end(1)


def t5_bucket(dist):
    n = np.maximum(dist, 0)
    ratio = np.log(np.maximum(n, 1).astype(np.float32) / np.float32(16)) / np.float32(math.log(2048 / 16))
    large = np.minimum(16 + (ratio * np.float32(16)).astype(np.int32), 31)
    return np.where(n < 16, n, large)


def onehot_rows():
    oh = np.zeros((33, BROW_N), np.float32)

    def fill(kind, width, top, ok, step=1):
        x = np.arange(width)
        d = top - x
        good = ok(d)
        b = np.where(good, t5_bucket(d * step), 32)
        oh[b, BROW[kind] + x] = ISCALE

    fill("sel", 1152, S - 1, lambda d: d >= 0)
    fill("win", 768, WIN_W - 1, lambda d: (d >= 0) & (d < 512))
    fill("d1", 384, DIL_W - 1, lambda d: (d >= 0) & (d <= 128))
    fill("d4", 384, DIL_W - 1, lambda d: (d >= 0) & (d <= 128), 4)
    fill("d16", 256, D16_W - 1, lambda d: (d >= 0) & (d % 2 == 0), 8)
    return oh


def constants():
    c = {"ident": np.eye(P, dtype=np.float32), "onehot": onehot_rows()}
    q, k = np.arange(P)[:, None], np.arange(P)[None]
    c["mask"] = np.where(k > q, np.float32(NEG * ISCALE), np.float32(0))
    u = np.arange(S)[None]
    c["mlamask"] = np.where(u - (S - P) > q, np.float32(NEG), np.float32(0))
    t = np.arange(S).reshape(NB, P).T[:, :, None]
    n = np.arange(HD)[None, None]
    ok = (16 * n + 31 <= t) & (n < N_CMP)
    c["cmpmask"] = np.where(ok, np.float32(0), np.float32(NEG * ISCALE)).reshape(P, NB * HD).copy()
    k = np.zeros((P, 8), np.float32)
    inv = (10000.0 ** (-np.arange(0, 32, 2, dtype=np.float32) / np.float32(32))).astype(np.float32)
    row = np.arange(P)
    k[:, 0] = EPS
    k[:, 1] = inv[row % 16]
    cos = (row // 32) % 2 == 0
    k[:, 2] = np.where(cos, 0.25, 0.0)
    k[:, 3] = np.where(cos, math.pi / 2, 0.0)
    k[:, 4] = np.where(cos, 1.0, np.where(row % 32 < 16, -1.0, 1.0))
    k[:, 6] = (row >= 31).astype(np.float32)
    c["const"] = k
    return c


def weight_stream(a):
    f = lambda w: np.asarray(w)[0]
    out = []

    def full(w, cols):
        x = np.zeros((D, P), np.float32)
        cols = np.asarray(cols)
        x[:, cols >= 0] = w[:, cols[cols >= 0]]
        out.append(x.reshape(DC, P, P).transpose(1, 0, 2).reshape(P, D))

    def span(w, kc, c0, tiles):
        x = w[:, c0:c0 + tiles * P].reshape(kc, P, tiles, P)
        out.append(x.transpose(1, 2, 0, 3).reshape(P, D))

    r = lambda c0, n=P: list(range(c0, c0 + n))
    w = f(a["ev_w_in"])
    for c in range(3):
        full(w, r(c * P))
    kr = 384
    full(w, r(kr, 32) + r(kr + 16, 16) + r(kr, 16) + r(kr + 32 + 3 * 512, 8) + [-1] * 56)
    for c in range(12):
        full(w, r(kr + 32 + c * P))
    uq = f(a["ev_w_uq"]).reshape(256, 8, 96)
    uq = np.concatenate([uq, uq[:, :, 80:96], uq[:, :, 64:80]], axis=2).reshape(256, 1024)
    span(uq, 2, 0, 4)
    span(uq, 2, 512, 4)
    span(f(a["ev_w_ukv"]), 1, 0, 8)
    for c in range(8):
        full(f(a["ev_w_out"]), r(c * P))

    def rest(l):
        up, down = np.asarray(a["w_mlp_up"])[l], np.asarray(a["w_mlp_down"])[l]
        for g in range(N_GROUPS):
            for c in range(HID_GROUP):
                full(up, r((g * HID_GROUP + c) * P))
            for j in range(DC // 2):
                span(down[g * 512:(g + 1) * 512], 4, 2 * j * P, 2)
        for h in range(2):
            span(np.asarray(a["w_ple_proj"])[l], 2, 512 * h, 4)
        for c in range(8):
            full(np.asarray(a["w_ple_gate"])[l], r(c * P))

    rest(0)
    w = f(a["od_w_in"])
    full(w, r(0))
    full(w, r(P))
    full(w, r(20 * P))
    full(w, r(23 * P, 12) + [-1] * 116)
    for c in range(2, 18):
        full(w, r(c * P))
    for c in (18, 19, 21, 22):
        full(w, r(c * P))
    for c in range(4):
        span(f(a["od_w_out"]), 4, 2 * c * P, 2)
    rest(1)
    return np.stack(out)


def layout(a):
    a = {k: np.asarray(v) for k, v in a.items()}
    cols = lambda g: g.reshape(-1, P).T
    m = constants()
    m["xT"] = a["x"][0].T.reshape(DC, P, S)
    m["pT"] = a["p"][:, 0].transpose(0, 2, 1).reshape(2, 2, P, S)
    m["positions"] = a["positions"].reshape(1, S)
    m["w"] = weight_stream(a)
    gains = [a[k][l] for k in ("norm_mix_pre", "norm_mix_post", "norm_mlp_pre", "norm_mlp_post", "ple_norm")
             for l in range(2)]
    m["gains"] = np.stack([cols(g) for g in gains], axis=1)
    m["qkvg"] = np.concatenate([cols(a["ev_q_norm"][0]), cols(a["ev_kv_norm"][0])], axis=1)
    m["const"][64:72, 5] = a["ev_forget_bias"][0]
    m["t5"] = a["t5_bias"]
    pos = np.stack([a["od_cmp_pos_k"][0], a["od_cmp_pos_v"][0]])
    m["posc"] = pos.reshape(2, 16, P).transpose(2, 1, 0)
    k2 = a["od_cmp_w2_k"][0].reshape(2, P, HD).transpose(1, 0, 2)
    m["w2k"] = np.concatenate([k2, k2], axis=2)
    m["w1"] = np.stack([a[key][0].reshape(4, 4, P, 256).transpose(2, 0, 1, 3).reshape(P, 4, S)
                        for key in ("od_cmp_w1_k", "od_cmp_w1_v")])
    m["w2v"] = a["od_cmp_w2_v"][0].reshape(2, P, HD).transpose(1, 0, 2)
    return {k: np.ascontiguousarray(v) for k, v in m.items()}


def kernel(**inputs):
    import concourse.bacc as bacc
    from concourse.bass_utils import run_bass_kernel_spmd

    nc = bacc.Bacc("TRN2", target_bir_lowering=False, num_devices=1)
    arrays = layout(inputs)
    ins = {k: nc.dram_tensor(f"in_{k}", v.shape, mybir.dt.from_np(v.dtype), kind="ExternalInput").ap()
           for k, v in arrays.items()}
    out = nc.dram_tensor("out", (DC, P, S), F32, kind="ExternalOutput").ap()
    program(nc, ins, out)
    r = run_bass_kernel_spmd(nc, [{f"in_{k}": v for k, v in arrays.items()}], core_ids=[0])
    y = np.asarray(r.results[0]["out"])
    return np.ascontiguousarray(y.reshape(D, S).T)[None]
```
